# Optimizing a Trainium2 kernel written in Bass

```python
import math
import jax
import jax.numpy as jnp
from jax import lax
import numpy as np
import jax, jax.numpy as jnp

D_MODEL = 1024
BATCH = 1
SEQ = 256
DEPTH = 2

PLE_DIM = 256
N_EVEN = (DEPTH + 1) // 2
N_ODD = DEPTH // 2
SSD_HEADS = 16
SSD_HEAD_DIM = 64
SSD_INNER = SSD_HEADS * SSD_HEAD_DIM
SSD_GROUPS = 2
SSD_HPG = SSD_HEADS // SSD_GROUPS
SSD_STATE = 128
SSD_CONV = 4
SSD_CHUNK = 128
SSD_XBC = SSD_INNER + 2 * SSD_GROUPS * SSD_STATE
SC_DIM = 1024
SC_CONV = 3
MIX_IN = SSD_INNER + SSD_XBC + SSD_HEADS + 3 * SC_DIM
MIX_OUT = SSD_INNER + SC_DIM
ATTN_HEADS = 16
ATTN_KV_HEADS = 4
ATTN_GROUP = ATTN_HEADS // ATTN_KV_HEADS
ATTN_HEAD_DIM = 64
WINDOW = 128
ATTN_BLOCK = 128
QKV_DIM = (ATTN_HEADS + 2 * ATTN_KV_HEADS) * ATTN_HEAD_DIM
D_FF = ((8 * D_MODEL + 3 * 256 - 1) // (3 * 256)) * 256
ALPHA = (2 * DEPTH) ** 0.25
BETA = (8 * DEPTH) ** -0.25
LN_EPS = 1e-5
RMS_EPS = 1e-5


def layer_norm(x, g, b):
    xf = x.astype(jnp.float32)
    mu = jnp.mean(xf, axis=-1, keepdims=True)
    xc = xf - mu
    var = jnp.mean(xc * xc, axis=-1, keepdims=True)
    return (xc * lax.rsqrt(var + LN_EPS) * g.astype(jnp.float32) + b.astype(jnp.float32)).astype(x.dtype)

def causal_dwconv(x, w):
    k, c = w.shape
    return lax.conv_general_dilated(
        x, w[:, None, :].astype(x.dtype), window_strides=(1,), padding=[(k - 1, 0)],
        dimension_numbers=('NWC', 'WIO', 'NWC'), feature_group_count=c)

def ssd_mixer(z, xbc, dt_raw, conv_w, conv_b, dt_bias, a_log, d_skip, norm_w):
    f32 = jnp.float32
    bsz, seqlen, _ = z.shape
    nc = seqlen // SSD_CHUNK
    xbc = jax.nn.silu(causal_dwconv(xbc, conv_w) + conv_b.astype(xbc.dtype)).astype(f32)
    xs = xbc[..., :SSD_INNER].reshape(bsz, nc, SSD_CHUNK, SSD_GROUPS, SSD_HPG, SSD_HEAD_DIM)
    bm = xbc[..., SSD_INNER:SSD_INNER + SSD_GROUPS * SSD_STATE].reshape(bsz, nc, SSD_CHUNK, SSD_GROUPS, SSD_STATE)
    cm = xbc[..., SSD_INNER + SSD_GROUPS * SSD_STATE:].reshape(bsz, nc, SSD_CHUNK, SSD_GROUPS, SSD_STATE)
    dt = jax.nn.softplus(dt_raw.astype(f32) + dt_bias.astype(f32))
    a = -jnp.exp(a_log.astype(f32))
    dt = dt.reshape(bsz, nc, SSD_CHUNK, SSD_GROUPS, SSD_HPG)
    da = dt * a.reshape(SSD_GROUPS, SSD_HPG)
    xdt = xs * dt[..., None]
    a_cs = jnp.cumsum(da, axis=2)
    seg = a_cs[:, :, :, None] - a_cs[:, :, None, :]
    causal = jnp.tril(jnp.ones((SSD_CHUNK, SSD_CHUNK), dtype=bool))[:, :, None, None]
    decay_ls = jnp.exp(jnp.where(causal, seg, -jnp.inf))
    cb = jnp.einsum('bclgn,bcsgn->bclsg', cm, bm)
    y_diag = jnp.einsum('bclsgr,bcsgrp->bclgrp', cb[..., None] * decay_ls, xdt)
    decay_to_end = jnp.exp(a_cs[:, :, -1:] - a_cs)
    chunk_states = jnp.einsum('bclgn,bclgrp->bcgrpn', bm, xdt * decay_to_end[..., None])
    chunk_decay = jnp.exp(a_cs[:, :, -1])

    def step(h, inp):
        s_c, d_c = inp
        return h * d_c[..., None, None] + s_c, h

    h0 = jnp.zeros((bsz, SSD_GROUPS, SSD_HPG, SSD_HEAD_DIM, SSD_STATE), f32)
    _, h_in = lax.scan(step, h0, (jnp.moveaxis(chunk_states, 1, 0), jnp.moveaxis(chunk_decay, 1, 0)))
    h_in = jnp.moveaxis(h_in, 0, 1)
    y_off = jnp.einsum('bclgn,bcgrpn->bclgrp', cm, h_in) * jnp.exp(a_cs)[..., None]
    y = y_diag + y_off + xs * d_skip.astype(f32).reshape(SSD_GROUPS, SSD_HPG)[:, :, None]
    y = y.reshape(bsz, seqlen, SSD_INNER) * jax.nn.silu(z.astype(f32))
    yg = y.reshape(bsz, seqlen, SSD_GROUPS, SSD_INNER // SSD_GROUPS)
    yg = yg * lax.rsqrt(jnp.mean(yg * yg, axis=-1, keepdims=True) + RMS_EPS)
    return (yg.reshape(bsz, seqlen, SSD_INNER) * norm_w.astype(f32)).astype(z.dtype)

def ssd_shortconv_layer_mixer(x, w_in, conv_w, conv_b, dt_bias, a_log, d_skip, norm_w, sc_conv_w, w_out):
    proj = x @ w_in
    o1 = SSD_INNER
    o2 = o1 + SSD_XBC
    o3 = o2 + SSD_HEADS
    o4 = o3 + SC_DIM
    o5 = o4 + SC_DIM
    z, xbc, dt_raw = proj[..., :o1], proj[..., o1:o2], proj[..., o2:o3]
    sc_b, sc_c, sc_h = proj[..., o3:o4], proj[..., o4:o5], proj[..., o5:]
    y_ssd = ssd_mixer(z, xbc, dt_raw, conv_w, conv_b, dt_bias, a_log, d_skip, norm_w)
    y_sc = sc_b * causal_dwconv(sc_c * sc_h, sc_conv_w)
    return jnp.concatenate([y_ssd.astype(x.dtype), y_sc.astype(x.dtype)], axis=-1) @ w_out

def sliding_window_attention(x, w_qkv, b_qkv, sinks, w_o, b_o):
    bsz, seqlen, _ = x.shape
    nb = seqlen // ATTN_BLOCK
    qkv = x @ w_qkv + b_qkv
    nq = ATTN_HEADS * ATTN_HEAD_DIM
    nkv = ATTN_KV_HEADS * ATTN_HEAD_DIM
    q = qkv[..., :nq].reshape(bsz, nb, ATTN_BLOCK, ATTN_KV_HEADS, ATTN_GROUP, ATTN_HEAD_DIM)
    k = qkv[..., nq:nq + nkv].reshape(bsz, nb, ATTN_BLOCK, ATTN_KV_HEADS, ATTN_HEAD_DIM)
    v = qkv[..., nq + nkv:].reshape(bsz, nb, ATTN_BLOCK, ATTN_KV_HEADS, ATTN_HEAD_DIM)

    def with_prev(t):
        prev = jnp.concatenate([jnp.zeros_like(t[:, :1]), t[:, :-1]], axis=1)
        return jnp.concatenate([prev, t], axis=2)

    kk = with_prev(k)
    vv = with_prev(v)
    scale = ATTN_HEAD_DIM ** -0.5
    s = jnp.einsum('bnqkgd,bnskd->bnkgqs', q, kk, preferred_element_type=jnp.float32) * scale
    n_idx = jnp.arange(nb)[:, None, None]
    q_pos = n_idx * ATTN_BLOCK + jnp.arange(ATTN_BLOCK)[None, :, None]
    k_pos = (n_idx - 1) * ATTN_BLOCK + jnp.arange(2 * ATTN_BLOCK)[None, None, :]
    rel = q_pos - k_pos
    band = (rel >= 0) & (rel < WINDOW) & (k_pos >= 0)
    s = jnp.where(band[None, :, None, None], s, -jnp.inf)
    sink = sinks.astype(jnp.float32).reshape(ATTN_KV_HEADS, ATTN_GROUP)[None, None, :, :, None, None]
    sink = jnp.broadcast_to(sink, s.shape[:-1] + (1,))
    probs = jax.nn.softmax(jnp.concatenate([s, sink], axis=-1), axis=-1)[..., :-1]
    o = jnp.einsum('bnkgqs,bnskd->bnqkgd', probs.astype(vv.dtype), vv)
    return o.reshape(bsz, seqlen, nq) @ w_o + b_o

def swiglu(x, w_gate, w_up, w_down):
    return (jax.nn.silu(x @ w_gate) * (x @ w_up)) @ w_down

def first_inputs(seed: int = 0) -> dict:
    key = jax.random.key(seed)
    ks = jax.random.split(key, 32)
    f32 = jnp.float32

    def nrm(k, shape, scale):
        return jax.random.normal(k, shape, f32) * scale

    x = nrm(ks[0], (BATCH, SEQ, D_MODEL), 1.0)
    p = nrm(ks[1], (DEPTH, BATCH, SEQ, PLE_DIM), 1.0)
    w_in_mix = nrm(ks[2], (N_EVEN, D_MODEL, MIX_IN), D_MODEL ** -0.5)
    ssd_conv_w = nrm(ks[3], (N_EVEN, SSD_CONV, SSD_XBC), SSD_CONV ** -0.5)
    ssd_conv_b = nrm(ks[4], (N_EVEN, SSD_XBC), 0.02)
    dt0 = jnp.exp(jax.random.uniform(ks[5], (N_EVEN, SSD_HEADS), f32, math.log(1e-3), math.log(1e-1)))
    ssd_dt_bias = dt0 + jnp.log(-jnp.expm1(-dt0))
    ssd_a_log = jnp.log(jax.random.uniform(ks[6], (N_EVEN, SSD_HEADS), f32, 1.0, 16.0))
    ssd_d = 1.0 + nrm(ks[7], (N_EVEN, SSD_HEADS), 0.1)
    ssd_norm_w = 1.0 + nrm(ks[8], (N_EVEN, SSD_INNER), 0.02)
    sc_conv_w = nrm(ks[9], (N_EVEN, SC_CONV, SC_DIM), SC_CONV ** -0.5)
    w_out_mix = nrm(ks[10], (N_EVEN, MIX_OUT, D_MODEL), BETA * MIX_OUT ** -0.5)
    w_qkv = nrm(ks[11], (N_ODD, D_MODEL, QKV_DIM), D_MODEL ** -0.5)
    b_qkv = nrm(ks[12], (N_ODD, QKV_DIM), 0.02)
    attn_sinks = nrm(ks[13], (N_ODD, ATTN_HEADS), 0.5)
    w_o = nrm(ks[14], (N_ODD, ATTN_HEADS * ATTN_HEAD_DIM, D_MODEL), BETA * (ATTN_HEADS * ATTN_HEAD_DIM) ** -0.5)
    b_o = nrm(ks[15], (N_ODD, D_MODEL), 0.02)
    ln_mix_g = 1.0 + nrm(ks[16], (DEPTH, D_MODEL), 0.02)
    ln_mix_b = nrm(ks[17], (DEPTH, D_MODEL), 0.02)
    w_ffn_gate = nrm(ks[18], (DEPTH, D_MODEL, D_FF), D_MODEL ** -0.5)
    w_ffn_up = nrm(ks[19], (DEPTH, D_MODEL, D_FF), D_MODEL ** -0.5)
    w_ffn_down = nrm(ks[20], (DEPTH, D_FF, D_MODEL), BETA * D_FF ** -0.5)
    ln_ffn_g = 1.0 + nrm(ks[21], (DEPTH, D_MODEL), 0.02)
    ln_ffn_b = nrm(ks[22], (DEPTH, D_MODEL), 0.02)
    w_ple = nrm(ks[23], (DEPTH, PLE_DIM, D_MODEL), PLE_DIM ** -0.5)
    w_ple_gate = nrm(ks[24], (DEPTH, D_MODEL, D_MODEL), D_MODEL ** -0.5)
    b_ple_gate = nrm(ks[25], (DEPTH, D_MODEL), 0.02)
    return {'x': x, 'p': p, 'w_in_mix': w_in_mix, 'ssd_conv_w': ssd_conv_w, 'ssd_conv_b': ssd_conv_b,
            'ssd_dt_bias': ssd_dt_bias, 'ssd_a_log': ssd_a_log, 'ssd_d': ssd_d, 'ssd_norm_w': ssd_norm_w,
            'sc_conv_w': sc_conv_w, 'w_out_mix': w_out_mix, 'w_qkv': w_qkv, 'b_qkv': b_qkv,
            'attn_sinks': attn_sinks, 'w_o': w_o, 'b_o': b_o, 'ln_mix_g': ln_mix_g, 'ln_mix_b': ln_mix_b,
            'w_ffn_gate': w_ffn_gate, 'w_ffn_up': w_ffn_up, 'w_ffn_down': w_ffn_down,
            'ln_ffn_g': ln_ffn_g, 'ln_ffn_b': ln_ffn_b, 'w_ple': w_ple, 'w_ple_gate': w_ple_gate,
            'b_ple_gate': b_ple_gate}

def first_block(x, p, w_in_mix, ssd_conv_w, ssd_conv_b, ssd_dt_bias, ssd_a_log, ssd_d, ssd_norm_w,
              sc_conv_w, w_out_mix, w_qkv, b_qkv, attn_sinks, w_o, b_o, ln_mix_g, ln_mix_b,
              w_ffn_gate, w_ffn_up, w_ffn_down, ln_ffn_g, ln_ffn_b, w_ple, w_ple_gate, b_ple_gate):
    for i in range(DEPTH):
        j = i // 2
        if i % 2 == 0:
            mix = ssd_shortconv_layer_mixer(x, w_in_mix[j], ssd_conv_w[j], ssd_conv_b[j], ssd_dt_bias[j],
                                            ssd_a_log[j], ssd_d[j], ssd_norm_w[j], sc_conv_w[j], w_out_mix[j])
        else:
            mix = sliding_window_attention(x, w_qkv[j], b_qkv[j], attn_sinks[j], w_o[j], b_o[j])
        x = layer_norm(ALPHA * x + mix.astype(x.dtype), ln_mix_g[i], ln_mix_b[i])
        x = layer_norm(ALPHA * x + swiglu(x, w_ffn_gate[i], w_ffn_up[i], w_ffn_down[i]), ln_ffn_g[i], ln_ffn_b[i])
        gate = jax.nn.sigmoid(x @ w_ple_gate[i] + b_ple_gate[i])
        x = x + (p[i] @ w_ple[i]) * gate
    return x


DEPTH_2 = 1

CHUNK = 64
D_MIX = D_MODEL
HEAD_DIM = 64
D_RWKV = D_MIX // 2
D_SB = D_MIX - D_RWKV
H_RWKV = D_RWKV // HEAD_DIM
H_SB = D_SB // HEAD_DIM
DECAY_LORA = 64
ICLR_LORA = 64
GATE_LORA = 128
VRES_LORA = 32
C_RWKV = 3 * D_RWKV + DECAY_LORA + ICLR_LORA + GATE_LORA
C_IN = C_RWKV + 3 * D_SB
SB_BLOCK = 128
N_EXPERTS = 32
TOP_K = 4
D_FF_EXPERT = D_MODEL
SWIGLU_ALPHA = 1.702
SWIGLU_LIMIT = 7.0
MOE_BLOCK = 128
NORM_EPS = 1e-6
GN_EPS = 1e-5 * HEAD_DIM
L2_EPS = 1e-12


def rms_norm(x, g):
    xf = x.astype(jnp.float32)
    y = xf * lax.rsqrt(jnp.mean(jnp.square(xf), axis=-1, keepdims=True) + NORM_EPS)
    return (y * g.astype(jnp.float32)).astype(x.dtype)

def token_shift(z, mu):
    z_prev = jnp.pad(z[:, :-1], ((0, 0), (1, 0), (0, 0)))
    return z + (z_prev - z) * mu

def split_heads(t, n_heads):
    bsz, seq, _ = t.shape
    return t.reshape(bsz, seq, n_heads, HEAD_DIM)

def rwkv7_recurrence(r, decay, k, v, kk, a):
    bsz, seq, nh, hd = r.shape
    n_chunks = seq // CHUNK

    def to_chunks(t):
        return jnp.transpose(t, (1, 0, 2, 3)).reshape(n_chunks, CHUNK, bsz, nh, hd)

    def step(state, inp):
        r_t, w_t, k_t, v_t, kk_t, a_t = inp
        s_kk = jnp.einsum('bhvk,bhk->bhv', state, kk_t)
        state = (state * w_t[:, :, None, :]
                 - s_kk[..., None] * (kk_t * a_t)[:, :, None, :]
                 + v_t[..., None] * k_t[:, :, None, :])
        return state, jnp.einsum('bhvk,bhk->bhv', state, r_t)

    def chunk_step(state, chunk):
        return lax.scan(step, state, chunk)

    s0 = jnp.zeros((bsz, nh, hd, hd), jnp.float32)
    xs = tuple(to_chunks(t) for t in (r, decay, k, v, kk, a))
    _, y = lax.scan(chunk_step, s0, xs)
    return jnp.transpose(y.reshape(seq, bsz, nh, hd), (1, 0, 2, 3))

def rwkv7_time_mix(z, v_first, mu, decay_w0, decay_up, iclr_a0, iclr_up, gate_up,
                   k_k, k_a, r_k, lnx_w, lnx_b, vres):
    bsz, seq, _ = z.shape
    zs = token_shift(z, mu)
    r = zs[..., :D_RWKV]
    k = zs[..., D_RWKV:2 * D_RWKV]
    v = zs[..., 2 * D_RWKV:3 * D_RWKV]
    o = 3 * D_RWKV
    w_lo = zs[..., o:o + DECAY_LORA]
    a_lo = zs[..., o + DECAY_LORA:o + DECAY_LORA + ICLR_LORA]
    g_lo = zs[..., o + DECAY_LORA + ICLR_LORA:]
    w_pre = (decay_w0 + jnp.tanh(w_lo) @ decay_up).astype(jnp.float32)
    log_decay = -jnp.exp(-jax.nn.softplus(-w_pre) - 0.5)
    a = jax.nn.sigmoid(iclr_a0 + a_lo @ iclr_up)
    g = jax.nn.sigmoid(g_lo) @ gate_up
    if vres is None:
        v_first = v
    else:
        vres_down, vres_up, vres_b = vres
        v = v + (v_first - v) * jax.nn.sigmoid(vres_b + (v @ vres_down) @ vres_up)
    kk = split_heads((k * k_k).astype(jnp.float32), H_RWKV)
    kk = kk / jnp.maximum(jnp.sqrt(jnp.sum(jnp.square(kk), axis=-1, keepdims=True)), L2_EPS)
    k = k * (1.0 + (a - 1.0) * k_a)
    rh = split_heads(r.astype(jnp.float32), H_RWKV)
    kh = split_heads(k.astype(jnp.float32), H_RWKV)
    vh = split_heads(v.astype(jnp.float32), H_RWKV)
    ah = split_heads(a.astype(jnp.float32), H_RWKV)
    wh = split_heads(jnp.exp(log_decay), H_RWKV)
    y = rwkv7_recurrence(rh, wh, kh, vh, kk, ah)
    mean = jnp.mean(y, axis=-1, keepdims=True)
    var = jnp.mean(jnp.square(y - mean), axis=-1, keepdims=True)
    y = ((y - mean) * lax.rsqrt(var + GN_EPS)).reshape(bsz, seq, D_RWKV)
    y = y * lnx_w.astype(jnp.float32) + lnx_b.astype(jnp.float32)
    bonus = jnp.sum(rh * kh * r_k.astype(jnp.float32), axis=-1, keepdims=True) * vh
    out = (y + bonus.reshape(bsz, seq, D_RWKV)) * g.astype(jnp.float32)
    return out.astype(z.dtype), v_first

def stick_breaking_attention(q, k, v, q_norm_g, k_norm_g, out_g):
    bsz, seq, _ = q.shape
    qh = jnp.transpose(rms_norm(split_heads(q, H_SB), q_norm_g).astype(jnp.float32), (0, 2, 1, 3))
    kh = jnp.transpose(rms_norm(split_heads(k, H_SB), k_norm_g).astype(jnp.float32), (0, 2, 1, 3))
    vh = jnp.transpose(split_heads(v, H_SB).astype(jnp.float32), (0, 2, 1, 3))
    scale = 1.0 / math.sqrt(HEAD_DIM)
    blocks = []
    for blk in range(seq // SB_BLOCK):
        t0 = blk * SB_BLOCK
        t1 = t0 + SB_BLOCK
        logits = jnp.einsum('bhqd,bhkd->bhqk', qh[:, :, t0:t1], kh[:, :, :t1]) * scale
        mask = jnp.arange(t1)[None, :] < jnp.arange(t0, t1)[:, None]
        log_keep = jnp.where(mask, jax.nn.log_sigmoid(-logits), 0.0)
        log_between = lax.cumsum(log_keep, axis=3, reverse=True) - log_keep
        weight = jnp.where(mask, jnp.exp(jax.nn.log_sigmoid(logits) + log_between), 0.0)
        blocks.append(jnp.einsum('bhqk,bhkd->bhqd', weight, vh[:, :, :t1]))
    o = jnp.transpose(jnp.concatenate(blocks, axis=2), (0, 2, 1, 3))
    o = rms_norm(o, out_g.reshape(H_SB, HEAD_DIM))
    return o.reshape(bsz, seq, D_SB).astype(q.dtype)

def moe_ffn(h, router_w, router_b, w1, b1, w2, b2):
    bsz, seq, d = h.shape
    n_tok = bsz * seq
    xt = h.reshape(n_tok, d)
    logits = xt.astype(jnp.float32) @ router_w.astype(jnp.float32) + router_b.astype(jnp.float32)
    top_logit, top_idx = lax.top_k(logits, TOP_K)
    top_gate = jax.nn.softmax(top_logit, axis=-1)
    n_assign = n_tok * TOP_K
    flat_e = top_idx.reshape(-1)
    flat_tok = jnp.arange(n_assign, dtype=jnp.int32) // TOP_K
    order = jnp.argsort(flat_e, stable=True)
    e_sorted = flat_e[order]
    counts = jnp.bincount(flat_e, length=N_EXPERTS)
    padded = (counts + MOE_BLOCK - 1) // MOE_BLOCK * MOE_BLOCK
    padded_end = jnp.cumsum(padded)
    padded_start = padded_end - padded
    start = jnp.cumsum(counts) - counts
    dest = padded_start[e_sorted] + jnp.arange(n_assign, dtype=jnp.int32) - start[e_sorted]
    n_rows = n_assign + N_EXPERTS * MOE_BLOCK
    n_blocks = n_rows // MOE_BLOCK
    row_tok = jnp.zeros((n_rows,), jnp.int32).at[dest].set(flat_tok[order])
    row_gate = jnp.zeros((n_rows,), h.dtype).at[dest].set(top_gate.reshape(-1)[order].astype(h.dtype))
    block_expert = jnp.minimum(
        jnp.searchsorted(padded_end, jnp.arange(n_blocks, dtype=jnp.int32) * MOE_BLOCK, side='right'),
        N_EXPERTS - 1)

    def expert_block(args):
        tok, gate, e = args
        xb = xt[tok]
        hid = xb @ w1[e] + b1[e]
        glu = jnp.minimum(hid[:, :D_FF_EXPERT], SWIGLU_LIMIT)
        lin = jnp.clip(hid[:, D_FF_EXPERT:], -SWIGLU_LIMIT, SWIGLU_LIMIT)
        act = glu * jax.nn.sigmoid(SWIGLU_ALPHA * glu) * (lin + 1.0)
        return (act @ w2[e] + b2[e]) * gate[:, None]

    y = lax.map(expert_block, (row_tok.reshape(n_blocks, MOE_BLOCK),
                               row_gate.reshape(n_blocks, MOE_BLOCK), block_expert))
    out = jax.ops.segment_sum(y.reshape(n_rows, d), row_tok, num_segments=n_tok)
    return out.reshape(bsz, seq, d)

def second_inputs(seed: int = 0) -> dict:
    key = jax.random.key(seed)
    ks = iter(jax.random.split(key, 40))

    def normal(shape, scale):
        return jax.random.normal(next(ks), shape, jnp.float32) * scale

    def gain(shape, s=0.02):
        return 1.0 + normal(shape, s)

    L = DEPTH_2
    LV = max(DEPTH_2 - 1, 0)
    return {
        'x': normal((BATCH, SEQ, D_MODEL), 1.0),
        'c': normal((BATCH, D_MODEL), 1.0),
        'norm1_g': gain((L, D_MODEL)),
        'norm2_g': gain((L, D_MODEL)),
        'ada_w': normal((L, D_MODEL, 6 * D_MODEL), 0.5 * D_MODEL ** -0.5),
        'ada_b': normal((L, 6 * D_MODEL), 0.02),
        'w_in': normal((L, D_MODEL, C_IN), D_MODEL ** -0.5),
        'shift_mu': jax.random.uniform(next(ks), (L, C_RWKV), jnp.float32),
        'decay_w0': jax.random.uniform(next(ks), (L, D_RWKV), jnp.float32, -1.5, 1.5),
        'decay_up': normal((L, DECAY_LORA, D_RWKV), 0.5 * DECAY_LORA ** -0.5),
        'iclr_a0': normal((L, D_RWKV), 0.1),
        'iclr_up': normal((L, ICLR_LORA, D_RWKV), 0.5 * ICLR_LORA ** -0.5),
        'gate_up': normal((L, GATE_LORA, D_RWKV), GATE_LORA ** -0.5),
        'k_k': gain((L, D_RWKV), 0.1),
        'k_a': gain((L, D_RWKV), 0.1),
        'r_k': normal((L, H_RWKV, HEAD_DIM), 0.1),
        'lnx_w': gain((L, D_RWKV)),
        'lnx_b': normal((L, D_RWKV), 0.02),
        'vres_down': normal((LV, D_RWKV, VRES_LORA), D_RWKV ** -0.5),
        'vres_up': normal((LV, VRES_LORA, D_RWKV), 0.5 * VRES_LORA ** -0.5),
        'vres_b': normal((LV, D_RWKV), 0.1),
        'q_norm_g': gain((L, HEAD_DIM)),
        'k_norm_g': gain((L, HEAD_DIM)),
        'sb_out_g': gain((L, D_SB)),
        'w_out': normal((L, D_MIX, D_MODEL), D_MIX ** -0.5),
        'router_w': normal((L, D_MODEL, N_EXPERTS), D_MODEL ** -0.5),
        'router_b': normal((L, N_EXPERTS), 0.01),
        'exp_w1': normal((L, N_EXPERTS, D_MODEL, 2 * D_FF_EXPERT), D_MODEL ** -0.5),
        'exp_b1': normal((L, N_EXPERTS, 2 * D_FF_EXPERT), 0.02),
        'exp_w2': normal((L, N_EXPERTS, D_FF_EXPERT, D_MODEL), D_FF_EXPERT ** -0.5),
        'exp_b2': normal((L, N_EXPERTS, D_MODEL), 0.02),
    }

def second_block(x, c, norm1_g, norm2_g, ada_w, ada_b, w_in, shift_mu, decay_w0, decay_up,
              iclr_a0, iclr_up, gate_up, k_k, k_a, r_k, lnx_w, lnx_b, vres_down, vres_up,
              vres_b, q_norm_g, k_norm_g, sb_out_g, w_out, router_w, router_b,
              exp_w1, exp_b1, exp_w2, exp_b2):
    cond = jax.nn.silu(c)
    v_first = None
    for l in range(DEPTH_2):
        mod = cond @ ada_w[l] + ada_b[l]
        shift1, scale1, gate1, shift2, scale2, gate2 = jnp.split(mod[:, None, :], 6, axis=-1)
        h = rms_norm(x, norm1_g[l]) * (1.0 + scale1) + shift1
        z = h @ w_in[l]
        vres = None if l == 0 else (vres_down[l - 1], vres_up[l - 1], vres_b[l - 1])
        y_rwkv, v_first = rwkv7_time_mix(
            z[..., :C_RWKV], v_first, shift_mu[l], decay_w0[l], decay_up[l], iclr_a0[l],
            iclr_up[l], gate_up[l], k_k[l], k_a[l], r_k[l], lnx_w[l], lnx_b[l], vres)
        z_sb = z[..., C_RWKV:]
        y_sb = stick_breaking_attention(
            z_sb[..., :D_SB], z_sb[..., D_SB:2 * D_SB], z_sb[..., 2 * D_SB:],
            q_norm_g[l], k_norm_g[l], sb_out_g[l])
        mixed = jnp.concatenate([y_rwkv, y_sb], axis=-1) @ w_out[l]
        x = x + gate1 * mixed
        h2 = rms_norm(x, norm2_g[l]) * (1.0 + scale2) + shift2
        x = x + gate2 * moe_ffn(h2, router_w[l], router_b[l], exp_w1[l], exp_b1[l],
                                exp_w2[l], exp_b2[l])
    return x


DEPTH_3 = 1

MLA_HEADS = 8
MLA_NOPE_DIM = 64
MLA_ROPE_DIM = 32
MLA_V_DIM = 64
MLA_Q_RANK = 256
MLA_KV_RANK = 128
MLA_WIDTH = MLA_HEADS * MLA_V_DIM
MOBA_HEADS = 8
MOBA_HEAD_DIM = 64
MOBA_WIDTH = MOBA_HEADS * MOBA_HEAD_DIM
MOBA_BLOCK = 256
MOBA_TOPK = 3
MOBA_Q_CHUNK = 16
ATTN_Q_BLOCK = 128
ROPE_THETA = 10000.0
EPS = 1e-6
N_BRANCHES = 2
IN_SIZES = (MLA_Q_RANK, MLA_KV_RANK, MLA_ROPE_DIM, MLA_WIDTH,
            MOBA_WIDTH, MOBA_WIDTH, MOBA_WIDTH, MOBA_WIDTH, N_BRANCHES * D_MODEL)
D_IN = MLA_Q_RANK + MLA_KV_RANK + MLA_ROPE_DIM + MLA_WIDTH + 4 * MOBA_WIDTH + N_BRANCHES * D_MODEL


def rms_norm_3(t, g):
    tf = t.astype(jnp.float32)
    tf = tf * lax.rsqrt(jnp.mean(tf * tf, axis=-1, keepdims=True) + EPS)
    return (tf * g.astype(jnp.float32)).astype(t.dtype)

def apply_rope(t, positions):
    half = t.shape[-1] // 2
    inv_freq = ROPE_THETA ** (-jnp.arange(half, dtype=jnp.float32) / half)
    ang = positions.astype(jnp.float32)[:, :, None, None] * inv_freq
    cos, sin = jnp.cos(ang), jnp.sin(ang)
    tf = t.astype(jnp.float32)
    t1, t2 = tf[..., :half], tf[..., half:]
    return jnp.concatenate([t1 * cos - t2 * sin, t2 * cos + t1 * sin], axis=-1).astype(t.dtype)

def split_cols(t, sizes):
    outs, start = [], 0
    for n in sizes:
        outs.append(t[..., start:start + n])
        start += n
    return outs

def causal_dense_attention(q, k, v, scale):
    B, S, H, _ = q.shape
    kpos = jnp.arange(S)

    def one_block(i):
        start = i * ATTN_Q_BLOCK
        qb = lax.dynamic_slice_in_dim(q, start, ATTN_Q_BLOCK, axis=1)
        s = jnp.einsum('bqhd,bkhd->bhqk', qb, k).astype(jnp.float32) * scale
        qpos = start + jnp.arange(ATTN_Q_BLOCK)
        s = jnp.where(kpos[None, :] <= qpos[:, None], s, -jnp.inf)
        p = jax.nn.softmax(s, axis=-1).astype(v.dtype)
        return jnp.einsum('bhqk,bkhd->bqhd', p, v)

    out = lax.map(one_block, jnp.arange(S // ATTN_Q_BLOCK))
    return out.transpose(1, 0, 2, 3, 4).reshape(B, S, H, v.shape[-1])

def moba_attention(q, k, v):
    B, S, H, dh = q.shape
    nb = -(-S // MOBA_BLOCK)
    n_top = min(MOBA_TOPK, nb)
    pad = nb * MOBA_BLOCK - S
    kp = jnp.pad(k, ((0, 0), (0, pad), (0, 0), (0, 0)))
    vp = jnp.pad(v, ((0, 0), (0, pad), (0, 0), (0, 0)))
    kb = kp.reshape(B, nb, MOBA_BLOCK, H, dh).transpose(0, 3, 1, 2, 4)
    vb = vp.reshape(B, nb, MOBA_BLOCK, H, dh).transpose(0, 3, 1, 2, 4)
    kmean = jnp.mean(kb.astype(jnp.float32), axis=3)
    scale = dh ** -0.5
    bi = jnp.arange(B)[:, None, None, None]
    hi = jnp.arange(H)[None, :, None, None]
    in_blk = jnp.arange(MOBA_BLOCK)
    blk_ids = jnp.arange(nb)
    n_sel = n_top * MOBA_BLOCK

    def one_chunk(i):
        start = i * MOBA_Q_CHUNK
        qc = lax.dynamic_slice_in_dim(q, start, MOBA_Q_CHUNK, axis=1)
        qpos = start + jnp.arange(MOBA_Q_CHUNK)
        own = start // MOBA_BLOCK
        gate = jnp.einsum('bqhd,bhnd->bhqn', qc.astype(jnp.float32), kmean)
        gate = jnp.where(blk_ids < own, gate, -jnp.inf)
        _, idx = lax.top_k(gate, n_top)
        valid = jnp.arange(n_top) < own
        k_sel = kb[bi, hi, idx]
        v_sel = vb[bi, hi, idx]
        s_sel = jnp.einsum('bqhd,bhqnkd->bhqnk', qc, k_sel).astype(jnp.float32) * scale
        s_sel = jnp.where(valid[:, None], s_sel, -jnp.inf)
        k_own = lax.dynamic_index_in_dim(kb, own, axis=2, keepdims=False)
        v_own = lax.dynamic_index_in_dim(vb, own, axis=2, keepdims=False)
        s_own = jnp.einsum('bqhd,bhkd->bhqk', qc, k_own).astype(jnp.float32) * scale
        kpos_own = own * MOBA_BLOCK + in_blk
        s_own = jnp.where(kpos_own[None, :] <= qpos[:, None], s_own, -jnp.inf)
        s = jnp.concatenate([s_sel.reshape(B, H, MOBA_Q_CHUNK, n_sel), s_own], axis=-1)
        p = jax.nn.softmax(s, axis=-1).astype(v.dtype)
        p_sel = p[..., :n_sel].reshape(B, H, MOBA_Q_CHUNK, n_top, MOBA_BLOCK)
        p_own = p[..., n_sel:]
        return (jnp.einsum('bhqnk,bhqnkd->bqhd', p_sel, v_sel)
                + jnp.einsum('bhqk,bhkd->bqhd', p_own, v_own))

    out = lax.map(one_chunk, jnp.arange(S // MOBA_Q_CHUNK))
    return out.transpose(1, 0, 2, 3, 4).reshape(B, S, H, dh)

def third_inputs(seed: int = 0) -> dict:
    key = jax.random.key(seed)
    ks = jax.random.split(key, 20)

    def w(k, shape, fan_in, mult=1.0):
        return jax.random.normal(k, shape, jnp.float32) * (mult * fan_in ** -0.5)

    def gain(k, n):
        return 1.0 + 0.05 * jax.random.normal(k, (DEPTH_3, n), jnp.float32)

    x = jax.random.normal(ks[0], (BATCH, SEQ, D_MODEL), jnp.float32)
    c = jax.random.normal(ks[1], (BATCH, D_MODEL), jnp.float32)
    offset = jax.random.randint(ks[2], (BATCH, 1), 0, 1024, dtype=jnp.int32)
    positions = (offset + jnp.arange(SEQ, dtype=jnp.int32)[None, :]).astype(jnp.int32)
    return {
        "x": x,
        "c": c,
        "positions": positions,
        "w_ada": w(ks[3], (DEPTH_3, D_MODEL, 3 * D_MODEL), D_MODEL, 0.5),
        "b_ada": 0.01 * jax.random.normal(ks[4], (DEPTH_3, 3 * D_MODEL), jnp.float32),
        "g_pre": gain(ks[5], D_MODEL),
        "g_post": gain(ks[6], D_MODEL),
        "w_in": w(ks[7], (DEPTH_3, D_MODEL, D_IN), D_MODEL),
        "g_q_lat": gain(ks[8], MLA_Q_RANK),
        "w_uq": w(ks[9], (DEPTH_3, MLA_Q_RANK, MLA_HEADS * (MLA_NOPE_DIM + MLA_ROPE_DIM)), MLA_Q_RANK),
        "g_kv_lat": gain(ks[10], MLA_KV_RANK),
        "w_ukv": w(ks[11], (DEPTH_3, MLA_KV_RANK, MLA_HEADS * (MLA_NOPE_DIM + MLA_V_DIM)), MLA_KV_RANK),
        "w_o_mla": w(ks[12], (DEPTH_3, MLA_WIDTH, D_MODEL), MLA_WIDTH),
        "w_o_moba": w(ks[13], (DEPTH_3, MOBA_WIDTH, D_MODEL), MOBA_WIDTH),
        "b_merge": 0.01 * jax.random.normal(ks[14], (DEPTH_3, N_BRANCHES * D_MODEL), jnp.float32),
        "w_out": w(ks[15], (DEPTH_3, D_MODEL, D_MODEL), D_MODEL),
    }

def third_block(x, c, positions, w_ada, b_ada, g_pre, g_post, w_in, g_q_lat, w_uq,
              g_kv_lat, w_ukv, w_o_mla, w_o_moba, b_merge, w_out):
    B, S, D = x.shape
    for l in range(DEPTH_3):
        mod = jax.nn.silu(c) @ w_ada[l] + b_ada[l]
        shift, scale, gate = jnp.split(mod, 3, axis=-1)
        h = rms_norm_3(x, g_pre[l]) * (1 + scale[:, None, :]) + shift[:, None, :]

        proj = h @ w_in[l]
        (q_lat, kv_lat, k_rope, z_mla, q_mb, k_mb, v_mb, z_mb,
         merge_logits) = split_cols(proj, IN_SIZES)

        q = (rms_norm_3(q_lat, g_q_lat[l]) @ w_uq[l]).reshape(B, S, MLA_HEADS, MLA_NOPE_DIM + MLA_ROPE_DIM)
        q_nope, q_pe = q[..., :MLA_NOPE_DIM], q[..., MLA_NOPE_DIM:]
        kv = (rms_norm_3(kv_lat, g_kv_lat[l]) @ w_ukv[l]).reshape(B, S, MLA_HEADS, MLA_NOPE_DIM + MLA_V_DIM)
        k_nope, v_mla = kv[..., :MLA_NOPE_DIM], kv[..., MLA_NOPE_DIM:]
        q_pe = apply_rope(q_pe, positions)
        k_pe = apply_rope(k_rope[:, :, None, :], positions)
        q_full = jnp.concatenate([q_nope, q_pe], axis=-1)
        k_full = jnp.concatenate([k_nope, jnp.broadcast_to(k_pe, (B, S, MLA_HEADS, MLA_ROPE_DIM))], axis=-1)
        o_mla = causal_dense_attention(q_full, k_full, v_mla,
                                       (MLA_NOPE_DIM + MLA_ROPE_DIM) ** -0.5).reshape(B, S, MLA_WIDTH)
        y_mla = (o_mla * jax.nn.silu(z_mla)) @ w_o_mla[l]

        qm = apply_rope(q_mb.reshape(B, S, MOBA_HEADS, MOBA_HEAD_DIM), positions)
        km = apply_rope(k_mb.reshape(B, S, MOBA_HEADS, MOBA_HEAD_DIM), positions)
        vm = v_mb.reshape(B, S, MOBA_HEADS, MOBA_HEAD_DIM)
        o_mb = moba_attention(qm, km, vm).reshape(B, S, MOBA_WIDTH)
        y_mb = (o_mb * jax.nn.silu(z_mb)) @ w_o_moba[l]

        gates = jax.nn.sigmoid(merge_logits + b_merge[l])
        g_a, g_b = jnp.split(gates, 2, axis=-1)
        y = (g_a * y_mla + g_b * y_mb) @ w_out[l]

        x = x + gate[:, None, :] * rms_norm_3(y, g_post[l])
    return x


def setup_inputs(seed=0):
    out = dict(first_inputs(seed))
    for name, value in second_inputs(seed + 1).items():
        if name != "x":
            out[name + "_2"] = value
    for name, value in third_inputs(seed + 2).items():
        if name != "x":
            out[name + "_3"] = value
    return out


def reference(
    x, p, w_in_mix, ssd_conv_w, ssd_conv_b, ssd_dt_bias, ssd_a_log, ssd_d, ssd_norm_w,
    sc_conv_w, w_out_mix, w_qkv, b_qkv, attn_sinks, w_o, b_o, ln_mix_g, ln_mix_b, w_ffn_gate,
    w_ffn_up, w_ffn_down, ln_ffn_g, ln_ffn_b, w_ple, w_ple_gate, b_ple_gate, c_2, norm1_g_2,
    norm2_g_2, ada_w_2, ada_b_2, w_in_2, shift_mu_2, decay_w0_2, decay_up_2, iclr_a0_2,
    iclr_up_2, gate_up_2, k_k_2, k_a_2, r_k_2, lnx_w_2, lnx_b_2, vres_down_2, vres_up_2,
    vres_b_2, q_norm_g_2, k_norm_g_2, sb_out_g_2, w_out_2, router_w_2, router_b_2, exp_w1_2,
    exp_b1_2, exp_w2_2, exp_b2_2, c_3, positions_3, w_ada_3, b_ada_3, g_pre_3, g_post_3, w_in_3,
    g_q_lat_3, w_uq_3, g_kv_lat_3, w_ukv_3, w_o_mla_3, w_o_moba_3, b_merge_3, w_out_3,
):
    x = first_block(
        x, p, w_in_mix, ssd_conv_w, ssd_conv_b, ssd_dt_bias, ssd_a_log, ssd_d, ssd_norm_w,
        sc_conv_w, w_out_mix, w_qkv, b_qkv, attn_sinks, w_o, b_o, ln_mix_g, ln_mix_b,
        w_ffn_gate, w_ffn_up, w_ffn_down, ln_ffn_g, ln_ffn_b, w_ple, w_ple_gate, b_ple_gate,
    )
    x = second_block(
        x, c_2, norm1_g_2, norm2_g_2, ada_w_2, ada_b_2, w_in_2, shift_mu_2, decay_w0_2,
        decay_up_2, iclr_a0_2, iclr_up_2, gate_up_2, k_k_2, k_a_2, r_k_2, lnx_w_2, lnx_b_2,
        vres_down_2, vres_up_2, vres_b_2, q_norm_g_2, k_norm_g_2, sb_out_g_2, w_out_2,
        router_w_2, router_b_2, exp_w1_2, exp_b1_2, exp_w2_2, exp_b2_2,
    )
    return third_block(
        x, c_3, positions_3, w_ada_3, b_ada_3, g_pre_3, g_post_3, w_in_3, g_q_lat_3, w_uq_3,
        g_kv_lat_3, w_ukv_3, w_o_mla_3, w_o_moba_3, b_merge_3, w_out_3,
    )


_drawn_inputs = setup_inputs


def setup_inputs(seed=0):
    import zlib

    import numpy as np

    out = dict(_drawn_inputs(seed))
    spreads = {}
    factors = {'ssd_conv_b': 6.449,
     'ssd_d': 3.119,
     'ssd_norm_w': 8.0,
     'b_qkv': 5.614,
     'attn_sinks': 8.0,
     'b_o': 3.273,
     'b_ple_gate': 6.59,
     'norm1_g_2': 5.566,
     'norm2_g_2': 18.833,
     'decay_up_2': 4.528,
     'iclr_a0_2': 7.187,
     'k_k_2': 53.048,
     'k_a_2': 3.154,
     'lnx_w_2': 64.0,
     'lnx_b_2': 64.0,
     'q_norm_g_2': 33.081,
     'k_norm_g_2': 45.304,
     'sb_out_g_2': 54.048,
     'router_b_2': 53.896,
     'exp_b1_2': 41.088,
     'exp_b2_2': 64.0,
     'b_ada_3': 4.96,
     'g_pre_3': 3.423,
     'g_post_3': 37.76,
     'g_q_lat_3': 24.439,
     'g_kv_lat_3': 16.622,
     'b_merge_3': 64.0}
    for name, (base, spread) in spreads.items():
        noise = np.random.default_rng([zlib.crc32(name.encode()), seed]).standard_normal(out[name].shape)
        drawn = base * np.exp(spread * noise) if base else spread * noise
        out[name] = jnp.asarray(drawn.astype(out[name].dtype))
    for name, factor in factors.items():
        out[name] = (out[name] * factor).astype(out[name].dtype)
    return out
```

```python
import numpy as np
from contextlib import ExitStack

import concourse.bass as bass
from concourse import mybir

F32 = mybir.dt.float32
I32 = mybir.dt.int32
U32 = mybir.dt.uint32
ALU = mybir.AluOpType
ACT = mybir.ActivationFunctionType
AX = mybir.AxisListType.X

P = 128
TOK = 256
NB = TOK // P
D = 1024
DT = D // P
DEPTH = 2
PANEL = 256
KG = 8
RING = 6
SLOT = KG * PANEL
ALPHA = (2 * DEPTH) ** 0.25
LN_EPS = 1e-5

SSD_HEADS, SSD_CHUNK, SSD_CONV, SC_CONV = 16, 128, 4, 3
SSD_GROUPS, HPG = 2, 8
XBC_T = 12
D_FF = 2816
FF_T = D_FF // P
HD = 64

C_RWKV_T, CHUNK = 14, 64
N_EXPERTS, TOP_K = 32, 4
UNIT = 64
MAX_UNITS = N_EXPERTS + TOK * TOP_K // UNIT
SWIGLU_ALPHA, SWIGLU_LIMIT = 1.702, 7.0
RMS_EPS = 1e-6
BIG = 1.0e30


VECTORS = [
    ("dt_bias", 1), ("a_log", 1), ("conv_w", SSD_CONV * XBC_T), ("conv_b", XBC_T), ("sc_w", SC_CONV * DT),
    ("ssd_d", DT), ("ssd_norm", DT),
    ("ln_mix_g", 2 * DT), ("ln_mix_b", 2 * DT), ("ln_ffn_g", 2 * DT), ("ln_ffn_b", 2 * DT), ("b_ple", 2 * DT),
    ("b_qkv", 12), ("b_o", DT), ("sinks", 16),
    ("c_2", DT), ("norm1", DT), ("norm2", DT), ("ada_b_2", 48), ("mu", C_RWKV_T), ("decay_w0", 4), ("iclr_a0", 4),
    ("k_k", 4), ("k_a", 4), ("r_k", 4), ("lnx_w", 4), ("lnx_b", 4), ("q_norm", 1), ("k_norm", 1), ("sb_out", 4),
    ("router_b", N_EXPERTS),
    ("c_3", DT), ("b_ada_3", 24), ("g_pre", DT), ("g_post", DT), ("g_q_lat", 2), ("g_kv_lat", 1), ("b_merge", 16),
]
MATRICES = [
    ("ident", P), ("ones", P), ("head_ones", P), ("tri_le", P), ("tri_lt", P), ("tri_gt", P),
    ("lt64", P), ("le64", P), ("level", 6 * P), ("rot64", P), ("rot32", P), ("band", 3 * P), ("causal", 3 * P),
    ("iota_slot", UNIT), ("iota_e", N_EXPERTS), ("iota_u", MAX_UNITS), ("col_e", 1), ("invf64", 1), ("invf32", 1),
    ("scan_keep", TOK),
]


def offsets(table):
    at, out = 0, {}
    for name, n in table:
        out[name] = (at, n)
        at += n
    return out, at


def constant_matrices():
    r = np.arange(P)[:, None]
    c = np.arange(P)[None, :]
    c2 = np.arange(2 * P)[None, :]
    m = {
        "ident": r == c, "ones": np.ones((P, P)), "head_ones": r // HD == c // HD,
        "tri_le": r <= c, "tri_lt": r < c, "tri_gt": r > c,
        "lt64": (r // CHUNK == c // CHUNK) & (r < c), "le64": (r // CHUNK == c // CHUNK) & (r <= c),
    }
    m["level"] = np.concatenate([
        (r // (2 * b) == c // (2 * b)) & ((c // b) % 2 == 1) & ((r // b) % 2 == 0) for b in (1, 2, 4, 8, 16, 32)], axis=1)

    def rotation(width):
        half = width // 2
        low = c % width < half
        return np.where(low, -1.0 * (r == c + half), 1.0 * (r == c - half))

    m["rot64"] = rotation(64)
    rotated = (c >= 64) & (c < 96)
    m["rot32"] = rotation(32) * rotated
    rel = r + P - c2
    for name, ok in (("band", (rel >= 0) & (rel < 128)), ("causal", rel >= 0)):
        full = np.where(ok, 0.0, -BIG)
        m[name] = np.concatenate([full[:, P:], full], axis=1)
    m["iota_slot"] = np.broadcast_to(np.arange(UNIT), (P, UNIT))
    m["iota_e"] = np.broadcast_to(np.arange(N_EXPERTS), (P, N_EXPERTS))
    m["iota_u"] = np.broadcast_to(np.arange(MAX_UNITS), (P, MAX_UNITS))
    m["col_e"] = r
    m["invf64"] = np.float32(10000.0) ** (-(np.arange(P) % 32).astype(np.float32) / np.float32(32))[:, None]
    m["invf32"] = np.float32(10000.0) ** (-(np.arange(P) % 16).astype(np.float32) / np.float32(16))[:, None] * rotated.T
    m["scan_keep"] = np.broadcast_to((np.arange(TOK) % CHUNK != 0), (P, TOK))
    return np.concatenate([np.asarray(m[n], np.float32).reshape(P, w) for n, w in MATRICES], axis=1)


STREAM_1 = [
    ("w_in", 22, 8, 256), ("w_out", 4, 16, 256),
    ("ffn_up0", 22, 8, 256), ("ffn_dn0", 4, 22, 256), ("ple_g0", 4, 8, 256), ("ple_p0", 4, 2, 256),
    ("qkv", 6, 8, 256), ("w_o", 4, 8, 256),
    ("ffn_up1", 22, 8, 256), ("ffn_dn1", 4, 22, 256), ("ple_g1", 4, 8, 256), ("ple_p1", 4, 2, 256),
    ("ada2", 24, 8, 256), ("w_in2", 13, 8, 256), ("w_out2", 4, 8, 256),
]
STREAM_2 = [
    ("ada3", 12, 8, 256),
    ("w_in3", 20, 8, 256), ("w_uq", 4, 2, 256), ("w_ukv", 6, 1, 256),
    ("w_om", 4, 4, 256), ("w_ob", 4, 4, 256), ("w_out3", 4, 8, 256),
]


def panels_of(stream):
    out = []
    for name, n, kt, _ in stream:
        for j in range(n):
            for k0 in range(0, kt, KG):
                out.append((name, j, k0, min(KG, kt - k0)))
    return out


class Signal:

    def __init__(self, sem):
        self.sem, self.base = sem, 0

    def at(self, n):
        return self.base + n

    def close(self, n):
        self.base += n


class Core:

    def __init__(self, nc, a, ctx):
        self.nc, self.a, self.ctx = nc, a, ctx
        self.v_at, nv = offsets(VECTORS)
        self.m_at, nm = offsets(MATRICES)
        self.vec = self.sb("vec", [P, nv])
        self.mat = self.sb("mat", [P, nm])
        self.x = self.sb("x_res", [P, DT, TOK])
        self.ring = self.sb("ring", [P, RING, SLOT])
        self.ps = ctx.enter_context(nc.psum_tensor("ps", [P, 8, 512], F32))
        self.panel_loaded = [self.counter(f"panel_loaded{s}") for s in range(RING)]
        self.panel_used = self.counter("panel_used")
        self.act_evac = self.counter("act_evac")
        self.dve_evac = self.counter("dve_evac")
        self.const_loaded = self.counter("const_loaded")
        self.chain = {e: self.counter(f"{e}_chain") for e in ("pe", "act", "dve", "pool")}
        self.sem_a, self.sem_b, self.sem_c, self.sem_d, self.sem_e = (
            self.counter(n) for n in ("stage_in", "stage_mid", "stage_exp", "stage_mul", "stage_out"))
        self.sem_f, self.sem_g, self.sem_h = self.counter("stage_aux"), self.counter("stage_aux2"), self.counter("stage_end")
        small = self.sb("modulations", [P, 48 + 24 + 2 * DT])
        self.mod2, self.mod3 = small[:, 0:48], small[:, 48:72]
        self.cond2, self.cond3 = small[:, 72:80], small[:, 80:88]
        self.stream, self.issued, self.used = panels_of(STREAM_1), 0, 0

    def sb(self, name, shape, dt=F32):
        return self.ctx.enter_context(self.nc.sbuf_tensor(name, shape, dt))

    def counter(self, name):
        return Signal(self.ctx.enter_context(self.nc.semaphore(name)))

    def v(self, name, i=0, parts=P):
        at, n = self.v_at[name]
        return self.vec[0:parts, at + i:at + i + 1]

    def vs(self, name):
        at, n = self.v_at[name]
        return self.vec[:, at:at + n]

    def m(self, name, i=0, w=None):
        at, n = self.m_at[name]
        w = w or min(n, P)
        return self.mat[:, at + i * w:at + i * w + w]

    def dump(self, name, ap):
        if name in self.a:
            with self.block() as block:
                @block.scalar
                def _(act):
                    act.dma_start(self.a[name], ap).then_inc(self.const_loaded.sem, 16)
                    act.wait_ge(self.const_loaded.sem, self.const_loaded.at(16))
            self.const_loaded.close(16)

    def block(self):
        return self.nc.Block(no_gpsimd_drain=True)

    def link(self, which, eng):
        sig = self.chain[which]

        def link(ins):
            sig.base += 1
            ins.then_inc(sig.sem, 1)
            eng.wait_ge(sig.sem, sig.base)
        return link


def issue_panels(core, sp, upto):
    while core.issued < min(upto, len(core.stream)):
        i = core.issued
        name, j, k0, kn = core.stream[i]
        slot = i % RING
        if i >= RING:
            sp.wait_ge(core.panel_used.sem, core.panel_used.at(i - RING + 1))
        w = core.a[name][j, :, k0 * PANEL:(k0 + kn) * PANEL]
        sp.dma_start(core.ring[:, slot, 0:kn * PANEL], w).then_inc(core.panel_loaded[slot].sem, 16)
        core.issued += 1


def linear(core, name, src, tiles, head=None):
    nc = core.nc
    mine = []
    i = core.used
    while i < len(core.stream) and core.stream[i][0] == name:
        mine.append(i)
        i += 1
    assert mine, name
    kt = max(core.stream[i][2] + core.stream[i][3] for i in mine)
    last_panel = {core.stream[i][1]: i for i in mine}
    order = {}
    counts = {"act": 0, "dve": 0}
    for i, t in enumerate(tiles):
        counts[t[0]] += 1
        order[i] = (t[0], counts[t[0]])
    evac = {"act": core.act_evac, "dve": core.dve_evac}
    BANKS = 4

    def wait_tile(eng, i):
        which, n = order[i]
        eng.wait_ge(evac[which].sem, evac[which].at(n))

    with core.block() as block:
        @block.sync
        def _(sp):
            issue_panels(core, sp, mine[-1] + 1 + RING)

        @block.tensor
        def _(pe):
            for i in mine:
                _, j, k0, kn = core.stream[i]
                slot = i % RING
                pe.wait_ge(core.panel_loaded[slot].sem, core.panel_loaded[slot].at(16 * (i // RING + 1)))
                for c in range(2):
                    t = 2 * j + c
                    if k0 == 0 and t >= BANKS:
                        wait_tile(pe, t - BANKS)
                    for k in range(kn):
                        mm = pe.matmul(core.ps[:, t % BANKS, 0:TOK],
                                       core.ring[:, slot, k * PANEL + c * P:k * PANEL + c * P + P],
                                       src(k0 + k), start=(k0 + k == 0), stop=(k0 + k == kt - 1))
                mm.then_inc(core.panel_used.sem, 1)

        def evacuations(eng, which):
            link = core.link(which, eng)
            for i, (e, take, after) in enumerate(tiles):
                if e != which:
                    continue
                eng.wait_ge(core.panel_used.sem, core.panel_used.at(last_panel[i // 2] + 1))
                take(eng, core.ps[:, i % BANKS, 0:TOK]).then_inc(evac[which].sem, 1)
                if after is not None:
                    after(eng, link, wait_tile)

        @block.scalar
        def _(act):
            evacuations(act, "act")

        @block.vector
        def _(dve):
            if head is not None:
                head(dve, core.link("dve", dve))
            evacuations(dve, "dve")
    core.used = mine[-1] + 1
    core.act_evac.close(counts["act"])
    core.dve_evac.close(counts["dve"])


def bcast(ap, shape):
    return ap.to_broadcast(shape)


def column_sums(core, jobs):
    with core.block() as block:
        @block.tensor
        def _(pe):
            for out, mat, srcs in jobs:
                for n, s in enumerate(srcs):
                    pe.matmul(out, mat, s, start=(n == 0), stop=(n == len(srcs) - 1))


def rstd_of(core, ps, out, scale, eps):
    with core.block() as block:
        @block.vector
        def _(dve):
            dve.tensor_scalar(out, ps, scale, eps, ALU.mult, ALU.add)
    with core.block() as block:
        @block.scalar
        def _(act):
            act.activation(out, out, ACT.Sqrt)
    with core.block() as block:
        @block.vector
        def _(dve):
            dve.reciprocal(out, out)


def layer_norm(core, g, b, layer):
    x = core.x
    with ExitStack() as s:
        sq = s.enter_context(core.nc.sbuf_tensor(f"ln_sq_{g}{layer}", [P, DT, TOK], F32))
        rs = s.enter_context(core.nc.sbuf_tensor(f"ln_rs_{g}{layer}", [P, TOK], F32))
        column_sums(core, [(core.ps[:, 4, 0:TOK], core.m("ones"), [x[:, k, :] for k in range(DT)])])
        with core.block() as block:
            @block.vector
            def _(dve):
                for h in range(2):
                    part = x[:, 4 * h:4 * h + 4, :]
                    dve.scalar_tensor_tensor(out=part, in0=bcast(core.ps[:, 4:5, 0:TOK], [P, 4, TOK]), scalar=-1.0 / D,
                                             in1=part, op0=ALU.mult, op1=ALU.add).then_inc(core.sem_a.sem, 1)

            @block.scalar
            def _(act):
                for h in range(2):
                    act.wait_ge(core.sem_a.sem, core.sem_a.at(h + 1))
                    for k in range(4 * h, 4 * h + 4, 2):
                        act.activation(sq[:, k:k + 2, :], x[:, k:k + 2, :], ACT.Square).then_inc(core.sem_b.sem, 1)

            @block.tensor
            def _(pe):
                for k in range(DT):
                    pe.wait_ge(core.sem_b.sem, core.sem_b.at(k // 2 + 1))
                    pe.matmul(core.ps[:, 5, 0:TOK], core.m("ones"), sq[:, k, :], start=(k == 0), stop=(k == DT - 1))
        core.sem_a.close(2)
        core.sem_b.close(4)
        rstd_of(core, core.ps[:, 5, 0:TOK], rs[:, :], 1.0 / D, LN_EPS)
        with core.block() as block:
            @block.vector
            def _(dve):
                for k in range(DT):
                    dve.scalar_tensor_tensor(out=x[:, k, :], in0=x[:, k, :], scalar=core.v(g, layer * DT + k),
                                             in1=rs[:, :], op0=ALU.mult, op1=ALU.mult).then_inc(core.sem_a.sem, 1)

            @block.scalar
            def _(act):
                for k in range(DT):
                    act.wait_ge(core.sem_a.sem, core.sem_a.at(k + 1))
                    act.activation(x[:, k, :], x[:, k, :], ACT.Identity, bias=core.v(b, layer * DT + k))
        core.sem_a.close(DT)


def residual_tiles(core, scale):
    def take(m):
        return lambda eng, ps: eng.scalar_tensor_tensor(out=core.x[:, m, :], in0=core.x[:, m, :], scalar=scale, in1=ps,
                                                        op0=ALU.mult, op1=ALU.add)
    return [("dve", take(m), None) for m in range(DT)]


def copy_tiles(core, dst, eng="act", func=None, bias=None, scale=1.0):
    def take(m):
        if eng == "dve":
            return lambda e, ps: e.tensor_copy(dst(m), ps)
        if bias is None:
            return lambda e, ps: e.activation(dst(m), ps, func or ACT.Copy, scale=scale)
        return lambda e, ps: e.activation(dst(m), ps, func or ACT.Identity, bias=bias(m), scale=scale)
    return take


def ffn(core, layer):
    with ExitStack() as s:
        h = s.enter_context(core.nc.sbuf_tensor(f"ffn_h{layer}", [P, FF_T, TOK], F32))
        tiles = []
        for j in range(FF_T):
            def gate(e, ps, j=j):
                return e.activation(h[:, j, :], ps, ACT.Silu)

            def up(e, ps, j=j):
                e.wait_ge(core.act_evac.sem, core.act_evac.at(j + 1))
                return e.tensor_tensor(h[:, j, :], h[:, j, :], ps, ALU.mult)
            tiles += [("act", gate, None), ("dve", up, None)]
        linear(core, f"ffn_up{layer}", lambda k: core.x[:, k, :], tiles)
        linear(core, f"ffn_dn{layer}", lambda k: h[:, k, :], residual_tiles(core, ALPHA))
    layer_norm(core, "ln_ffn_g", "ln_ffn_b", layer)


def per_layer_embedding(core, layer):
    nc = core.nc
    with ExitStack() as s:
        gate = s.enter_context(nc.sbuf_tensor(f"ple_gate{layer}", [P, DT, TOK], F32))
        pt = s.enter_context(nc.sbuf_tensor(f"ple_p{layer}_sb", [P, 2, TOK], F32))
        take = copy_tiles(core, lambda m: gate[:, m, :], func=ACT.Sigmoid, bias=lambda m: core.v("b_ple", layer * DT + m))
        with core.block() as block:
            @block.scalar
            def _(act):
                act.dma_start(pt[:, :, :], core.a["p"][layer]).then_inc(core.const_loaded.sem, 16)
                act.wait_ge(core.const_loaded.sem, core.const_loaded.at(16))
        core.const_loaded.close(16)
        linear(core, f"ple_g{layer}", lambda k: core.x[:, k, :], [("act", take(m), None) for m in range(DT)])
        tiles = []
        for m in range(DT):
            def take(e, ps, m=m):
                return e.tensor_tensor(gate[:, m, :], gate[:, m, :], ps, ALU.mult)

            def after(e, link, wait_tile, m=m):
                wait_tile(e, m)
                link(e.tensor_tensor(core.x[:, m, :], core.x[:, m, :], gate[:, m, :], ALU.add))
            tiles.append(("dve", take, after))
        linear(core, f"ple_p{layer}", lambda k: pt[:, k, :], tiles)


def ssd_layer(core):
    nc, ps = core.nc, core.ps
    with ExitStack() as s:
        def sb(name, shape):
            return s.enter_context(nc.sbuf_tensor(name, shape, F32))
        y_sc = sb("y_sc", [P, DT, TOK])
        z = sb("z_gate", [P, DT, TOK])
        xbc = sb("xbc", [P, XBC_T, TOK])
        dt = sb("dt16", [16, TOK])
        acs = sb("acs16", [16, TOK])
        dte = sb("dte16", [16, SSD_CHUNK])
        with ExitStack() as s2:
            xbp = s2.enter_context(nc.sbuf_tensor("xbc_pad", [P, 2, TOK + 4], F32))
            scp = s2.enter_context(nc.sbuf_tensor("sc_pad", [P, DT, TOK + 4], F32))
            dtw = s2.enter_context(nc.sbuf_tensor("dt_w", [P, DT, 16], F32))
            acc = s2.enter_context(nc.sbuf_tensor("conv_acc", [P, TOK], F32))
            ab = s2.enter_context(nc.sbuf_tensor("dt_abs", [16, TOK], F32))
            with core.block() as block:
                @block.scalar
                def _(act):
                    act.dma_start(dtw[:, :, :], core.a["w_dt"]).then_inc(core.const_loaded.sem, 16)

                @block.vector
                def _(dve):
                    dve.memset(xbp[:, :, 0:4], 0.0)
                    dve.memset(scp[:, :, 0:4], 0.0)

                @block.tensor
                def _(pe):
                    pe.wait_ge(core.const_loaded.sem, core.const_loaded.at(16))
                    for k in range(DT):
                        pe.matmul(ps[0:16, 7, 0:TOK], dtw[:, k, :], core.x[:, k, :], start=(k == 0), stop=(k == DT - 1))
            core.const_loaded.close(16)

            tiles = []
            for t in range(XBC_T):
                def take(e, p_, t=t):
                    if t >= 2:
                        e.wait_ge(core.sem_c.sem, core.sem_c.at(t - 1))
                    return e.activation(xbp[:, t % 2, 4:4 + TOK], p_, ACT.Copy)
                tiles.append(("act", take, None))
            for t in range(DT):
                tiles.append(("act", copy_tiles(core, lambda m: scp[:, m, 4:4 + TOK])(t), None))
            for t in range(DT):
                def take(e, p_, t=t):
                    e.wait_ge(core.act_evac.sem, core.act_evac.at(XBC_T + t + 1))
                    return e.tensor_tensor(scp[:, t, 4:4 + TOK], scp[:, t, 4:4 + TOK], p_, ALU.mult)
                tiles.append(("dve", take, None))
            for t in range(DT):
                def take(e, p_, t=t):
                    return e.tensor_tensor(y_sc[:, t, :], y_sc[:, t, :], p_, ALU.mult)
                tiles.append(("dve", take, None))
            for t in range(DT):
                tiles.append(("act", copy_tiles(core, lambda m: z[:, m, :], func=ACT.Silu)(t), None))

            def conv(link, dve, dst, src, w, n, bias=None):
                if bias is None:
                    link(dve.tensor_scalar(dst, src[:, 4:4 + TOK], w(n - 1), None, ALU.mult))
                else:
                    link(dve.tensor_scalar(dst, src[:, 4:4 + TOK], w(n - 1), bias, ALU.mult, ALU.add))
                for i in range(n - 1):
                    lag = n - 1 - i
                    link(dve.scalar_tensor_tensor(out=dst, in0=src[:, 4 - lag:4 - lag + TOK], scalar=w(i), in1=dst,
                                                  op0=ALU.mult, op1=ALU.add))

            def conv_xbc(e, link, t):
                e.wait_ge(core.act_evac.sem, core.act_evac.at(t + 1))
                conv(link, e, xbc[:, t, :], xbp[:, t % 2, :], lambda i: core.v("conv_w", i * XBC_T + t), SSD_CONV,
                     core.v("conv_b", t))

            def conv_sc(e, link, wait_tile, t):
                wait_tile(e, XBC_T + DT + t)
                conv(link, e, y_sc[:, t, :], scp[:, t, :], lambda i: core.v("sc_w", i * DT + t), SC_CONV)
            for t in range(DT):
                i = XBC_T + DT + t
                e_, take_, _ = tiles[i]
                tiles[i] = (e_, take_, lambda e, link, wt, t=t: conv_sc(e, link, wt, t))

            def head(dve, link):
                for t in range(XBC_T):
                    conv_xbc(dve, link, t)
                    dve.sem_inc(core.sem_c.sem, 1)
            linear(core, "w_in", lambda k: core.x[:, k, :], tiles, head=head)
            core.sem_c.close(XBC_T)
            with core.block() as block:
                @block.scalar
                def _(act):
                    link = core.link("act", act)
                    link(act.activation(xbc[:, :, :], xbc[:, :, :], ACT.Silu))
                    link(act.activation(dt[:, :], ps[0:16, 7, 0:TOK], ACT.Identity, bias=core.v("dt_bias", 0, 16)))
                    link(act.activation(ab[:, :], dt[:, :], ACT.Abs))
                    link(act.activation(ab[:, :], ab[:, :], ACT.Exp, scale=-1.0))
                    link(act.activation(ab[:, :], ab[:, :], ACT.Ln, bias=1.0))
                    link(act.activation(acc[0:16, 0:1], core.v("a_log", 0, 16), ACT.Exp))
            with core.block() as block:
                @block.vector
                def _(dve):
                    link = core.link("dve", dve)
                    link(dve.scalar_tensor_tensor(out=dt[:, :], in0=dt[:, :], scalar=0.0, in1=ab[:, :], op0=ALU.max,
                                                  op1=ALU.add))
                    link(dve.tensor_scalar(ab[:, :], dt[:, :], acc[0:16, 0:1], -1.0, ALU.mult, ALU.mult))
                    for c in range(NB):
                        link(dve.tensor_tensor_scan(acs[:, c * P:c * P + P], core.m("ones")[0:16, :],
                                                    ab[:, c * P:c * P + P], 0.0, ALU.mult, ALU.add))
            with core.block() as block:
                @block.scalar
                def _(act):
                    act.activation(dte[:, :], acs[:, 0:P], ACT.Exp, scale=-1.0, bias=acs[:, P - 1:P])
        xdt = sb("xdt", [P, NB, SSD_HEADS, HD])
        xde = sb("xde", [P, SSD_HEADS, HD])
        cols = sb("ssd_cols", [P, 5, 16])
        btok = sb("btok", [P, SSD_GROUPS, P])
        cbm = sb("cbm", [P, SSD_GROUPS * NB, P])
        hst = sb("h_state", [P, SSD_GROUPS, HPG * HD])
        ident = core.m("ident")
        with core.block() as block:
            @block.tensor
            def _(pe):
                for n, src in enumerate([dt[:, 0:P], dt[:, P:2 * P], acs[:, 0:P], acs[:, P:2 * P], dte[:, :]]):
                    pe.transpose(ps[:, 6, 16 * n:16 * n + 16], src, ident[0:16, 0:16])
                for g in range(SSD_GROUPS):
                    pe.transpose(ps[:, 7, g * P:g * P + P], xbc[:, 8 + g, 0:P], ident)
                for c in range(NB):
                    for t in range(DT):
                        n = c * DT + t
                        pe.transpose(ps[:, n // 4, (n % 4) * P:(n % 4) * P + P], xbc[:, t, c * P:c * P + P], ident)
                for g in range(SSD_GROUPS):
                    for c in range(NB):
                        n = g * NB + c
                        pe.matmul(ps[:, 5, n * P:n * P + P], xbc[:, 8 + g, c * P:c * P + P],
                                  xbc[:, 10 + g, c * P:c * P + P], start=True, stop=True)
        with core.block() as block:
            @block.vector
            def _(dve):
                link = core.link("dve", dve)
                link(dve.tensor_copy(cols[:, :, :], ps[:, 6, 0:80].rearrange("p (a b) -> p a b", b=16)))
                for c in range(NB):
                    for q in range(2):
                        link(dve.tensor_tensor(xdt[:, c, 8 * q:8 * q + 8, :],
                                               ps[:, 2 * c + q, :].rearrange("p (h d) -> p h d", d=HD),
                                               bcast(cols[:, c, 8 * q:8 * q + 8].unsqueeze(2), [P, 8, HD]), ALU.mult))
                link(dve.tensor_tensor(xde[:, :, :], xdt[:, 0, :, :],
                                       bcast(cols[:, 4, :].unsqueeze(2), [P, SSD_HEADS, HD]), ALU.mult))
                link(dve.tensor_tensor(cbm[:, :, :], ps[:, 5, :].rearrange("p (a b) -> p a b", b=P),
                                       bcast(core.m("tri_le").unsqueeze(1), [P, 4, P]), ALU.mult))

            @block.scalar
            def _(act):
                act.activation(btok[:, :, :], ps[:, 7, 0:2 * P].rearrange("p (a b) -> p a b", b=P), ACT.Copy)
        with core.block() as block:
            @block.tensor
            def _(pe):
                for g in range(SSD_GROUPS):
                    pe.matmul(ps[:, g, :], btok[:, g, :], xde[:, g * HPG:g * HPG + HPG, :], start=True, stop=True)
        with core.block() as block:
            @block.vector
            def _(dve):
                dve.tensor_copy(hst[:, :, :], ps[:, 0:2, :])
        seg = sb("seg", [P, 2, TOK])
        ex = sb("seg_exp", [P, 2, TOK + P])
        wl = sb("w_local", [P, 2, TOK + P])
        bc_ready, seg_ready, exp_ready, w_ready, y_ready = core.sem_a, core.sem_b, core.sem_c, core.sem_d, core.sem_e
        y_taken, xd = core.sem_f, xbc
        with core.block() as block:
            @block.tensor
            def _(pe):
                def spread(h):
                    if h >= 2:
                        pe.wait_ge(seg_ready.sem, seg_ready.at(h - 1))
                        pe.wait_ge(exp_ready.sem, exp_ready.at(h - 1))
                    pe.matmul(ps[:, h % 2, 0:TOK], bcast(ident[0:16, h:h + 1], [16, P]), acs[:, :], start=True,
                              stop=True).then_inc(bc_ready.sem, 1)
                spread(0)
                for h in range(SSD_HEADS):
                    if h + 1 < SSD_HEADS:
                        spread(h + 1)
                    pe.wait_ge(w_ready.sem, w_ready.at(h + 1))
                    j, o = h // 2, HD * (h % 2)
                    if h % 2 == 0 and j >= 2:
                        pe.wait_ge(y_taken.sem, y_taken.at(j - 1))
                    out = ps[o:o + HD, 2 + j % 2, :]
                    w = wl[:, h % 2, :]
                    pe.matmul(out[:, 0:P], xdt[:, 0, h, :], w[:, 0:P], start=True, stop=True)
                    pe.matmul(out[:, P:TOK], xdt[:, 1, h, :], w[:, P:TOK], start=True, stop=False)
                    pe.matmul(out[:, P:TOK], hst[:, h // HPG, (h % HPG) * HD:(h % HPG) * HD + HD], w[:, TOK:TOK + P],
                              start=False, stop=True).then_inc(y_ready.sem, 1)

            @block.vector
            def _(dve):
                link = core.link("dve", dve)

                def y_out(j):
                    dve.wait_ge(y_ready.sem, y_ready.at(2 * j + 2))
                    link(dve.scalar_tensor_tensor(out=xd[:, j, :], in0=xd[:, j, :], scalar=core.v("ssd_d", j),
                                                  in1=ps[:, 2 + j % 2, 0:TOK], op0=ALU.mult, op1=ALU.add))
                    dve.sem_inc(y_taken.sem, 1)
                    link(dve.tensor_tensor(xd[:, j, :], xd[:, j, :], z[:, j, :], ALU.mult))
                for h in range(SSD_HEADS):
                    dve.wait_ge(bc_ready.sem, bc_ready.at(h + 1))
                    if h >= 2:
                        dve.wait_ge(exp_ready.sem, exp_ready.at(h - 1))
                    for c in range(NB):
                        ins = dve.tensor_scalar(seg[:, h % 2, c * P:c * P + P], ps[:, h % 2, c * P:c * P + P],
                                                cols[:, 2 + c, h:h + 1], 0.0, ALU.subtract, ALU.min)
                    ins.then_inc(seg_ready.sem, 1)
                    if h >= 3 and h % 2 == 1:
                        y_out((h - 3) // 2)
                y_out(SSD_HEADS // 2 - 1)

            @block.scalar
            def _(act):
                for h in range(SSD_HEADS):
                    act.wait_ge(seg_ready.sem, seg_ready.at(h + 1))
                    if h >= 2:
                        act.wait_ge(w_ready.sem, w_ready.at(h - 1))
                    act.activation(ex[:, h % 2, 0:TOK], seg[:, h % 2, :], ACT.Exp)
                    act.activation(ex[:, h % 2, TOK:TOK + P], ps[:, h % 2, P:TOK], ACT.Exp).then_inc(exp_ready.sem, 1)

            @block.gpsimd
            def _(pool):
                for h in range(SSD_HEADS):
                    g = h // HPG
                    pool.wait_ge(exp_ready.sem, exp_ready.at(h + 1))
                    if h >= 2:
                        pool.wait_ge(y_ready.sem, y_ready.at(h - 1))
                    pool.tensor_tensor(wl[:, h % 2, 0:TOK], ex[:, h % 2, 0:TOK],
                                       cbm[:, g * NB:g * NB + NB, :].rearrange("p a b -> p (a b)"), ALU.mult)
                    pool.tensor_tensor(wl[:, h % 2, TOK:TOK + P], ex[:, h % 2, TOK:TOK + P],
                                       xbc[:, 10 + g, P:TOK], ALU.mult).then_inc(w_ready.sem, 1)
        for sig in (bc_ready, seg_ready, exp_ready, w_ready, y_ready):
            sig.close(SSD_HEADS)
        y_taken.close(SSD_HEADS // 2)
        with core.block() as block:
            @block.scalar
            def _(act):
                act.activation(z[:, :, :], xd[:, 0:DT, :], ACT.Square)
        column_sums(core, [(ps[:, 4 + g, 0:TOK], core.m("ones"), [z[:, 4 * g + k, :] for k in range(4)])
                           for g in range(SSD_GROUPS)])
        rstd = seg[:, :, :]
        rstd_of(core, ps[:, 4:6, 0:TOK], rstd, 1.0 / (SSD_HEADS * HD // SSD_GROUPS), 1e-5)
        with core.block() as block:
            @block.vector
            def _(dve):
                for t in range(DT):
                    dve.scalar_tensor_tensor(out=xd[:, t, :], in0=xd[:, t, :], scalar=core.v("ssd_norm", t),
                                             in1=rstd[:, t // 4, :], op0=ALU.mult, op1=ALU.mult)
        linear(core, "w_out", lambda k: xd[:, k, :] if k < DT else y_sc[:, k - DT, :], residual_tiles(core, ALPHA))
    layer_norm(core, "ln_mix_g", "ln_mix_b", 0)


def to_token_major(core, srcs, dst):
    ps, ident = core.ps, core.m("ident")
    jobs = [(t, b) for t in range(len(srcs)) for b in range(NB)]
    for first in range(0, len(jobs), 16):
        part = jobs[first:first + 16]
        with core.block() as block:
            @block.tensor
            def _(pe):
                for n, (t, b) in enumerate(part):
                    pe.transpose(ps[:, n // 4, (n % 4) * P:(n % 4) * P + P], srcs[t][:, b * P:b * P + P],
                                 ident).then_inc(core.sem_a.sem, 1)

            @block.scalar
            def _(act):
                for n, (t, b) in enumerate(part):
                    if n // 4 % 2 == 0:
                        act.wait_ge(core.sem_a.sem, core.sem_a.at(min(len(part), n // 4 * 4 + 4)))
                        act.activation(dst(t, b), ps[:, n // 4, (n % 4) * P:(n % 4) * P + P], ACT.Copy)

            @block.vector
            def _(dve):
                for n, (t, b) in enumerate(part):
                    if n // 4 % 2 == 1:
                        dve.wait_ge(core.sem_a.sem, core.sem_a.at(min(len(part), n // 4 * 4 + 4)))
                        dve.tensor_copy(dst(t, b), ps[:, n // 4, (n % 4) * P:(n % 4) * P + P])
        core.sem_a.close(len(part))


def softmax_attention(core, name, heads, q, k, v, mask, scale, take, sinks=None):
    nc, ps, ident = core.nc, core.ps, core.m("ident")
    scored, shifted, exped, normed, turned, copied, summed = (
        core.sem_a, core.sem_b, core.sem_c, core.sem_d, core.sem_e, core.sem_f, core.sem_g)
    H, W = len(heads), 3 * P
    with ExitStack() as s:
        prob = s.enter_context(nc.sbuf_tensor(f"{name}_prob", [P, 2, W], F32))
        pt = s.enter_context(nc.sbuf_tensor(f"{name}_pt", [P, 2, W], F32))
        st = s.enter_context(nc.sbuf_tensor(f"{name}_st", [P, 2, 8], F32))
        spans = [(0, P), (P, W)]

        with core.block() as block:
            @block.tensor
            def _(pe):
                def scores(i):
                    if i >= 2:
                        pe.wait_ge(shifted.sem, shifted.at(i - 1))
                    h = heads[i]
                    pe.matmul(ps[:, i % 2, 0:P], q(h)[:, 0:P], k(h)[:, 0:P], start=True, stop=True)
                    pe.matmul(ps[:, i % 2, P:W], q(h)[:, P:TOK], k(h), start=True, stop=True).then_inc(scored.sem, 1)

                def turn(i):
                    pe.wait_ge(normed.sem, normed.at(i + 1))
                    if i >= 2:
                        pe.wait_ge(copied.sem, copied.at(i - 1))
                    for n in range(3):
                        t = pe.transpose(ps[:, 2 + i % 2, n * P:n * P + P], prob[:, i % 2, n * P:n * P + P], ident)
                    t.then_inc(turned.sem, 1)

                def weigh(i):
                    pe.wait_ge(copied.sem, copied.at(i + 1))
                    if i % 2 == 0 and i >= 4:
                        pe.wait_ge(core.dve_evac.sem, core.dve_evac.at(i // 2 - 1))
                    o = HD * (i % 2)
                    out = ps[o:o + HD, 4 + i // 2 % 2, :]
                    p = pt[:, i % 2, :]
                    pe.matmul(out[:, 0:P], v(heads[i], 0), p[:, 0:P], start=True, stop=True)
                    pe.matmul(out[:, P:TOK], v(heads[i], 0), p[:, P:2 * P], start=True, stop=False)
                    pe.matmul(out[:, P:TOK], v(heads[i], 1), p[:, 2 * P:W], start=False, stop=True).then_inc(summed.sem, 1)
                for i in range(H + 2):
                    if i < H:
                        scores(i)
                    if 1 <= i <= H:
                        turn(i - 1)
                    if i >= 2:
                        weigh(i - 2)

            @block.vector
            def _(dve):
                link = core.link("dve", dve)

                def shift(i):
                    pr, t = prob[:, i % 2, :], st[:, i % 2, :]
                    dve.wait_ge(scored.sem, scored.at(i + 1))
                    if i >= 2:
                        dve.wait_ge(turned.sem, turned.at(i - 1))
                    link(dve.scalar_tensor_tensor(out=pr, in0=ps[:, i % 2, 0:W], scalar=scale, in1=core.m(mask, 0, W),
                                                  op0=ALU.mult, op1=ALU.add))
                    for b, (lo, hi) in enumerate(spans):
                        link(dve.tensor_reduce(t[:, b:b + 1], pr[:, lo:hi], AX, ALU.max))
                    if sinks is None:
                        ins = dve.tensor_scalar(t[:, 2:4], t[:, 0:2], -1.0, None, ALU.mult)
                    else:
                        ins = dve.tensor_scalar(t[:, 2:4], t[:, 0:2], sinks(heads[i]), -1.0, ALU.max, ALU.mult)
                    ins.then_inc(shifted.sem, 1)

                def normalise(i):
                    pr, t = prob[:, i % 2, :], st[:, i % 2, :]
                    dve.wait_ge(exped.sem, exped.at(i + 1))
                    if sinks is not None:
                        link(dve.tensor_tensor(t[:, 4:6], t[:, 4:6], t[:, 6:8], ALU.add))
                    link(dve.reciprocal(t[:, 4:6], t[:, 4:6]))
                    for b, (lo, hi) in enumerate(spans):
                        ins = dve.tensor_scalar(pr[:, lo:hi], pr[:, lo:hi], t[:, 4 + b:5 + b], None, ALU.mult)
                    ins.then_inc(normed.sem, 1)

                def store(j):
                    dve.wait_ge(summed.sem, summed.at(2 * j + 2))
                    take(dve, j, ps[:, 4 + j % 2, 0:TOK]).then_inc(core.dve_evac.sem, 1)
                for i in range(H + 3):
                    if i < H:
                        shift(i)
                    if 1 <= i <= H:
                        normalise(i - 1)
                    if i >= 4 and i % 2 == 0:
                        store((i - 4) // 2)

            @block.scalar
            def _(act):
                def exponentials(i):
                    pr, t = prob[:, i % 2, :], st[:, i % 2, :]
                    act.wait_ge(shifted.sem, shifted.at(i + 1))
                    for b, (lo, hi) in enumerate(spans):
                        ins = act.activation(pr[:, lo:hi], pr[:, lo:hi], ACT.Exp, bias=t[:, 2 + b:3 + b],
                                             accum_out=t[:, 4 + b:5 + b])
                    if sinks is not None:
                        ins = act.activation(t[:, 6:8], t[:, 2:4], ACT.Exp, bias=sinks(heads[i]))
                    ins.then_inc(exped.sem, 1)

                def copy(i):
                    act.wait_ge(turned.sem, turned.at(i + 1))
                    if i >= 2:
                        act.wait_ge(summed.sem, summed.at(i - 1))
                    act.activation(pt[:, i % 2, :], ps[:, 2 + i % 2, 0:W], ACT.Copy).then_inc(copied.sem, 1)
                for i in range(H + 1):
                    if i < H:
                        exponentials(i)
                    if i >= 1:
                        copy(i - 1)
        for sig in (scored, shifted, exped, normed, turned, copied, summed):
            sig.close(H)
        core.dve_evac.close(H // 2)


def attention_layer(core):
    nc = core.nc
    with ExitStack() as s:
        qkv = s.enter_context(nc.sbuf_tensor("swa_qkv", [P, 12, TOK], F32))
        vt = s.enter_context(nc.sbuf_tensor("swa_v", [P, NB, 2 * P], F32))
        o = s.enter_context(nc.sbuf_tensor("swa_o", [P, DT, TOK], F32))
        take = copy_tiles(core, lambda m: qkv[:, m, :], bias=lambda m: core.v("b_qkv", m))
        linear(core, "qkv", lambda k: core.x[:, k, :], [("act", take(m), None) for m in range(12)])
        to_token_major(core, [qkv[:, 10 + t, :] for t in range(2)], lambda t, b: vt[:, b, t * P:t * P + P])

        def kv_of(u):
            return 2 * (u // 2 // 4) + u % 2

        def half(u):
            return slice(HD * (u % 2), HD * (u % 2) + HD)

        def sink(u):
            return core.v("sinks", 8 * (u // 8) + 4 * (u % 2) + u // 2 % 4)
        softmax_attention(core, "swa", range(16), lambda u: qkv[half(u), u // 2, :],
                          lambda u: qkv[half(u), 8 + u // 8, :],
                          lambda u, b: vt[:, b, HD * kv_of(u):HD * kv_of(u) + HD], "band", HD ** -0.5,
                          lambda e, j, p: e.tensor_copy(o[:, j, :], p), sink)
        tiles = []
        for m in range(DT):
            def take(e, p, m=m):
                return e.scalar_tensor_tensor(out=o2[:, m, :], in0=core.x[:, m, :], scalar=ALPHA, in1=p, op0=ALU.mult, op1=ALU.add)

            def after(e, link, wait_tile, m=m):
                wait_tile(e, m)
                link(e.tensor_scalar(core.x[:, m, :], o2[:, m, :], core.v("b_o", m), None, ALU.add))
            tiles.append(("dve", take, after))
        o2 = qkv
        linear(core, "w_o", lambda k: o[:, k, :], tiles)
    layer_norm(core, "ln_mix_g", "ln_mix_b", 1)


def modulation(core, name, cond, out, bias):
    mine = [i for i in range(core.used, len(core.stream)) if core.stream[i][0] == name]
    ps = core.ps
    with core.block() as block:
        @block.sync
        def _(sp):
            issue_panels(core, sp, mine[-1] + 1 + RING)

        @block.tensor
        def _(pe):
            for i in mine:
                j, slot = core.stream[i][1], i % RING
                pe.wait_ge(core.panel_loaded[slot].sem, core.panel_loaded[slot].at(16 * (i // RING + 1)))
                for c in range(2):
                    for k in range(DT):
                        mm = pe.matmul(ps[:, 7, 2 * j + c:2 * j + c + 1],
                                       core.ring[:, slot, k * PANEL + c * P:k * PANEL + c * P + P],
                                       cond[:, k:k + 1], start=(k == 0), stop=(k == DT - 1))
                mm.then_inc(core.panel_used.sem, 1)
    n = 2 * len(mine)
    with core.block() as block:
        @block.vector
        def _(dve):
            dve.tensor_tensor(out, ps[:, 7, 0:n], bias, ALU.add)
    core.used = mine[-1] + 1


def rms_modulate(core, name, out, g, scale, shift):
    x = core.x
    with ExitStack() as s:
        rs = s.enter_context(core.nc.sbuf_tensor(f"{name}_rs", [P, TOK], F32))
        gs = s.enter_context(core.nc.sbuf_tensor(f"{name}_gs", [P, DT], F32))
        with core.block() as block:
            @block.scalar
            def _(act):
                for k in range(DT):
                    act.activation(out[:, k, :], x[:, k, :], ACT.Square).then_inc(core.sem_a.sem, 1)

            @block.tensor
            def _(pe):
                for k in range(DT):
                    pe.wait_ge(core.sem_a.sem, core.sem_a.at(k + 1))
                    pe.matmul(core.ps[:, 4, 0:TOK], core.m("ones"), out[:, k, :], start=(k == 0), stop=(k == DT - 1))

            @block.vector
            def _(dve):
                dve.scalar_tensor_tensor(out=gs[:, :], in0=scale, scalar=1.0, in1=g, op0=ALU.add, op1=ALU.mult)
        core.sem_a.close(DT)
        rstd_of(core, core.ps[:, 4, 0:TOK], rs[:, :], 1.0 / D, RMS_EPS)
        with core.block() as block:
            @block.vector
            def _(dve):
                for k in range(DT):
                    dve.scalar_tensor_tensor(out=out[:, k, :], in0=x[:, k, :], scalar=gs[:, k:k + 1], in1=rs[:, :],
                                             op0=ALU.mult, op1=ALU.mult).then_inc(core.sem_a.sem, 1)

            @block.scalar
            def _(act):
                for k in range(DT):
                    act.wait_ge(core.sem_a.sem, core.sem_a.at(k + 1))
                    act.activation(out[:, k, :], out[:, k, :], ACT.Identity, bias=shift[:, k:k + 1])
        core.sem_a.close(DT)


def head_sums(core, bank, src, tiles):
    column_sums(core, [(core.ps[:, bank + t // 2, (t % 2) * TOK:(t % 2) * TOK + TOK], core.m("head_ones"), [src[:, t, :]])
                       for t in range(tiles)])
    return core.ps[:, bank:bank + (tiles + 1) // 2, :].rearrange("p a (b n) -> p (a b) n", n=TOK)


def stick_breaking(core, q, k, v, o):
    nc, ps = core.nc, core.ps
    H, W = 8, 3 * P
    scale = HD ** -0.5
    with ExitStack() as s:
        def sb(name, shape):
            return s.enter_context(nc.sbuf_tensor("stick_" + name, shape, F32))
        sq, vt = sb("sq", [P, 8, TOK]), sb("vt", [P, NB, 4 * P])
        for half, (t, g) in enumerate(((q, "q_norm"), (k, "k_norm"))):
            part = sq[:, 4 * half:4 * half + 4, :]
            with core.block() as block:
                @block.scalar
                def _(act):
                    act.activation(part, t, ACT.Square)
            sums = head_sums(core, 2 * half, part, 4)
            rstd_of(core, sums, part, 1.0 / HD, RMS_EPS)
            with core.block() as block:
                @block.vector
                def _(dve):
                    dve.scalar_tensor_tensor(out=t, in0=t, scalar=core.v(g), in1=part, op0=ALU.mult, op1=ALU.mult)
        to_token_major(core, [v[:, t, :] for t in range(4)], lambda t, b: vt[:, b, t * P:t * P + P])
        lg, ln, lk = sb("logit", [P, H, W]), sb("log", [P, H, W]), sb("keep", [P, H, W])
        mask = sb("mask", [P, W])
        scored, logged, kept, masked, between, weight, exped, final = (
            core.sem_a, core.sem_b, core.sem_c, core.sem_d, core.sem_e, core.sem_f, core.sem_g, core.sem_h)
        done, scaled = core.act_evac, core.chain["pe"]
        with core.block() as block:
            @block.vector
            def _(dve):
                dve.tensor_copy(mask[:, 0:P], core.m("tri_lt"))
                dve.tensor_copy(mask[:, P:2 * P], core.m("ones"))
                dve.tensor_copy(mask[:, 2 * P:W], core.m("tri_lt"))
        with core.block() as block:
            def rows_of(h):
                return slice(HD * (h % 2), HD * (h % 2) + HD)

            @block.tensor
            def _(pe):
                def score(h):
                    if h >= 2:
                        pe.wait_ge(scaled.sem, scaled.at(h - 1))
                    r, t = rows_of(h), h // 2
                    pe.matmul(ps[:, h % 2, 0:TOK], k[r, t, 0:P], q[r, t, :], start=True, stop=True)
                    pe.matmul(ps[:, h % 2, TOK:W], k[r, t, P:TOK], q[r, t, P:TOK], start=True,
                              stop=True).then_inc(scored.sem, 1)

                def suffix(h):
                    pe.wait_ge(masked.sem, masked.at(h + 1))
                    if h >= 2:
                        pe.wait_ge(weight.sem, weight.at(h - 1))
                    out = ps[:, 2 + h % 2, :]
                    pe.matmul(out[:, 0:TOK], core.m("tri_gt"), lk[:, h, 0:TOK], start=True, stop=False)
                    pe.matmul(out[:, P:TOK], core.m("ones"), lk[:, h, TOK:W], start=False, stop=True)
                    pe.matmul(out[:, TOK:W], core.m("tri_gt"), lk[:, h, TOK:W], start=True, stop=True).then_inc(between.sem, 1)

                def weigh(h):
                    pe.wait_ge(final.sem, final.at(h + 1))
                    if h % 2 == 0 and h >= 4:
                        pe.wait_ge(core.dve_evac.sem, core.dve_evac.at(h // 2 - 1))
                    out = ps[HD * (h % 2):HD * (h % 2) + HD, 4 + h // 2 % 2, :]
                    pe.matmul(out[:, 0:TOK], vt[:, 0, HD * h:HD * h + HD], ln[:, h, 0:TOK], start=True, stop=False)
                    pe.matmul(out[:, P:TOK], vt[:, 1, HD * h:HD * h + HD], ln[:, h, TOK:W], start=False,
                              stop=True).then_inc(done.sem, 1)
                for i in range(H + 4):
                    if i < H:
                        score(i)
                    if 2 <= i < H + 2:
                        suffix(i - 2)
                    if i >= 4:
                        weigh(i - 4)

            @block.scalar
            def _(act):
                link = core.link("act", act)

                def logs(h):
                    act.wait_ge(scaled.sem, scaled.at(h + 1))
                    act.activation(ln[:, h, :], lg[:, h, :], ACT.Abs).then_inc(logged.sem, 1)
                    act.wait_ge(logged.sem, logged.at(h + 1))
                    link(act.activation(ln[:, h, :], ln[:, h, :], ACT.Exp, scale=-1.0))
                    act.activation(ln[:, h, :], ln[:, h, :], ACT.Ln, bias=1.0).then_inc(kept.sem, 1)

                def exponential(h):
                    act.wait_ge(weight.sem, weight.at(h + 1))
                    act.activation(ln[:, h, :], ln[:, h, :], ACT.Exp).then_inc(exped.sem, 1)
                for i in range(H + 3):
                    if i < H:
                        logs(i)
                    if i >= 3:
                        exponential(i - 3)

            @block.vector
            def _(dve):
                link = core.link("dve", dve)

                def logit(h):
                    dve.wait_ge(scored.sem, scored.at(h + 1))
                    dve.tensor_scalar(lg[:, h, :], ps[:, h % 2, 0:W], scale, None, ALU.mult).then_inc(scaled.sem, 1)
                    dve.wait_ge(scaled.sem, scaled.at(h + 1))
                    dve.wait_ge(kept.sem, kept.at(h + 1))
                    link(dve.scalar_tensor_tensor(out=ln[:, h, :], in0=lg[:, h, :], scalar=0.0, in1=ln[:, h, :],
                                                  op0=ALU.min, op1=ALU.subtract))
                    link(dve.tensor_tensor(lk[:, h, :], ln[:, h, :], lg[:, h, :], ALU.subtract))
                    dve.tensor_tensor(lk[:, h, :], lk[:, h, :], mask[:, :], ALU.mult).then_inc(masked.sem, 1)

                def exponent(h):
                    dve.wait_ge(between.sem, between.at(h + 1))
                    dve.tensor_tensor(ln[:, h, :], ln[:, h, :], ps[:, 2 + h % 2, 0:W], ALU.add).then_inc(weight.sem, 1)

                def store(j):
                    dve.wait_ge(done.sem, done.at(2 * j + 2))
                    dve.tensor_copy(o[:, j, :], ps[:, 4 + j % 2, 0:TOK]).then_inc(core.dve_evac.sem, 1)
                for i in range(H + 6):
                    if i < H:
                        logit(i)
                    if 2 <= i < H + 2:
                        exponent(i - 2)
                    if i >= 6 and i % 2 == 0:
                        store((i - 6) // 2)

            @block.gpsimd
            def _(pool):
                for h in range(H):
                    pool.wait_ge(exped.sem, exped.at(h + 1))
                    pool.tensor_tensor(ln[:, h, :], ln[:, h, :], mask[:, :], ALU.mult).then_inc(final.sem, 1)
        for sig in (scored, logged, kept, masked, between, weight, exped, final, done, scaled):
            sig.close(H)
        core.dve_evac.close(H // 2)
        part = sq[:, 0:4, :]
        with core.block() as block:
            @block.scalar
            def _(act):
                act.activation(part, o, ACT.Square)
        sums = head_sums(core, 0, part, 4)
        rstd_of(core, sums, part, 1.0 / HD, RMS_EPS)
        with core.block() as block:
            @block.vector
            def _(dve):
                for t in range(4):
                    dve.scalar_tensor_tensor(out=o[:, t, :], in0=o[:, t, :], scalar=core.v("sb_out", t),
                                             in1=part[:, t, :], op0=ALU.mult, op1=ALU.mult)


def rwkv_mix(core, z, lora, y):
    nc, ps = core.nc, core.ps
    T4, NC = 4, TOK // CHUNK
    with ExitStack() as s:
        def sb(name, shape):
            return s.enter_context(nc.sbuf_tensor("rwkv_" + name, shape, F32))
        r, k, v = z[:, 0:4, 1:], z[:, 4:8, 1:], z[:, 8:12, 1:]
        a, gate, bonus = (sb(n, [P, T4, TOK]) for n in ("a", "g", "bonus"))
        qq = sb("qq", [P, T4, 2, TOK])
        cm, fac = sb("mid", [P, T4, NC]), sb("fac", [P, T4, NC])
        vt, kt, btt = (sb(n, [P, NB, 4 * P]) for n in ("vt", "kt", "btt"))
        H = 8
        NP_ = H * NB
        mm_ = sb("mm", [P, NP_, 2, 2, P])
        early = s.enter_context(ExitStack())
        kk, lw, bt, en = (early.enter_context(nc.sbuf_tensor("rwkv_" + n, [P, T4, TOK], F32)) for n in ("kk", "lw", "b", "en"))
        with core.block() as block:
            @block.scalar
            def _(act):
                act.activation(z[0:HD, 12, 1:], z[0:HD, 12, 1:], ACT.Tanh)
                act.activation(z[:, 13, 1:], z[:, 13, 1:], ACT.Sigmoid)
        with core.block() as block:
            @block.tensor
            def _(pe):
                for t in range(T4):
                    c = slice((t % 2) * TOK, (t % 2) * TOK + TOK)
                    w = slice(t * P, t * P + P)
                    pe.matmul(ps[:, t // 2, c], lora[0:HD, w], z[0:HD, 12, 1:], start=True, stop=True)
                    pe.matmul(ps[:, 2 + t // 2, c], lora[HD:P, w], z[HD:P, 12, 1:], start=True, stop=True)
                    pe.matmul(ps[:, 4 + t // 2, c], lora[:, 512 + t * P:512 + t * P + P], z[:, 13, 1:], start=True,
                              stop=True)

            @block.vector
            def _(dve):
                link = core.link("dve", dve)
                for t in range(T4):
                    link(dve.tensor_scalar(kk[:, t, :], k[:, t, :], core.v("k_k", t), None, ALU.mult))
                link(dve.tensor_tensor(en[:, :, :], kk[:, :, :], kk[:, :, :], ALU.mult))
        with core.block() as block:
            @block.scalar
            def _(act):
                for t in range(T4):
                    c = slice((t % 2) * TOK, (t % 2) * TOK + TOK)
                    act.activation(lw[:, t, :], ps[:, t // 2, c], ACT.Sigmoid, bias=core.v("decay_w0", t))
                    act.activation(a[:, t, :], ps[:, 2 + t // 2, c], ACT.Sigmoid, bias=core.v("iclr_a0", t))
                    act.activation(gate[:, t, :], ps[:, 4 + t // 2, c], ACT.Copy)
        sums = head_sums(core, 6, en, T4)
        with core.block() as block:
            @block.scalar
            def _(act):
                act.activation(en[:, :, :], sums, ACT.Sqrt)

            @block.vector
            def _(dve):
                link = core.link("dve", dve)
                link(dve.tensor_scalar(lw[:, :, :], lw[:, :, :], -float(np.exp(-0.5)), None, ALU.mult))
                for t in range(T4):
                    link(dve.tensor_tensor_scan(bt[:, t, :], core.m("scan_keep", 0, TOK), lw[:, t, :], 0.0, ALU.mult, ALU.add))
                mid = bt[:, :, :].rearrange("p t (c n) -> p t c n", n=CHUNK)
                link(dve.tensor_copy(cm[:, :, :], mid[:, :, :, CHUNK // 2 - 1]))
                for t in range(T4):
                    link(dve.tensor_tensor(mid[:, t], mid[:, t], bcast(cm[:, t, :].unsqueeze(2), [P, NC, CHUNK]), ALU.subtract))
                link(dve.tensor_copy(fac[:, :, :], mid[:, :, :, CHUNK - 1]))
                link(dve.tensor_tensor(fac[:, :, 0:NC - 1], fac[:, :, 0:NC - 1], cm[:, :, 1:NC], ALU.add))
                link(dve.tensor_tensor(lw[:, :, :], bt[:, :, :], lw[:, :, :], ALU.subtract))
        with core.block() as block:
            @block.vector
            def _(dve):
                link = core.link("dve", dve)
                link(dve.tensor_scalar(en[:, :, :], en[:, :, :], 1e-12, None, ALU.max))
                link(dve.reciprocal(en[:, :, :], en[:, :, :]))
                link(dve.tensor_tensor(kk[:, :, :], kk[:, :, :], en[:, :, :], ALU.mult))
                for t in range(T4):
                    link(dve.tensor_scalar(en[:, t, :], a[:, t, :], 1.0, core.v("k_a", t), ALU.subtract, ALU.mult))
                    link(dve.scalar_tensor_tensor(out=k[:, t, :], in0=en[:, t, :], scalar=1.0, in1=k[:, t, :],
                                                  op0=ALU.add, op1=ALU.mult))
                    link(dve.scalar_tensor_tensor(out=bonus[:, t, :], in0=r[:, t, :], scalar=core.v("r_k", t),
                                                  in1=k[:, t, :], op0=ALU.mult, op1=ALU.mult))

            @block.scalar
            def _(act):
                act.activation(qq[:, :, 0, :], lw[:, :, :], ACT.Exp)
                act.activation(qq[:, :, 1, :], bt[:, :, :], ACT.Exp)
                act.activation(fac[:, :, :], fac[:, :, :], ACT.Exp)
        sums = head_sums(core, 6, bonus, T4)
        with core.block() as block:
            @block.scalar
            def _(act):
                act.activation(en[:, :, :], bt[:, :, :], ACT.Exp, scale=-1.0).then_inc(core.sem_a.sem, 1)

            @block.vector
            def _(dve):
                link = core.link("dve", dve)
                link(dve.tensor_tensor(bonus[:, :, :], v, sums, ALU.mult))
                link(dve.tensor_tensor(qq[:, :, 0, :], qq[:, :, 0, :], kk[:, :, :], ALU.mult))
                link(dve.tensor_tensor(qq[:, :, 1, :], qq[:, :, 1, :], r, ALU.mult))
                dve.wait_ge(core.sem_a.sem, core.sem_a.at(1))
                link(dve.tensor_tensor(bt[:, :, :], kk[:, :, :], a[:, :, :], ALU.mult))
                link(dve.tensor_tensor(bt[:, :, :], bt[:, :, :], en[:, :, :], ALU.mult))
                link(dve.tensor_tensor(k, k, en[:, :, :], ALU.mult))
        core.sem_a.close(1)
        for src, dst in ((v, vt), (k, kt), (bt, btt)):
            to_token_major(core, [src[:, t, :] for t in range(T4)], lambda t, b: dst[:, b, t * P:t * P + P])
        with core.block() as block:
            @block.tensor
            def _(pe):
                for n in range(NP_):
                    h, b = n // NB, n % NB
                    rr = slice(HD * (h % 2), HD * (h % 2) + HD)
                    if n >= 4:
                        pe.wait_ge(core.dve_evac.sem, core.dve_evac.at(n - 3))
                    for i, src in enumerate((k, bt)):
                        x = pe.matmul(ps[:, n % 4, i * TOK:i * TOK + TOK], src[rr, h // 2, b * P:b * P + P],
                                      qq[rr, h // 2, :, b * P:b * P + P], start=True, stop=True)
                    x.then_inc(core.sem_a.sem, 1)

            @block.vector
            def _(dve):
                both = core.m("lt64", 0, 2 * P)
                for n in range(NP_):
                    dve.wait_ge(core.sem_a.sem, core.sem_a.at(n + 1))
                    dve.tensor_tensor(mm_[:, n].rearrange("p i j t -> p i (j t)"),
                                      ps[:, n % 4, :].rearrange("p (i t) -> p i t", i=2),
                                      bcast(both.unsqueeze(1), [P, 2, 2 * P]), ALU.mult).then_inc(core.dve_evac.sem, 1)
        core.sem_a.close(NP_)
        core.dve_evac.close(NP_)
        early.close()
        tt, tn, xx, nl = (sb(n, [P, NP_, P]) for n in ("tt", "tn", "xx", "nl"))
        ident = core.m("ident")
        with core.block() as block:
            @block.vector
            def _(dve):
                for g in range(4):
                    gs = slice(4 * g, 4 * g + 4)
                    dve.tensor_copy(tt[:, gs, :], bcast(ident.unsqueeze(1), [P, 4, P]))
                    dve.tensor_copy(tn[:, gs, :], bcast(ident.unsqueeze(1), [P, 4, P]))
        for lev in range(6):
            last = lev == 5
            with core.block() as block:
                @block.gpsimd
                def _(pool):
                    for g in range(4):
                        gs = slice(4 * g, 4 * g + 4)
                        pool.tensor_tensor(nl[:, gs, :], mm_[:, gs, 1, 0, :],
                                           bcast(core.m("level", lev, P).unsqueeze(1), [P, 4, P]),
                                           ALU.mult).then_inc(core.sem_a.sem, 1)

                @block.tensor
                def _(pe):
                    for g in range(5):
                        if g < 4:
                            pe.wait_ge(core.sem_a.sem, core.sem_a.at(g + 1))
                            for i in range(4):
                                n = 4 * g + i
                                x = pe.matmul(ps[:, g, i * P:i * P + P], nl[:, n, :], tn[:, n, :], start=True, stop=True)
                            x.then_inc(core.sem_b.sem, 1)
                        if g >= 1:
                            g1 = g - 1
                            pe.wait_ge(core.sem_c.sem, core.sem_c.at(g1 + 1))
                            if g1 >= 2:
                                pe.wait_ge(core.sem_e.sem, core.sem_e.at(g1 - 1))
                            for i in range(4):
                                n = 4 * g1 + i
                                if not last:
                                    pe.matmul(ps[:, 4 + 2 * (g1 % 2), i * P:i * P + P], tt[:, n, :], xx[:, n, :],
                                              start=True, stop=True)
                                x = pe.matmul(ps[:, 5 + 2 * (g1 % 2), i * P:i * P + P], xx[:, n, :], tt[:, n, :],
                                              start=True, stop=True)
                            x.then_inc(core.sem_d.sem, 1)

                @block.scalar
                def _(act):
                    for g in range(4):
                        act.wait_ge(core.sem_b.sem, core.sem_b.at(g + 1))
                        act.activation(xx[:, 4 * g:4 * g + 4, :], ps[:, g, :].rearrange("p (i t) -> p i t", t=P),
                                       ACT.Copy).then_inc(core.sem_c.sem, 1)

                @block.vector
                def _(dve):
                    for g in range(4):
                        gs = slice(4 * g, 4 * g + 4)
                        dve.wait_ge(core.sem_d.sem, core.sem_d.at(g + 1))
                        if not last:
                            dve.tensor_tensor(tn[:, gs, :], tn[:, gs, :],
                                              ps[:, 4 + 2 * (g % 2), :].rearrange("p (i t) -> p i t", t=P), ALU.subtract)
                        dve.tensor_tensor(tt[:, gs, :], tt[:, gs, :],
                                          ps[:, 5 + 2 * (g % 2), :].rearrange("p (i t) -> p i t", t=P),
                                          ALU.subtract).then_inc(core.sem_e.sem, 1)
            for sig in (core.sem_a, core.sem_b, core.sem_c, core.sem_d, core.sem_e):
                sig.close(4)
        st = sb("state", [P, NC, T4, HD])
        rs, un = sb("rhs", [P, NB, 2, T4, HD]), sb("neg_u", [P, NB, 2, T4, HD])
        for c in range(NC):
            b, off = c // 2, HD * (c % 2)
            po = slice(off, off + HD)
            with core.block() as block:
                @block.tensor
                def _(pe):
                    for par in range(2):
                        rr = slice(HD * par, HD * par + HD)
                        for t in range(T4):
                            h = 2 * t + par
                            n = h * NB + b
                            out = ps[po, par, t * HD:t * HD + HD]
                            x = pe.matmul(out, mm_[:, n, 0, 0, po], vt[:, b, h * HD:h * HD + HD], start=True, stop=(c == 0))
                            if c > 0:
                                x = pe.matmul(out, qq[rr, t, 0, c * CHUNK:c * CHUNK + CHUNK], st[rr, c, t, :], start=False,
                                              stop=True)
                        x.then_inc(core.sem_a.sem, 1)
                    for par in range(2):
                        pe.wait_ge(core.sem_b.sem, core.sem_b.at(par + 1))
                        for t in range(T4):
                            h = 2 * t + par
                            x = pe.matmul(ps[po, 2 + par, t * HD:t * HD + HD], tt[po, h * NB + b, po], rs[po, b, par, t, :],
                                          start=True, stop=True)
                        x.then_inc(core.sem_c.sem, 1)
                    if c < NC - 1:
                        for par in range(2):
                            pe.wait_ge(core.sem_d.sem, core.sem_d.at(par + 1))
                            for t in range(T4):
                                h = 2 * t + par
                                hs = slice(h * HD, h * HD + HD)
                                out = ps[HD * par:HD * par + HD, 4, t * HD:t * HD + HD]
                                pe.matmul(out, kt[po, b, hs], vt[po, b, hs], start=True, stop=False)
                                x = pe.matmul(out, btt[po, b, hs], un[po, b, par, t, :], start=False, stop=True)
                        x.then_inc(core.sem_e.sem, 1)

                @block.vector
                def _(dve):
                    link = core.link("dve", dve)
                    for par in range(2):
                        dve.wait_ge(core.sem_a.sem, core.sem_a.at(par + 1))
                        dve.tensor_copy(rs[po, b, par], ps[po, par, 0:T4 * HD].rearrange("p (t v) -> p t v", v=HD)
                                        ).then_inc(core.sem_b.sem, 1)
                    if c < NC - 1:
                        dve.wait_ge(core.sem_e.sem, core.sem_e.at(1))
                        nxt = st[:, c + 1]
                        new = ps[:, 4, 0:T4 * HD].rearrange("p (t v) -> p t v", v=HD)
                        f = bcast(fac[:, :, c:c + 1], [P, T4, HD])
                        if c == 0:
                            link(dve.tensor_tensor(nxt, new, f, ALU.mult))
                        else:
                            link(dve.tensor_tensor(nxt, st[:, c], new, ALU.add))
                            link(dve.tensor_tensor(nxt, nxt, f, ALU.mult))

                @block.scalar
                def _(act):
                    for par in range(2):
                        act.wait_ge(core.sem_c.sem, core.sem_c.at(par + 1))
                        act.activation(un[po, b, par], ps[po, 2 + par, 0:T4 * HD].rearrange("p (t v) -> p t v", v=HD),
                                       ACT.Copy, scale=-1.0).then_inc(core.sem_d.sem, 1)
            for sig in (core.sem_a, core.sem_b, core.sem_c, core.sem_d):
                sig.close(2)
            if c < NC - 1:
                core.sem_e.close(1)
        with core.block() as block:
            @block.tensor
            def _(pe):
                for par in range(2):
                    rr = slice(HD * par, HD * par + HD)
                    for t in range(T4):
                        h = 2 * t + par
                        for b in range(NB):
                            n = h * NB + b
                            out = ps[rr, 2 * par + t // 2, (t % 2) * TOK + b * P:(t % 2) * TOK + b * P + P]
                            pe.matmul(out, vt[:, b, h * HD:h * HD + HD], mm_[:, n, 0, 1, :], start=True, stop=False)
                            pe.matmul(out, un[:, b, par, t, :], mm_[:, n, 1, 1, :], start=False, stop=False)
                            for c in (2 * b, 2 * b + 1):
                                if c > 0:
                                    half = out[:, (c % 2) * CHUNK:(c % 2) * CHUNK + CHUNK]
                                    pe.matmul(half, st[rr, c, t, :], qq[rr, t, 1, c * CHUNK:c * CHUNK + CHUNK],
                                              start=False, stop=(c % 2 == 1))
        with core.block() as block:
            @block.vector
            def _(dve):
                for par in range(2):
                    rr = slice(HD * par, HD * par + HD)
                    dve.tensor_copy(y[rr, :, :], ps[rr, 2 * par:2 * par + 2, :].rearrange("p a (b n) -> p (a b) n", n=TOK))
        sums = head_sums(core, 4, y, T4)
        with core.block() as block:
            @block.vector
            def _(dve):
                link = core.link("dve", dve)
                link(dve.scalar_tensor_tensor(out=y[:, :, :], in0=sums, scalar=-1.0 / HD, in1=y[:, :, :], op0=ALU.mult, op1=ALU.add))
                link(dve.tensor_tensor(a[:, :, :], y[:, :, :], y[:, :, :], ALU.mult))
        sums = head_sums(core, 6, a, T4)
        rstd_of(core, sums, a[:, :, :], 1.0 / HD, 1e-5 * HD)
        with core.block() as block:
            @block.vector
            def _(dve):
                link = core.link("dve", dve)
                link(dve.tensor_tensor(y[:, :, :], y[:, :, :], a[:, :, :], ALU.mult))
                for t in range(T4):
                    link(dve.tensor_scalar(y[:, t, :], y[:, t, :], core.v("lnx_w", t), core.v("lnx_b", t), ALU.mult, ALU.add))
                link(dve.tensor_tensor(y[:, :, :], y[:, :, :], bonus[:, :, :], ALU.add))
                link(dve.tensor_tensor(y[:, :, :], y[:, :, :], gate[:, :, :], ALU.mult))


def gated_residual(core, gate):
    def take(m):
        return lambda eng, ps: eng.scalar_tensor_tensor(out=core.x[:, m, :], in0=ps, scalar=gate[:, m:m + 1],
                                                        in1=core.x[:, m, :], op0=ALU.mult, op1=ALU.add)
    return [("dve", take(m), None) for m in range(DT)]


def second_block(core):
    nc = core.nc
    mod = core.mod2
    with core.block() as block:
        @block.scalar
        def _(act):
            act.activation(core.cond2, core.vs("c_2"), ACT.Silu)
    modulation(core, "ada2", core.cond2, mod, core.vs("ada_b_2"))
    shift1, scale1, gate1, shift2, scale2, gate2 = (mod[:, 8 * i:8 * i + 8] for i in range(6))
    with ExitStack() as s:
        y = s.enter_context(nc.sbuf_tensor("mix2_y", [P, DT, TOK], F32))
        z = s.enter_context(nc.sbuf_tensor("mix2_z", [P, C_RWKV_T, TOK + 1], F32))
        lora = s.enter_context(nc.sbuf_tensor("lora_w", [P, 1024], F32))
        with ExitStack() as s2:
            qkv = s2.enter_context(nc.sbuf_tensor("stick_qkv", [P, 12, TOK], F32))
            with ExitStack() as s3:
                h = s3.enter_context(nc.sbuf_tensor("mix2_h", [P, DT, TOK], F32))
                tmp = s3.enter_context(nc.sbuf_tensor("shift_tmp", [P, TOK], F32))
                rms_modulate(core, "mix2", h, core.vs("norm1"), scale1, shift1)
                with core.block() as block:
                    @block.vector
                    def _(dve):
                        dve.memset(z[:, :, 0:1], 0.0)

                    @block.scalar
                    def _(act):
                        act.dma_start(lora[:, :], core.a["lora"]).then_inc(core.const_loaded.sem, 16)
                        act.wait_ge(core.const_loaded.sem, core.const_loaded.at(16))
                core.const_loaded.close(16)
                tiles = [("act", copy_tiles(core, lambda m: z[:, m, 1:])(m), None) for m in range(C_RWKV_T)]
                tiles += [("act", copy_tiles(core, lambda m: qkv[:, m - C_RWKV_T, :])(m), None)
                          for m in range(C_RWKV_T, 26)]

                def token_shift(dve, link):
                    for t in range(C_RWKV_T):
                        dve.wait_ge(core.act_evac.sem, core.act_evac.at(t + 1))
                        link(dve.tensor_tensor(tmp[:, :], z[:, t, 0:TOK], z[:, t, 1:], ALU.subtract))
                        link(dve.scalar_tensor_tensor(out=z[:, t, 1:], in0=tmp[:, :], scalar=core.v("mu", t),
                                                      in1=z[:, t, 1:], op0=ALU.mult, op1=ALU.add))
                linear(core, "w_in2", lambda k: h[:, k, :], tiles, head=token_shift)
            stick_breaking(core, qkv[:, 0:4, :], qkv[:, 4:8, :], qkv[:, 8:12, :], y[:, 4:8, :])
        rwkv_mix(core, z, lora, y[:, 0:4, :])
        linear(core, "w_out2", lambda k: y[:, k, :], gated_residual(core, gate1))
    moe_layer(core)


class LoopChain:

    def __init__(self, sig, eng, u, per_turn):
        self.sig, self.eng, self.u, self.per_turn, self.n = sig, eng, u, per_turn, 0

    def __call__(self, ins):
        self.n += 1
        ins.then_inc(self.sig.sem, 1)
        self.eng.wait_ge(self.sig.sem, self.u * self.per_turn + self.n)

    def done(self):
        assert self.n == self.per_turn, self.n


def mixture_of_experts(core, h, acc):
    nc, ps = core.nc, core.ps
    E, S = N_EXPERTS, UNIT
    with ExitStack() as s:
        def sb(name, shape, dt=F32):
            return s.enter_context(nc.sbuf_tensor("moe_" + name, shape, dt))
        ht = sb("ht", [P, NB, D])
        table = sb("table", [P, MAX_UNITS, 2, NB])
        unit_int = sb("unit_int", [1, MAX_UNITS + 1], I32)
        to_token_major(core, [h[:, t, :] for t in range(DT)], lambda t, b: ht[:, b, t * P:t * P + P])
        with ExitStack() as s2:
            def sb2(name, shape, dt=F32):
                return s2.enter_context(nc.sbuf_tensor("route_" + name, shape, dt))
            rw = sb2("rw", [P, DT, E])
            lg, m, g, r = (sb2(n, [P, NB, E]) for n in ("lg", "m", "g", "r"))
            mx, ix, ixf = sb2("mx", [P, NB, 8]), sb2("ix", [P, NB, 8], U32), sb2("ixf", [P, NB, 8])
            sm = sb2("sm", [P, NB, 2])
            cnt, units, cum, first = (sb2(n, [P, E]) for n in ("cnt", "units", "cum", "first"))
            ecol, onehot = sb2("ecol", [E, 2]), sb2("onehot", [E, MAX_UNITS])
            rt, gt = sb2("rt", [E, TOK]), sb2("gt", [E, TOK])
            row = sb2("row", [1, MAX_UNITS + 1])
            with core.block() as block:
                @block.scalar
                def _(act):
                    act.dma_start(rw[:, :, :], core.a["router"]).then_inc(core.const_loaded.sem, 16)

                @block.tensor
                def _(pe):
                    pe.wait_ge(core.const_loaded.sem, core.const_loaded.at(16))
                    for b in range(NB):
                        for k in range(DT):
                            pe.matmul(ps[:, 0, b * E:b * E + E], h[:, k, b * P:b * P + P], rw[:, k, :], start=(k == 0),
                                      stop=(k == DT - 1))
            core.const_loaded.close(16)
            with core.block() as block:
                @block.vector
                def _(dve):
                    link = core.link("dve", dve)
                    link(dve.tensor_tensor(lg[:, :, :], ps[:, 0, 0:NB * E].rearrange("p (b e) -> p b e", e=E),
                                           bcast(core.vs("router_b").unsqueeze(1), [P, NB, E]), ALU.add))
                    for b in range(NB):
                        link(dve.max(mx[:, b, :], lg[:, b, :]))
                        link(dve.max_index(ix[:, b, :], mx[:, b, :], lg[:, b, :]))
                    link(dve.tensor_copy(ixf[:, :, :], ix[:, :, :]))
                    for b in range(NB):
                        link(dve.tensor_scalar(m[:, b, :], core.m("iota_e"), ixf[:, b, 0:1], None, ALU.is_equal))
                        for j in range(1, TOP_K):
                            link(dve.scalar_tensor_tensor(out=m[:, b, :], in0=core.m("iota_e"), scalar=ixf[:, b, j:j + 1],
                                                          in1=m[:, b, :], op0=ALU.is_equal, op1=ALU.add))
                    link(dve.tensor_scalar(sm[:, :, 0], mx[:, :, 0], -1.0, None, ALU.mult))
            with core.block() as block:
                @block.scalar
                def _(act):
                    for b in range(NB):
                        act.activation(g[:, b, :], lg[:, b, :], ACT.Exp, bias=sm[:, b, 0:1])

                @block.tensor
                def _(pe):
                    pe.matmul(ps[:, 1, 0:E], core.m("tri_lt"), m[:, 0, :], start=True, stop=True)
                    pe.matmul(ps[:, 1, E:2 * E], core.m("tri_lt"), m[:, 1, :], start=True, stop=False)
                    pe.matmul(ps[:, 1, E:2 * E], core.m("ones"), m[:, 0, :], start=False, stop=True)
                    for b in range(NB):
                        pe.matmul(ps[:, 2, 0:E], core.m("ones"), m[:, b, :], start=(b == 0), stop=(b == NB - 1))
            with core.block() as block:
                @block.vector
                def _(dve):
                    link = core.link("dve", dve)
                    link(dve.tensor_tensor(g[:, :, :], g[:, :, :], m[:, :, :], ALU.mult))
                    link(dve.tensor_reduce(sm[:, :, 1], g[:, :, :], AX, ALU.add))
                    link(dve.reciprocal(sm[:, :, 1], sm[:, :, 1]))
                    link(dve.tensor_tensor(g[:, :, :], g[:, :, :], bcast(sm[:, :, 1:2], [P, NB, E]), ALU.mult))
                    link(dve.tensor_copy(cnt[:, :], ps[:, 2, 0:E]))
                    link(dve.tensor_scalar(units[:, :], cnt[:, :], 0.0, None, ALU.is_gt))
                    for j in range(1, TOK // S):
                        link(dve.scalar_tensor_tensor(out=units[:, :], in0=cnt[:, :], scalar=float(j * S),
                                                      in1=units[:, :], op0=ALU.is_gt, op1=ALU.add))
                    link(dve.tensor_tensor_scan(cum[:, :], core.m("ones")[:, 0:E], units[:, :], 0.0, ALU.mult, ALU.add))
                    link(dve.tensor_tensor(first[:, :], cum[:, :], units[:, :], ALU.subtract))
                    link(dve.scalar_tensor_tensor(out=r[:, :, :], in0=ps[:, 1, 0:NB * E].rearrange("p (b e) -> p b e", e=E),
                                                  scalar=1000.0, in1=m[:, :, :], op0=ALU.add, op1=ALU.mult))
                    link(dve.tensor_scalar(cnt[:, :], first[:, :], float(S), -1000.0, ALU.mult, ALU.add))
                    link(dve.tensor_tensor(r[:, :, :], r[:, :, :], bcast(cnt[:, :].unsqueeze(1), [P, NB, E]), ALU.add))
            with core.block() as block:
                @block.tensor
                def _(pe):
                    ident = core.m("ident")
                    pe.transpose(ps[0:E, 0, 0:E], cum[0:E, :], ident[0:E, 0:E])
                    pe.transpose(ps[0:E, 0, E:2 * E], first[0:E, :], ident[0:E, 0:E])
                    for b in range(NB):
                        pe.transpose(ps[0:E, 1, b * P:b * P + P], r[:, b, :], ident)
                        pe.transpose(ps[0:E, 2, b * P:b * P + P], g[:, b, :], ident)
            with core.block() as block:
                @block.vector
                def _(dve):
                    link = core.link("dve", dve)
                    link(dve.tensor_copy(ecol[:, :], ps[0:E, 0, 0:2 * E:E]))
                    link(dve.tensor_copy(rt[:, :], ps[0:E, 1, 0:TOK]))
                    link(dve.tensor_copy(gt[:, :], ps[0:E, 2, 0:TOK]))
                    iu = core.m("iota_u")[0:E, :]
                    link(dve.tensor_scalar(onehot[:, :], iu, ecol[:, 0:1], None, ALU.is_lt))
                    link(dve.scalar_tensor_tensor(out=onehot[:, :], in0=iu, scalar=ecol[:, 1:2], in1=onehot[:, :],
                                                  op0=ALU.is_ge, op1=ALU.mult))
            with core.block() as block:
                @block.tensor
                def _(pe):
                    for b in range(NB):
                        pe.matmul(ps[:, 0, b * S:b * S + MAX_UNITS], rt[:, b * P:b * P + P], onehot[:, :], start=True, stop=True)
                        pe.matmul(ps[:, 1, b * S:b * S + MAX_UNITS], gt[:, b * P:b * P + P], onehot[:, :], start=True, stop=True)
                    pe.matmul(ps[0:1, 2, 0:MAX_UNITS], core.m("col_e")[0:E, :], onehot[:, :], start=True, stop=True)
            with core.block() as block:
                @block.vector
                def _(dve):
                    link = core.link("dve", dve)
                    link(dve.tensor_copy(row[:, 0:MAX_UNITS], ps[0:1, 2, 0:MAX_UNITS]))
                    link(dve.tensor_copy(row[:, MAX_UNITS:], cum[0:1, E - 1:E]))
                    link(dve.tensor_copy(unit_int[:, :], row[:, :]))
                    for b in range(NB):
                        link(dve.scalar_tensor_tensor(out=table[:, :, 0, b], in0=core.m("iota_u"), scalar=-float(S),
                                                      in1=ps[:, 0, b * S:b * S + MAX_UNITS], op0=ALU.mult, op1=ALU.add))
                        link(dve.tensor_copy(table[:, :, 1, b], ps[:, 1, b * S:b * S + MAX_UNITS]))

        cur = sb("cur", [P, 2, NB])
        sel, selg = sb("sel", [P, NB, S]), sb("selg", [P, NB, S])
        selt, ytok = sb("selt", [S, TOK]), sb("ytok", [S, D])
        xg, hid, yb = sb("xg", [P, DT, S]), sb("hid", [P, DT, S]), sb("yb", [P, DT, S])
        glu, lin, sg = sb("glu", [P, 2, 2, S]), sb("lin", [P, 2, 2, S]), sb("sg", [P, 2, 2, S])
        eb = sb("eb", [P, 24])
        loaded = [core.counter(f"expert_panel{i}") for i in range(RING)]
        names = ("expert_bias", "expert_panel_used", "picked", "gathered", "gathered_copied", "select_turned",
                 "select_copied", "hidden_read", "glu_ready", "sigmoid_ready", "hidden_ready", "expert_out",
                 "expert_out_read", "out_turned", "out_copied", "scattered", "added", "dve_turn")
        (bias, used, picked, gathered, xg_ready, sel_turned, sel_copied, hid_read, glu_ready, sig_ready,
         hid_ready, outs, outs_read, turned, copied, scattered, added, turn) = (core.counter(n) for n in names)
        PANELS = 12
        with core.block() as block:
            @block.vector
            def _(dve):
                dve.memset(acc[:, :, :], 0.0)

            @block.tensor
            def _(pe):
                for sig in (sel_turned, xg_ready, sel_copied, outs_read, copied, added):
                    pe.sem_inc(sig.sem, 1)
                pe.sem_inc(used.sem, RING)
        for sig in (sel_turned, xg_ready, sel_copied, outs_read, copied, added):
            sig.close(1)

        def unit_count(eng):
            return eng.value_load(unit_int[0:1, MAX_UNITS:MAX_UNITS + 1], min_val=1, max_val=MAX_UNITS)

        with core.block() as block:
            @block.sync
            def _(sp):
                n = unit_count(sp)
                with sp.Fori(0, n) as u:
                    e = sp.value_load(unit_int[0:1, bass.ds(u, 1)], min_val=0, max_val=E - 1)
                    for j in range(PANELS):
                        sp.wait_ge(used.sem, used.at(u * PANELS + (j + 1)))
                        src = core.a["w1"][bass.ds(e * 8 + j, 1)] if j < 8 else core.a["w2"][bass.ds(e * 4 + (j - 8), 1)]
                        sp.dma_start(core.ring[:, j % RING, :], src.rearrange("a p n -> p (a n)")
                                     ).then_inc(loaded[j % RING].sem, 16)
                        if j == RING - 1:
                            sp.wait_ge(outs_read.sem, outs_read.at(u * 4))
                            sp.dma_start(eb[:, :], core.a["eb"][bass.ds(e, 1)].rearrange("a p n -> p (a n)")
                                         ).then_inc(bias.sem, 16)

            @block.tensor
            def _(pe):
                n = unit_count(pe)
                ident = core.m("ident")
                with pe.Fori(0, n) as u:
                    def panel(j):
                        pe.wait_ge(loaded[j % RING].sem, u * (16 * PANELS // RING) + 16 * (j // RING + 1))
                        return core.ring[:, j % RING, :]
                    pe.wait_ge(picked.sem, picked.at(u + 1))
                    pe.wait_ge(xg_ready.sem, xg_ready.at(u))
                    for k in range(DT):
                        for b in range(NB):
                            mm = pe.matmul(ps[:, 2, k * S:k * S + S], ht[:, b, k * P:k * P + P], sel[:, b, :],
                                           start=(b == 0), stop=(b == NB - 1))
                    mm.then_inc(gathered.sem, 1)
                    pe.wait_ge(sel_copied.sem, sel_copied.at(u))
                    for b in range(NB):
                        mm = pe.matmul(ps[0:S, 3, b * P:b * P + P], selg[:, b, :], ident, start=True, stop=True)
                    mm.then_inc(sel_turned.sem, 1)
                    pe.wait_ge(xg_ready.sem, xg_ready.at(u + 1))
                    pe.wait_ge(outs_read.sem, outs_read.at(u * 4))
                    for j in range(8):
                        w = panel(j)
                        c = j // 2
                        if j % 2 == 0 and c >= 2:
                            pe.wait_ge(hid_read.sem, hid_read.at(u * 4 + (c - 1)))
                        for part in range(2):
                            at = part * 2 * S + (j % 2) * S
                            for k in range(DT):
                                mm = pe.matmul(ps[:, c % 2, at:at + S], w[:, k * PANEL + part * P:k * PANEL + part * P + P],
                                               xg[:, k, :], start=(k == 0), stop=(k == DT - 1))
                        mm.then_inc(used.sem, 1)
                    for q in range(4):
                        w = panel(8 + q)
                        if q == 0:
                            pe.wait_ge(hid_ready.sem, hid_ready.at(u * 4 + 4))
                        if q >= 2:
                            pe.wait_ge(outs_read.sem, outs_read.at(u * 4 + (q - 1)))
                        for c in range(2):
                            for k in range(DT):
                                mm = pe.matmul(ps[:, q % 2, c * S:c * S + S], w[:, k * PANEL + c * P:k * PANEL + c * P + P],
                                               hid[:, k, :], start=(k == 0), stop=(k == DT - 1))
                        mm.then_inc(used.sem, 1)
                    for i in range(2):
                        pe.wait_ge(outs_read.sem, outs_read.at(u * 4 + (2 * i + 2)))
                        if i == 0:
                            pe.wait_ge(copied.sem, copied.at(u * 2))
                        for k in range(4):
                            mm = pe.matmul(ps[0:S, 4 + i, k * P:k * P + P], yb[:, 4 * i + k, :], ident, start=True, stop=True)
                        mm.then_inc(turned.sem, 1)
                    pe.wait_ge(sel_copied.sem, sel_copied.at(u + 1))
                    for i in range(4):
                        pe.wait_ge(copied.sem, copied.at(u * 2 + (i // 2 + 1)))
                        if i >= 2:
                            pe.wait_ge(added.sem, added.at(u * 4 + (i - 1)))
                        elif i == 0:
                            pe.wait_ge(added.sem, added.at(u * 4))
                        for c in range(2):
                            t = 2 * i + c
                            mm = pe.matmul(ps[:, 6 + i % 2, c * TOK:c * TOK + TOK], ytok[:, t * P:t * P + P], selt[:, :],
                                           start=True, stop=True)
                        mm.then_inc(scattered.sem, 1)

            @block.scalar
            def _(act):
                n = unit_count(act)
                with act.Fori(0, n) as u:
                    act.wait_ge(gathered.sem, gathered.at(u + 1))
                    act.activation(xg[:, :, :], ps[:, 2, :].rearrange("p (k n) -> p k n", n=S), ACT.Copy).then_inc(xg_ready.sem, 1)
                    act.wait_ge(sel_turned.sem, sel_turned.at(u + 1))
                    act.activation(selt[:, :], ps[0:S, 3, 0:TOK], ACT.Copy).then_inc(sel_copied.sem, 1)
                    for c in range(4):
                        act.wait_ge(glu_ready.sem, glu_ready.at(u * 4 + (c + 1)))
                        act.activation(sg[:, c % 2], glu[:, c % 2], ACT.Sigmoid, scale=SWIGLU_ALPHA).then_inc(sig_ready.sem, 1)
                    for i in range(2):
                        act.wait_ge(turned.sem, turned.at(u * 2 + (i + 1)))
                        act.activation(ytok[:, 512 * i:512 * i + 512], ps[0:S, 4 + i, :], ACT.Copy).then_inc(copied.sem, 1)

            @block.vector
            def _(dve):
                n = unit_count(dve)
                with dve.Fori(0, n) as u:
                    link = LoopChain(turn, dve, u, 1 + 4 * 5)
                    dve.wait_ge(sel_turned.sem, sel_turned.at(u))
                    link(dve.tensor_copy(cur[:, :, :], table[:, bass.ds(u, 1)].rearrange("p a i b -> p (a i) b")))
                    for b in range(NB):
                        dve.tensor_scalar(sel[:, b, :], core.m("iota_slot"), cur[:, 0, b:b + 1], None, ALU.is_equal)
                        ins = dve.tensor_scalar(selg[:, b, :], core.m("iota_slot"), cur[:, 0, b:b + 1], cur[:, 1, b:b + 1],
                                                ALU.is_equal, ALU.mult)
                    ins.then_inc(picked.sem, 1)
                    dve.wait_ge(bias.sem, u * 16 + 16)
                    for c in range(4):
                        gl, ln = glu[:, c % 2], lin[:, c % 2]
                        dve.wait_ge(used.sem, used.at(u * PANELS + (RING + 2 * c + 2)))
                        src = ps[:, c % 2, 0:4 * S].rearrange("p (a k n) -> p a k n", a=2, n=S)
                        link(dve.tensor_tensor(gl, src[:, 0], bcast(eb[:, 2 * c:2 * c + 2].unsqueeze(2), [P, 2, S]), ALU.add))
                        dve.tensor_tensor(ln, src[:, 1], bcast(eb[:, 8 + 2 * c:10 + 2 * c].unsqueeze(2), [P, 2, S]),
                                          ALU.add).then_inc(hid_read.sem, 1)
                        dve.tensor_scalar(gl, gl, SWIGLU_LIMIT, None, ALU.min).then_inc(glu_ready.sem, 1)
                        dve.wait_ge(hid_read.sem, hid_read.at(u * 4 + (c + 1)))
                        link(dve.tensor_scalar(ln, ln, SWIGLU_LIMIT, -SWIGLU_LIMIT, ALU.min, ALU.max))
                        link(dve.tensor_scalar(ln, ln, 1.0, None, ALU.add))
                        dve.wait_ge(glu_ready.sem, glu_ready.at(u * 4 + (c + 1)))
                        link(dve.tensor_tensor(ln, ln, gl, ALU.mult))
                        dve.wait_ge(sig_ready.sem, sig_ready.at(u * 4 + (c + 1)))
                        link(dve.tensor_tensor(hid[:, 2 * c:2 * c + 2, :], ln, sg[:, c % 2], ALU.mult))
                        dve.sem_inc(hid_ready.sem, 1)
                    for q in range(4):
                        dve.wait_ge(used.sem, used.at(u * PANELS + (RING + 8 + q + 1)))
                        dve.tensor_tensor(yb[:, 2 * q:2 * q + 2, :], ps[:, q % 2, 0:2 * S].rearrange("p (k n) -> p k n", n=S),
                                          bcast(eb[:, 16 + 2 * q:18 + 2 * q].unsqueeze(2), [P, 2, S]), ALU.add
                                          ).then_inc(outs_read.sem, 1)
                    for i in range(4):
                        dve.wait_ge(scattered.sem, scattered.at(u * 4 + (i + 1)))
                        dve.wait_ge(added.sem, added.at(u * 4 + i))
                        dve.tensor_tensor(acc[:, 2 * i:2 * i + 2, :], acc[:, 2 * i:2 * i + 2, :],
                                          ps[:, 6 + i % 2, :].rearrange("p (k n) -> p k n", n=TOK), ALU.add
                                          ).then_inc(added.sem, 1)
                    link.done()


def moe_layer(core):
    nc = core.nc
    with ExitStack() as s:
        h = s.enter_context(nc.sbuf_tensor("moe_h", [P, DT, TOK], F32))
        acc = s.enter_context(nc.sbuf_tensor("moe_acc", [P, DT, TOK], F32))
        mod = core.mod2
        rms_modulate(core, "moe", h, core.vs("norm2"), mod[:, 32:40], mod[:, 24:32])
        mixture_of_experts(core, h, acc)
        with core.block() as block:
            @block.vector
            def _(dve):
                for k in range(DT):
                    dve.scalar_tensor_tensor(out=core.x[:, k, :], in0=acc[:, k, :], scalar=mod[:, 40 + k:41 + k],
                                             in1=core.x[:, k, :], op0=ALU.mult, op1=ALU.add)


def switch_stream(core, stream):
    assert core.issued == core.used == len(core.stream)
    for slot in range(RING):
        core.panel_loaded[slot].close(16 * len(range(slot, len(core.stream), RING)))
    core.panel_used.close(len(core.stream))
    core.stream, core.issued, core.used = panels_of(stream), 0, 0


def rms_tiles(core, name, t, g, width):
    n = width // P
    with ExitStack() as s:
        sq = s.enter_context(core.nc.sbuf_tensor(f"{name}_sq", [P, n, TOK], F32))
        rs = s.enter_context(core.nc.sbuf_tensor(f"{name}_rs", [P, TOK], F32))
        with core.block() as block:
            @block.scalar
            def _(act):
                act.activation(sq[:, :, :], t, ACT.Square)
        column_sums(core, [(core.ps[:, 4, 0:TOK], core.m("ones"), [sq[:, k, :] for k in range(n)])])
        rstd_of(core, core.ps[:, 4, 0:TOK], rs[:, :], 1.0 / width, RMS_EPS)
        with core.block() as block:
            @block.vector
            def _(dve):
                for k in range(n):
                    dve.scalar_tensor_tensor(out=t[:, k, :], in0=t[:, k, :], scalar=core.v(g, k), in1=rs[:, :],
                                             op0=ALU.mult, op1=ALU.mult)


TWO_PI_PARTS = (6.28125, 1.935303211212158e-03, 2.535181590533e-09)
ROUND = 1.5 * 2.0 ** 23
HALF_PI = float(np.float32(np.pi / 2))
PI = float(np.nextafter(np.float32(np.pi), np.float32(0)))


def rope_tables(core, pos, tables):
    nc = core.nc
    with ExitStack() as s:
        ang = s.enter_context(nc.sbuf_tensor("rope_angle", [P, TOK], F32))
        turns = s.enter_context(nc.sbuf_tensor("rope_turns", [P, TOK], F32))
        with core.block() as block:
            @block.vector
            def _(dve):
                link = core.link("dve", dve)
                for invf, cos, sin in tables:
                    for out, lead in ((sin, 0.0), (cos, HALF_PI)):
                        link(dve.tensor_scalar(ang[:, :], pos, core.m(invf), None, ALU.mult))
                        link(dve.tensor_scalar(turns[:, :], ang[:, :], 1.0 / (2 * np.pi), lead / (2 * np.pi), ALU.mult, ALU.add))
                        link(dve.tensor_scalar(turns[:, :], turns[:, :], ROUND, None, ALU.add))
                        link(dve.tensor_scalar(turns[:, :], turns[:, :], ROUND, None, ALU.subtract))
                        for c in TWO_PI_PARTS:
                            link(dve.scalar_tensor_tensor(out=ang[:, :], in0=turns[:, :], scalar=-c, in1=ang[:, :],
                                                          op0=ALU.mult, op1=ALU.add))
                        if lead:
                            link(dve.tensor_scalar(ang[:, :], ang[:, :], lead, None, ALU.add))
                        link(dve.tensor_scalar(out, ang[:, :], PI, -PI, ALU.min, ALU.max))
        with core.block() as block:
            @block.scalar
            def _(act):
                for _, cos, sin in tables:
                    act.activation(cos, cos, ACT.Sin)
                    act.activation(sin, sin, ACT.Sin)


def rope(core, name, tiles, rot, cos, sin):
    nc, ps = core.nc, core.ps
    with ExitStack() as s:
        part = s.enter_context(nc.sbuf_tensor(f"{name}_part", [P, 2, TOK], F32))
        swapped, done = core.sem_a, core.sem_b
        with core.block() as block:
            @block.tensor
            def _(pe):
                for i, t in enumerate(tiles):
                    if i >= 4:
                        pe.wait_ge(done.sem, done.at(i - 3))
                    pe.matmul(ps[:, i % 4, 0:TOK], core.m(rot), t, start=True, stop=True).then_inc(swapped.sem, 1)

            @block.vector
            def _(dve):
                link = core.link("dve", dve)
                for i, t in enumerate(tiles):
                    dve.wait_ge(swapped.sem, swapped.at(i + 1))
                    dve.tensor_tensor(part[:, i % 2, :], ps[:, i % 4, 0:TOK], sin, ALU.mult).then_inc(done.sem, 1)
                    link(dve.tensor_tensor(t, t, cos, ALU.mult))
                    dve.wait_ge(done.sem, done.at(i + 1))
                    link(dve.tensor_tensor(t, t, part[:, i % 2, :], ALU.add))
        swapped.close(len(tiles))
        done.close(len(tiles))


def third_block(core):
    nc, x = core.nc, core.x
    switch_stream(core, STREAM_2)
    with ExitStack() as s:
        def sb(name, shape, dt=F32):
            return s.enter_context(nc.sbuf_tensor("third_" + name, shape, dt))
        pos_int, pos = sb("pos_int", [P, TOK], I32), sb("pos", [P, TOK])
        tab = sb("tab", [P, 4, TOK])
        cos32, sin32, cos64, sin64 = (tab[:, i, :] for i in range(4))
        with core.block() as block:
            @block.sync
            def _(sp):
                issue_panels(core, sp, RING)

            @block.scalar
            def _(act):
                act.dma_start(pos_int[:, :], core.a["positions"]).then_inc(core.const_loaded.sem, 16)
                act.activation(core.cond3, core.vs("c_3"), ACT.Silu)

            @block.vector
            def _(dve):
                dve.wait_ge(core.const_loaded.sem, core.const_loaded.at(16))
                dve.tensor_copy(pos[:, :], pos_int[:, :])
        core.const_loaded.close(16)
        modulation(core, "ada3", core.cond3, core.mod3, core.vs("b_ada_3"))
        rope_tables(core, pos[:, :], [("invf32", cos32, sin32), ("invf64", cos64, sin64)])
        shift, scale, gate = (core.mod3[:, 8 * i:8 * i + 8] for i in range(3))
        n_lat, n_z, n_mb = 4, 4, 12
        lat = sb("lat", [P, n_lat, TOK])
        z_mla, z_mb = sb("z_mla", [P, n_z, TOK]), sb("z_mb", [P, n_z, TOK])
        mb = sb("moba_qkv", [P, n_mb, TOK])
        merge = sb("merge", [P, 2 * DT, TOK])
        h = sb("h", [P, DT, TOK])
        rms_modulate(core, "third", h, core.vs("g_pre"), scale, shift)

        def plain(dst):
            return [("act", copy_tiles(core, lambda m: dst[:, m, :])(m), None) for m in range(dst.shape[1])]

        def silu(dst):
            return [("act", copy_tiles(core, lambda m: dst[:, m, :], func=ACT.Silu)(m), None) for m in range(n_z)]
        gates = [("act", copy_tiles(core, lambda m: merge[:, m, :], func=ACT.Sigmoid,
                                    bias=lambda m: core.v("b_merge", m))(m), None) for m in range(2 * DT)]
        linear(core, "w_in3", lambda k: h[:, k, :], plain(lat) + silu(z_mla) + plain(mb) + silu(z_mb) + gates)

        o = sb("o", [P, n_z, TOK])
        vt = sb("vt", [P, NB, 4 * P])
        with ExitStack() as s2:
            q = s2.enter_context(nc.sbuf_tensor("mla_q", [P, DT, TOK], F32))
            kv = s2.enter_context(nc.sbuf_tensor("mla_kv", [P, DT + 4, TOK], F32))
            rms_tiles(core, "q_lat", lat[:, 0:2, :], "g_q_lat", 2 * P)
            rms_tiles(core, "kv_lat", lat[:, 2:3, :], "g_kv_lat", P)
            linear(core, "w_uq", lambda k: lat[:, k, :], plain(q))
            linear(core, "w_ukv", lambda k: lat[:, 2, :], plain(kv))
            rope(core, "mla", [q[:, t, :] for t in range(DT)] + [lat[:, 3, :]], "rot32", cos32, sin32)
            with core.block() as block:
                @block.vector
                def _(dve):
                    for t in range(DT):
                        dve.tensor_copy(kv[64:96, t, :], lat[64:96, 3, :])
            to_token_major(core, [kv[:, DT + t, :] for t in range(4)], lambda t, b: vt[:, b, t * P:t * P + P])
            softmax_attention(core, "mla", range(8), lambda u: q[:, u, :], lambda u: kv[:, u, :],
                              lambda u, b: vt[:, b, HD * u:HD * u + HD], "causal", 96 ** -0.5,
                              lambda e, j, p: e.tensor_tensor(o[:, j, :], p, z_mla[:, j, :], ALU.mult))
        y = h
        tiles = []
        for m in range(DT):
            def take_a(e, p, m=m):
                return e.tensor_tensor(y[:, m, :], p, merge[:, m, :], ALU.mult)
            tiles.append(("dve", take_a, None))
        linear(core, "w_om", lambda k: o[:, k, :], tiles)

        rope(core, "moba", [mb[:, t, :] for t in range(8)], "rot64", cos64, sin64)
        to_token_major(core, [mb[:, 8 + t, :] for t in range(4)], lambda t, b: vt[:, b, t * P:t * P + P])

        def half(u):
            return slice(HD * (u % 2), HD * (u % 2) + HD)
        softmax_attention(core, "moba", range(8), lambda u: mb[half(u), u // 2, :], lambda u: mb[half(u), 4 + u // 2, :],
                          lambda u, b: vt[:, b, HD * u:HD * u + HD], "causal", HD ** -0.5,
                          lambda e, j, p: e.tensor_tensor(o[:, j, :], p, z_mb[:, j, :], ALU.mult))
        tiles = []
        for m in range(DT):
            def take_b(e, p, m=m):
                return e.tensor_tensor(merge[:, DT + m, :], p, merge[:, DT + m, :], ALU.mult)

            def after(e, link, wait_tile, m=m):
                wait_tile(e, m)
                link(e.tensor_tensor(y[:, m, :], y[:, m, :], merge[:, DT + m, :], ALU.add))
            tiles.append(("dve", take_b, after))
        linear(core, "w_ob", lambda k: o[:, k, :], tiles)

        out = merge[:, 0:DT, :]
        linear(core, "w_out3", lambda k: y[:, k, :], plain(out))
        sq, rs, gg = merge[:, DT:, :], sb("out_rs", [P, TOK]), sb("gg", [P, DT])
        with core.block() as block:
            @block.scalar
            def _(act):
                for k in range(DT):
                    act.activation(sq[:, k, :], out[:, k, :], ACT.Square).then_inc(core.sem_a.sem, 1)

            @block.tensor
            def _(pe):
                for k in range(DT):
                    pe.wait_ge(core.sem_a.sem, core.sem_a.at(k + 1))
                    pe.matmul(core.ps[:, 4, 0:TOK], core.m("ones"), sq[:, k, :], start=(k == 0), stop=(k == DT - 1))

            @block.vector
            def _(dve):
                dve.tensor_tensor(gg[:, :], gate, core.vs("g_post"), ALU.mult)
        core.sem_a.close(DT)
        rstd_of(core, core.ps[:, 4, 0:TOK], rs[:, :], 1.0 / D, RMS_EPS)
        with core.block() as block:
            @block.vector
            def _(dve):
                link = core.link("dve", dve)
                for k in range(DT):
                    link(dve.scalar_tensor_tensor(out=out[:, k, :], in0=out[:, k, :], scalar=gg[:, k:k + 1], in1=rs[:, :],
                                                  op0=ALU.mult, op1=ALU.mult))
                    link(dve.tensor_tensor(x[:, k, :], x[:, k, :], out[:, k, :], ALU.add))


def start(core):
    with core.block() as block:
        @block.scalar
        def _(act):
            act.dma_start(core.x[:, :, :], core.a["x"]).then_inc(core.const_loaded.sem, 16)
            act.dma_start(core.vec[:, :], core.a["vectors"]).then_inc(core.const_loaded.sem, 16)
            act.dma_start(core.mat[:, :], core.a["matrices"]).then_inc(core.const_loaded.sem, 16)
            act.wait_ge(core.const_loaded.sem, core.const_loaded.at(48))

        @block.sync
        def _(sp):
            issue_panels(core, sp, RING)
    core.const_loaded.close(48)


def finish(core):
    with core.block() as block:
        @block.scalar
        def _(act):
            act.dma_start(core.a["out"], core.x[:, :, :]).then_inc(core.const_loaded.sem, 16)
            act.wait_ge(core.const_loaded.sem, core.const_loaded.at(16))
    core.const_loaded.close(16)


def blocks_kernel(nc, a, stages=99):
    with ExitStack() as ctx:
        core = Core(nc, a, ctx)
        start(core)
        steps = [lambda: ssd_layer(core), lambda: ffn(core, 0), lambda: per_layer_embedding(core, 0),
                 lambda: attention_layer(core), lambda: ffn(core, 1), lambda: per_layer_embedding(core, 1),
                 lambda: second_block(core), lambda: third_block(core)]
        for step in steps[:stages]:
            step()
        finish(core)


def tokens_last(x):
    return np.ascontiguousarray(x.reshape(x.shape[0], -1, P).transpose(2, 1, 0))


def column(v):
    return v.reshape(-1, P).T


def panels(w, width=PANEL):
    k, n = w.shape
    return np.ascontiguousarray(w.reshape(k // P, P, n // width, width).transpose(2, 1, 0, 3)).reshape(n // width, P, -1)


def short(v):
    out = np.zeros((P, 1), np.float32)
    out[:v.size, 0] = v.ravel()
    return out


def rows(v, n=None):
    return np.broadcast_to(v.reshape(1, -1), (P, v.size))


def head_order(first):
    order = []
    for t in range(8):
        pair = t // 4
        for half in range(2):
            h = 8 * pair + 4 * half + t % 4
            order += [first + HD * h + i for i in range(HD)]
    return order


def layout(i):
    f = {k: np.asarray(v) for k, v in i.items()}
    a = {"x": tokens_last(f["x"][0]), "p": np.stack([tokens_last(f["p"][l, 0]) for l in range(DEPTH)])}
    w = f["w_in_mix"][0]
    z, xbc, dt, sc = np.split(w, [1024, 2560, 2576], axis=1)
    sb, sc_c, sc_h = np.split(sc, 3, axis=1)
    a["w_in"] = panels(np.concatenate([xbc, sc_c, sc_h, sb, z], axis=1))
    a["w_dt"] = np.ascontiguousarray(dt.reshape(DT, P, 16).transpose(1, 0, 2))
    a["w_out"] = panels(f["w_out_mix"][0])
    for l in range(DEPTH):
        g, u = f["w_ffn_gate"][l].reshape(D, FF_T, P), f["w_ffn_up"][l].reshape(D, FF_T, P)
        a[f"ffn_up{l}"] = panels(np.stack([g, u], axis=2).reshape(D, 2 * D_FF))
        a[f"ffn_dn{l}"] = panels(f["w_ffn_down"][l])
        a[f"ple_g{l}"] = panels(f["w_ple_gate"][l])
        a[f"ple_p{l}"] = panels(f["w_ple"][l])
    qo = head_order(0)
    perm = np.array(qo + list(range(D, 1536)))
    a["qkv"] = panels(f["w_qkv"][0][:, perm])
    a["w_o"] = panels(f["w_o"][0][np.array(qo), :])
    vec = {
        "dt_bias": short(f["ssd_dt_bias"]), "a_log": short(f["ssd_a_log"]),
        "conv_w": column(f["ssd_conv_w"][0]), "conv_b": column(f["ssd_conv_b"][0]), "sc_w": column(f["sc_conv_w"][0]),
        "ssd_d": column(np.repeat(f["ssd_d"][0], HD)), "ssd_norm": column(f["ssd_norm_w"][0]),
        "ln_mix_g": column(f["ln_mix_g"]), "ln_mix_b": column(f["ln_mix_b"]),
        "ln_ffn_g": column(f["ln_ffn_g"]), "ln_ffn_b": column(f["ln_ffn_b"]), "b_ple": column(f["b_ple_gate"]),
        "b_qkv": column(f["b_qkv"][0][perm]), "b_o": column(f["b_o"]), "sinks": rows(f["attn_sinks"][0]),
        "c_2": column(f["c_2"]), "norm1": column(f["norm1_g_2"]), "norm2": column(f["norm2_g_2"]),
        "ada_b_2": column(f["ada_b_2"]), "mu": column(f["shift_mu_2"]), "decay_w0": column(f["decay_w0_2"]),
        "iclr_a0": column(f["iclr_a0_2"]), "k_k": column(f["k_k_2"]), "k_a": column(f["k_a_2"]),
        "r_k": column(f["r_k_2"]), "lnx_w": column(f["lnx_w_2"]), "lnx_b": column(f["lnx_b_2"]),
        "q_norm": np.tile(f["q_norm_g_2"].reshape(HD, 1), (2, 1)), "k_norm": np.tile(f["k_norm_g_2"].reshape(HD, 1), (2, 1)),
        "sb_out": column(f["sb_out_g_2"]), "router_b": rows(f["router_b_2"]),
        "c_3": column(f["c_3"]), "b_ada_3": column(f["b_ada_3"]), "g_pre": column(f["g_pre_3"]),
        "g_post": column(f["g_post_3"]), "g_q_lat": column(f["g_q_lat_3"]), "g_kv_lat": column(f["g_kv_lat_3"]),
        "b_merge": column(f["b_merge_3"]),
    }
    assert all(vec[n].shape == (P, w) for n, w in VECTORS), [n for n, w in VECTORS if vec[n].shape != (P, w)]
    a["vectors"] = np.ascontiguousarray(np.concatenate([vec[n] for n, _ in VECTORS], axis=1))
    a["matrices"] = constant_matrices()
    a["ada2"] = panels(f["ada_w_2"][0])
    a["w_in2"] = panels(f["w_in_2"][0])
    a["w_out2"] = panels(f["w_out_2"][0])
    a["lora"] = np.ascontiguousarray(np.concatenate([
        np.concatenate([f["decay_up_2"][0], f["iclr_up_2"][0]], axis=0), f["gate_up_2"][0]], axis=1))
    a["router"] = np.ascontiguousarray(f["router_w_2"][0].reshape(DT, P, N_EXPERTS).transpose(1, 0, 2))
    a["w1"] = np.ascontiguousarray(f["exp_w1_2"][0].reshape(N_EXPERTS, DT, P, 2, 8, P).transpose(0, 4, 2, 1, 3, 5)
                                   ).reshape(N_EXPERTS * 8, P, SLOT)
    a["w2"] = np.ascontiguousarray(f["exp_w2_2"][0].reshape(N_EXPERTS, DT, P, 4, PANEL).transpose(0, 3, 2, 1, 4)
                                   ).reshape(N_EXPERTS * 4, P, SLOT)
    a["eb"] = np.ascontiguousarray(np.concatenate([
        f["exp_b1_2"][0].reshape(N_EXPERTS, 16, P), f["exp_b2_2"][0].reshape(N_EXPERTS, 8, P)], axis=1).transpose(0, 2, 1))
    w = f["w_in_3"][0]
    q_lat, kv_lat, k_rope, z_mla, q_mb, k_mb, v_mb, z_mb, merge = np.split(
        w, np.cumsum([256, 128, 32, 512, 512, 512, 512, 512]), axis=1)
    a["w_in3"] = panels(np.concatenate([q_lat, kv_lat, np.tile(k_rope, (1, 4)), z_mla, q_mb, k_mb, v_mb, z_mb, merge], axis=1))
    a["ada3"] = panels(f["w_ada_3"][0])
    uq = f["w_uq_3"][0].reshape(256, 8, 96)
    a["w_uq"] = panels(np.pad(uq, ((0, 0), (0, 0), (0, 32))).reshape(256, 1024))
    ukv = f["w_ukv_3"][0].reshape(128, 8, 2, 64)
    k_nope = np.pad(ukv[:, :, 0], ((0, 0), (0, 0), (0, 64))).reshape(128, 1024)
    a["w_ukv"] = panels(np.concatenate([k_nope, ukv[:, :, 1].reshape(128, 512)], axis=1))
    a["w_om"] = panels(f["w_o_mla_3"][0])
    a["w_ob"] = panels(f["w_o_moba_3"][0])
    a["w_out3"] = panels(f["w_out_3"][0])
    a["positions"] = np.ascontiguousarray(np.broadcast_to(f["positions_3"].astype(np.int32).reshape(1, TOK), (P, TOK)))
    return a


def kernel(**inputs):
    import concourse.bacc as bacc
    from concourse.bass_utils import run_bass_kernel_spmd

    nc = bacc.Bacc("TRN2", target_bir_lowering=False, num_devices=1)
    arrays = layout(inputs)
    a = {n: nc.dram_tensor(f"{n}_dram", v.shape, mybir.dt.from_np(v.dtype), kind="ExternalInput").ap()
         for n, v in arrays.items()}
    a["out"] = nc.dram_tensor("out_dram", (P, DT, TOK), F32, kind="ExternalOutput").ap()
    blocks_kernel(nc, a)
    r = run_bass_kernel_spmd(nc, [{f"{n}_dram": v for n, v in arrays.items()}], core_ids=[0])
    out = r.results[0]["out_dram"]
    return np.ascontiguousarray(out.transpose(2, 1, 0)).reshape(1, TOK, D)
```

```python
import numpy as np
from contextlib import ExitStack

import concourse.bass as bass
from concourse import mybir

F32 = mybir.dt.float32
I32 = mybir.dt.int32
BF16 = mybir.dt.bfloat16
U32 = mybir.dt.uint32
ALU = mybir.AluOpType
ACT = mybir.ActivationFunctionType
AX = mybir.AxisListType.X

P = 128
TOK = 256
NB = TOK // P
D = 1024
DT = D // P
DEPTH = 2
PANEL = 256
KG = 8
RING = 6
SLOT = KG * PANEL
ALPHA = (2 * DEPTH) ** 0.25
LN_EPS = 1e-5

SSD_HEADS, SSD_CHUNK, SSD_CONV, SC_CONV = 16, 128, 4, 3
SSD_GROUPS, HPG = 2, 8
XBC_T = 12
D_FF = 2816
FF_T = D_FF // P
HD = 64

C_RWKV_T, CHUNK = 14, 64
N_EXPERTS, TOP_K = 32, 4
UNIT = 64
MAX_UNITS = N_EXPERTS + TOK * TOP_K // UNIT
UNITS = MAX_UNITS + 1
SWIGLU_ALPHA, SWIGLU_LIMIT = 1.702, 7.0
RMS_EPS = 1e-6
BIG = 1.0e30


VECTORS = [
    ("dt_bias", 1), ("a_log", 1), ("conv_w", SSD_CONV * XBC_T), ("conv_b", XBC_T), ("sc_w", SC_CONV * DT),
    ("ssd_d", DT), ("ssd_norm", DT),
    ("ln_mix_g", 2 * DT), ("ln_mix_b", 2 * DT), ("ln_ffn_g", 2 * DT), ("ln_ffn_b", 2 * DT), ("b_ple", 2 * DT),
    ("b_qkv", 12), ("b_o", DT), ("sinks", 16),
    ("c_2", DT), ("norm1", DT), ("norm2", DT), ("ada_b_2", 48), ("mu", C_RWKV_T), ("decay_w0", 4), ("iclr_a0", 4),
    ("k_k", 4), ("k_a", 4), ("r_k", 4), ("lnx_w", 4), ("lnx_b", 4), ("q_norm", 1), ("k_norm", 1), ("sb_out", 4),
    ("router_b", N_EXPERTS),
    ("c_3", DT), ("b_ada_3", 24), ("g_pre", DT), ("g_post", DT), ("g_q_lat", 2), ("g_kv_lat", 1), ("b_merge", 16),
]
MATRICES = [
    ("ident", P), ("fold", 32), ("ones", P), ("head_ones", P), ("tri_le", P), ("tri_lt", P), ("tri_gt", P),
    ("lt64", P), ("le64", P), ("level", 6 * P), ("rot64", P), ("rot32", P), ("band", 3 * P), ("causal", 3 * P),
    ("iota_slot", 2 * UNIT), ("iota_e", N_EXPERTS), ("iota_u", UNITS), ("col_e", 1), ("invf64", 1), ("invf32", 1),
    ("scan_keep", TOK),
]


def offsets(table):
    at, out = 0, {}
    for name, n in table:
        out[name] = (at, n)
        at += n
    return out, at


def constant_matrices():
    r = np.arange(P)[:, None]
    c = np.arange(P)[None, :]
    c2 = np.arange(2 * P)[None, :]
    m = {
        "ident": r == c, "fold": r % 32 == c[:, :32], "ones": np.ones((P, P)), "head_ones": r // HD == c // HD,
        "tri_le": r <= c, "tri_lt": r < c, "tri_gt": r > c,
        "lt64": (r // CHUNK == c // CHUNK) & (r < c), "le64": (r // CHUNK == c // CHUNK) & (r <= c),
    }
    m["level"] = np.concatenate([
        (r // (2 * b) == c // (2 * b)) & ((c // b) % 2 == 1) & ((r // b) % 2 == 0) for b in (1, 2, 4, 8, 16, 32)], axis=1)

    def rotation(width):
        half = width // 2
        low = c % width < half
        return np.where(low, -1.0 * (r == c + half), 1.0 * (r == c - half))

    m["rot64"] = rotation(64)
    rotated = (c >= 64) & (c < 96)
    m["rot32"] = rotation(32) * rotated
    rel = r + P - c2
    for name, ok in (("band", (rel >= 0) & (rel < 128)), ("causal", rel >= 0)):
        full = np.where(ok, 0.0, -BIG)
        m[name] = np.concatenate([full[:, P:], full], axis=1)
    m["iota_slot"] = np.broadcast_to(np.arange(2 * UNIT) % UNIT, (P, 2 * UNIT))
    m["iota_e"] = np.broadcast_to(np.arange(N_EXPERTS), (P, N_EXPERTS))
    m["iota_u"] = np.broadcast_to(np.arange(UNITS), (P, UNITS))
    m["col_e"] = r % N_EXPERTS
    m["invf64"] = np.float32(10000.0) ** (-(np.arange(P) % 32).astype(np.float32) / np.float32(32))[:, None]
    m["invf32"] = np.float32(10000.0) ** (-(np.arange(P) % 16).astype(np.float32) / np.float32(16))[:, None] * rotated.T
    m["scan_keep"] = np.broadcast_to((np.arange(TOK) % CHUNK != 0), (P, TOK))
    return np.concatenate([np.asarray(m[n], np.float32).reshape(P, w) for n, w in MATRICES], axis=1)


STREAM_1 = [
    ("w_in", 22, 8, 256), ("w_out", 4, 16, 256),
    ("ffn_up0", 22, 8, 256, ("ada2", 24)), ("ffn_dn0", 4, 22, 256), ("ple_g0", 4, 8, 256), ("ple_p0", 4, 2, 256),
    ("qkv", 6, 8, 256), ("w_o", 4, 8, 256),
    ("ffn_up1", 22, 8, 256, ("ada3", 12)), ("ffn_dn1", 4, 22, 256), ("ple_g1", 4, 8, 256), ("ple_p1", 4, 2, 256),
    ("w_in2", 13, 8, 256), ("w_out2", 4, 8, 256),
]
STREAM_2 = [
    ("w_in3", 20, 8, 256), ("w_uq", 4, 2, 256), ("w_ukv", 6, 1, 256),
    ("w_om", 4, 4, 256), ("w_ob", 4, 4, 256), ("w_out3", 4, 8, 256),
]


def panels_of(stream):
    out = []
    for name, n, kt, _, *side in stream:
        side = [(side[0][0], j, 0, KG) for j in range(side[0][1])] if side else []
        for j in range(n):
            for k0 in range(0, kt, KG):
                out.append((name, j, k0, min(KG, kt - k0)))
            out += side[:1]
            side = side[1:]
        out += side
    return out


class Signal:

    def __init__(self, sem):
        self.sem, self.base = sem, 0

    def at(self, n):
        return self.base + n

    def close(self, n):
        self.base += n


class Core:

    def __init__(self, nc, a, ctx):
        self.nc, self.a, self.ctx = nc, a, ctx
        self.v_at, nv = offsets(VECTORS)
        self.m_at, nm = offsets(MATRICES)
        self.vec = self.sb("vec", [P, nv])
        self.mat = self.sb("mat", [P, nm])
        self.x = self.sb("x_res", [P, DT, TOK])
        self.ring = self.sb("ring", [P, RING, SLOT])
        self.ps = ctx.enter_context(nc.psum_tensor("ps", [P, 8, 512], F32))
        self.panel_loaded = [self.counter(f"panel_loaded{s}") for s in range(RING)]
        self.panel_used = self.counter("panel_used")
        self.act_evac = self.counter("act_evac")
        self.dve_evac = self.counter("dve_evac")
        self.const_loaded = self.counter("const_loaded")
        self.chain = {e: self.counter(f"{e}_chain") for e in ("pe", "act", "dve", "pool")}
        self.sem_a, self.sem_b, self.sem_c, self.sem_d, self.sem_e = (
            self.counter(n) for n in ("stage_in", "stage_mid", "stage_exp", "stage_mul", "stage_out"))
        self.sem_f, self.sem_g, self.sem_h = self.counter("stage_aux"), self.counter("stage_aux2"), self.counter("stage_end")
        small = self.sb("modulations", [P, 48 + 24])
        self.mod2, self.mod3 = small[:, 0:48], small[:, 48:72]
        self.stream, self.issued, self.used = panels_of(STREAM_1), 0, 0

    def sb(self, name, shape, dt=F32):
        return self.ctx.enter_context(self.nc.sbuf_tensor(name, shape, dt))

    def counter(self, name):
        return Signal(self.ctx.enter_context(self.nc.semaphore(name)))

    def v(self, name, i=0, parts=P):
        at, n = self.v_at[name]
        return self.vec[0:parts, at + i:at + i + 1]

    def vs(self, name):
        at, n = self.v_at[name]
        return self.vec[:, at:at + n]

    def m(self, name, i=0, w=None):
        at, n = self.m_at[name]
        w = w or min(n, P)
        return self.mat[:, at + i * w:at + i * w + w]

    def dump(self, name, ap):
        if name in self.a:
            with self.block() as block:
                @block.scalar
                def _(act):
                    act.dma_start(self.a[name], ap).then_inc(self.const_loaded.sem, 16)
                    act.wait_ge(self.const_loaded.sem, self.const_loaded.at(16))
            self.const_loaded.close(16)

    def block(self):
        return self.nc.Block(no_gpsimd_drain=True)

    def link(self, which, eng):
        sig = self.chain[which]

        def link(ins):
            sig.base += 1
            ins.then_inc(sig.sem, 1)
            eng.wait_ge(sig.sem, sig.base)
        return link


def issue_panels(core, sp, upto):
    while core.issued < min(upto, len(core.stream)):
        i = core.issued
        name, j, k0, kn = core.stream[i]
        slot = i % RING
        if i >= RING:
            sp.wait_ge(core.panel_used.sem, core.panel_used.at(i - RING + 1))
        w = core.a[name][j, :, k0 * PANEL:(k0 + kn) * PANEL]
        sp.dma_start(core.ring[:, slot, 0:kn * PANEL], w).then_inc(core.panel_loaded[slot].sem, 16)
        core.issued += 1


def linear(core, name, src, tiles, head=None, side=None, act_work=None, pool_work=None):
    nc = core.nc
    mine = []
    i = core.used
    while i < len(core.stream) and (core.stream[i][0] == name or side and core.stream[i][0].startswith("ada")):
        mine.append(i)
        i += 1
    assert mine, name
    own = [i for i in mine if core.stream[i][0] == name]
    kt = max(core.stream[i][2] + core.stream[i][3] for i in own)
    last_panel = {core.stream[i][1]: i for i in own}
    order = {}
    counts = {"act": 0, "dve": 0}
    for i, t in enumerate(tiles):
        counts[t[0]] += 1
        order[i] = (t[0], counts[t[0]])
    evac = {"act": core.act_evac, "dve": core.dve_evac}
    BANKS = 4

    def wait_tile(eng, i):
        which, n = order[i]
        eng.wait_ge(evac[which].sem, evac[which].at(n))

    with core.block() as block:
        @block.sync
        def _(sp):
            issue_panels(core, sp, mine[-1] + 1 + RING)

        @block.tensor
        def _(pe):
            for i in mine:
                panel, j, k0, kn = core.stream[i]
                slot = i % RING
                pe.wait_ge(core.panel_loaded[slot].sem, core.panel_loaded[slot].at(16 * (i // RING + 1)))
                if panel != name:
                    side(pe, j, core.ring[:, slot, :]).then_inc(core.panel_used.sem, 1)
                    continue
                for c in range(2):
                    t = 2 * j + c
                    if k0 == 0 and t >= BANKS:
                        wait_tile(pe, t - BANKS)
                    for k in range(kn):
                        mm = pe.matmul(core.ps[:, t % BANKS, 0:TOK],
                                       core.ring[:, slot, k * PANEL + c * P:k * PANEL + c * P + P],
                                       src(k0 + k), start=(k0 + k == 0), stop=(k0 + k == kt - 1))
                mm.then_inc(core.panel_used.sem, 1)

        def evacuations(eng, which):
            link = core.link(which, eng)
            for i, (e, take, after) in enumerate(tiles):
                if e != which:
                    continue
                eng.wait_ge(core.panel_used.sem, core.panel_used.at(last_panel[i // 2] + 1))
                take(eng, core.ps[:, i % BANKS, 0:TOK]).then_inc(evac[which].sem, 1)
                if after is not None:
                    after(eng, link, wait_tile)

        @block.scalar
        def _(act):
            if act_work is not None:
                act_work(act)
            evacuations(act, "act")

        @block.vector
        def _(dve):
            if head is not None:
                head(dve, core.link("dve", dve))
            evacuations(dve, "dve")

        @block.gpsimd
        def _(pool):
            if pool_work is not None:
                pool_work(pool)
    core.used = mine[-1] + 1
    core.act_evac.close(counts["act"])
    core.dve_evac.close(counts["dve"])


def bcast(ap, shape):
    return ap.to_broadcast(shape)


def column_sums(core, jobs):
    with core.block() as block:
        @block.tensor
        def _(pe):
            for out, mat, srcs in jobs:
                for n, s in enumerate(srcs):
                    pe.matmul(out, mat, s, start=(n == 0), stop=(n == len(srcs) - 1))


def rstd_of(core, ps, out, scale, eps):
    with core.block() as block:
        @block.vector
        def _(dve):
            dve.tensor_scalar(out, ps, scale, eps, ALU.mult, ALU.add)
    with core.block() as block:
        @block.scalar
        def _(act):
            act.activation(out, out, ACT.Sqrt)
    with core.block() as block:
        @block.vector
        def _(dve):
            dve.reciprocal(out, out)


def layer_norm(core, g, b, layer):
    x = core.x
    with ExitStack() as s:
        sq = s.enter_context(core.nc.sbuf_tensor(f"ln_sq_{g}{layer}", [P, DT, TOK], F32))
        rs = s.enter_context(core.nc.sbuf_tensor(f"ln_rs_{g}{layer}", [P, TOK], F32))
        column_sums(core, [(core.ps[:, 4, 0:TOK], core.m("ones"), [x[:, k, :] for k in range(DT)])])
        with core.block() as block:
            @block.vector
            def _(dve):
                for h in range(2):
                    part = x[:, 4 * h:4 * h + 4, :]
                    dve.scalar_tensor_tensor(out=part, in0=bcast(core.ps[:, 4:5, 0:TOK], [P, 4, TOK]), scalar=-1.0 / D,
                                             in1=part, op0=ALU.mult, op1=ALU.add).then_inc(core.sem_a.sem, 1)

            @block.scalar
            def _(act):
                for h in range(2):
                    act.wait_ge(core.sem_a.sem, core.sem_a.at(h + 1))
                    for k in range(4 * h, 4 * h + 4, 2):
                        act.activation(sq[:, k:k + 2, :], x[:, k:k + 2, :], ACT.Square).then_inc(core.sem_b.sem, 1)

            @block.tensor
            def _(pe):
                for k in range(DT):
                    pe.wait_ge(core.sem_b.sem, core.sem_b.at(k // 2 + 1))
                    pe.matmul(core.ps[:, 5, 0:TOK], core.m("ones"), sq[:, k, :], start=(k == 0), stop=(k == DT - 1))
        core.sem_a.close(2)
        core.sem_b.close(4)
        rstd_of(core, core.ps[:, 5, 0:TOK], rs[:, :], 1.0 / D, LN_EPS)
        with core.block() as block:
            @block.vector
            def _(dve):
                for k in range(DT):
                    dve.scalar_tensor_tensor(out=x[:, k, :], in0=x[:, k, :], scalar=core.v(g, layer * DT + k),
                                             in1=rs[:, :], op0=ALU.mult, op1=ALU.mult).then_inc(core.sem_a.sem, 1)

            @block.scalar
            def _(act):
                for k in range(DT):
                    act.wait_ge(core.sem_a.sem, core.sem_a.at(k + 1))
                    act.activation(x[:, k, :], x[:, k, :], ACT.Identity, bias=core.v(b, layer * DT + k))
        core.sem_a.close(DT)


def residual_tiles(core, scale):
    def take(m):
        return lambda eng, ps: eng.scalar_tensor_tensor(out=core.x[:, m, :], in0=core.x[:, m, :], scalar=scale, in1=ps,
                                                        op0=ALU.mult, op1=ALU.add)
    return [("dve", take(m), None) for m in range(DT)]


def copy_tiles(core, dst, eng="act", func=None, bias=None, scale=1.0):
    def take(m):
        if eng == "dve":
            return lambda e, ps: e.tensor_copy(dst(m), ps)
        if bias is None:
            return lambda e, ps: e.activation(dst(m), ps, func or ACT.Copy, scale=scale)
        return lambda e, ps: e.activation(dst(m), ps, func or ACT.Identity, bias=bias(m), scale=scale)
    return take


def ffn(core, layer):
    with ExitStack() as s:
        h = s.enter_context(core.nc.sbuf_tensor(f"ffn_h{layer}", [P, FF_T, TOK], F32))
        tiles = []
        for j in range(FF_T):
            def gate(e, ps, j=j):
                return e.activation(h[:, j, :], ps, ACT.Silu)

            def up(e, ps, j=j):
                e.wait_ge(core.act_evac.sem, core.act_evac.at(j + 1))
                return e.tensor_tensor(h[:, j, :], h[:, j, :], ps, ALU.mult)
            tiles += [("act", gate, None), ("dve", up, None)]
        name, out, bias = (("ada2", core.mod2, "ada_b_2"), ("ada3", core.mod3, "b_ada_3"))[layer]
        linear(core, f"ffn_up{layer}", lambda k: core.x[:, k, :], tiles,
               side=modulation_side(core, layer, out.shape[-1] // 2))
        finish_modulation(core, name, out, core.vs(bias))
        linear(core, f"ffn_dn{layer}", lambda k: h[:, k, :], residual_tiles(core, ALPHA))
    layer_norm(core, "ln_ffn_g", "ln_ffn_b", layer)


def per_layer_embedding(core, layer):
    nc = core.nc
    with ExitStack() as s:
        gate = s.enter_context(nc.sbuf_tensor(f"ple_gate{layer}", [P, DT, TOK], F32))
        pt = s.enter_context(nc.sbuf_tensor(f"ple_p{layer}_sb", [P, 2, TOK], F32))
        take = copy_tiles(core, lambda m: gate[:, m, :], func=ACT.Sigmoid, bias=lambda m: core.v("b_ple", layer * DT + m))
        with core.block() as block:
            @block.scalar
            def _(act):
                act.dma_start(pt[:, :, :], core.a["p"][layer]).then_inc(core.const_loaded.sem, 16)
                act.wait_ge(core.const_loaded.sem, core.const_loaded.at(16))
        core.const_loaded.close(16)
        linear(core, f"ple_g{layer}", lambda k: core.x[:, k, :], [("act", take(m), None) for m in range(DT)])
        tiles = []
        for m in range(DT):
            def take(e, ps, m=m):
                return e.tensor_tensor(gate[:, m, :], gate[:, m, :], ps, ALU.mult)

            def after(e, link, wait_tile, m=m):
                wait_tile(e, m)
                link(e.tensor_tensor(core.x[:, m, :], core.x[:, m, :], gate[:, m, :], ALU.add))
            tiles.append(("dve", take, after))
        linear(core, f"ple_p{layer}", lambda k: pt[:, k, :], tiles)


def ssd_layer(core):
    nc, ps = core.nc, core.ps
    with ExitStack() as s:
        def sb(name, shape):
            return s.enter_context(nc.sbuf_tensor(name, shape, F32))
        y_sc = sb("y_sc", [P, DT, TOK])
        z = sb("z_gate", [P, DT, TOK])
        xbc = sb("xbc", [P, XBC_T, TOK])
        dt = sb("dt16", [16, TOK])
        acs = sb("acs16", [16, TOK])
        dte = sb("dte16", [16, SSD_CHUNK])
        with ExitStack() as s2:
            xbp = s2.enter_context(nc.sbuf_tensor("xbc_pad", [P, 2, TOK + 4], F32))
            scp = s2.enter_context(nc.sbuf_tensor("sc_pad", [P, DT, TOK + 4], F32))
            dtw = s2.enter_context(nc.sbuf_tensor("dt_w", [P, DT, 16], F32))
            acc = s2.enter_context(nc.sbuf_tensor("conv_acc", [P, TOK], F32))
            ab = s2.enter_context(nc.sbuf_tensor("dt_abs", [16, TOK], F32))
            with core.block() as block:
                @block.scalar
                def _(act):
                    act.dma_start(dtw[:, :, :], core.a["w_dt"]).then_inc(core.const_loaded.sem, 16)

                @block.vector
                def _(dve):
                    dve.memset(xbp[:, :, 0:4], 0.0)
                    dve.memset(scp[:, :, 0:4], 0.0)

                @block.tensor
                def _(pe):
                    pe.wait_ge(core.const_loaded.sem, core.const_loaded.at(16))
                    for k in range(DT):
                        pe.matmul(ps[0:16, 7, 0:TOK], dtw[:, k, :], core.x[:, k, :], start=(k == 0), stop=(k == DT - 1))
            core.const_loaded.close(16)

            tiles = []
            for t in range(XBC_T):
                def take(e, p_, t=t):
                    if t >= 2:
                        e.wait_ge(core.sem_c.sem, core.sem_c.at(t - 1))
                    return e.activation(xbp[:, t % 2, 4:4 + TOK], p_, ACT.Copy)
                tiles.append(("act", take, None))
            for t in range(DT):
                tiles.append(("act", copy_tiles(core, lambda m: scp[:, m, 4:4 + TOK])(t), None))
            for t in range(DT):
                def take(e, p_, t=t):
                    e.wait_ge(core.act_evac.sem, core.act_evac.at(XBC_T + t + 1))
                    return e.tensor_tensor(scp[:, t, 4:4 + TOK], scp[:, t, 4:4 + TOK], p_, ALU.mult)
                tiles.append(("dve", take, None))
            for t in range(DT):
                def take(e, p_, t=t):
                    return e.tensor_tensor(y_sc[:, t, :], y_sc[:, t, :], p_, ALU.mult)
                tiles.append(("dve", take, None))
            for t in range(DT):
                tiles.append(("act", copy_tiles(core, lambda m: z[:, m, :], func=ACT.Silu)(t), None))

            def conv(link, dve, dst, src, w, n, bias=None):
                if bias is None:
                    link(dve.tensor_scalar(dst, src[:, 4:4 + TOK], w(n - 1), None, ALU.mult))
                else:
                    link(dve.tensor_scalar(dst, src[:, 4:4 + TOK], w(n - 1), bias, ALU.mult, ALU.add))
                for i in range(n - 1):
                    lag = n - 1 - i
                    link(dve.scalar_tensor_tensor(out=dst, in0=src[:, 4 - lag:4 - lag + TOK], scalar=w(i), in1=dst,
                                                  op0=ALU.mult, op1=ALU.add))

            def conv_xbc(e, link, t):
                e.wait_ge(core.act_evac.sem, core.act_evac.at(t + 1))
                conv(link, e, xbc[:, t, :], xbp[:, t % 2, :], lambda i: core.v("conv_w", i * XBC_T + t), SSD_CONV,
                     core.v("conv_b", t))

            def conv_sc(e, link, wait_tile, t):
                wait_tile(e, XBC_T + DT + t)
                conv(link, e, y_sc[:, t, :], scp[:, t, :], lambda i: core.v("sc_w", i * DT + t), SC_CONV)
            for t in range(DT):
                i = XBC_T + DT + t
                e_, take_, _ = tiles[i]
                tiles[i] = (e_, take_, lambda e, link, wt, t=t: conv_sc(e, link, wt, t))

            def head(dve, link):
                for t in range(XBC_T):
                    conv_xbc(dve, link, t)
                    dve.sem_inc(core.sem_c.sem, 1)
            linear(core, "w_in", lambda k: core.x[:, k, :], tiles, head=head)
            core.sem_c.close(XBC_T)
            with core.block() as block:
                @block.scalar
                def _(act):
                    link = core.link("act", act)
                    link(act.activation(xbc[:, :, :], xbc[:, :, :], ACT.Silu))
                    link(act.activation(dt[:, :], ps[0:16, 7, 0:TOK], ACT.Identity, bias=core.v("dt_bias", 0, 16)))
                    link(act.activation(ab[:, :], dt[:, :], ACT.Abs))
                    link(act.activation(ab[:, :], ab[:, :], ACT.Exp, scale=-1.0))
                    link(act.activation(ab[:, :], ab[:, :], ACT.Ln, bias=1.0))
                    link(act.activation(acc[0:16, 0:1], core.v("a_log", 0, 16), ACT.Exp))
            with core.block() as block:
                @block.vector
                def _(dve):
                    link = core.link("dve", dve)
                    link(dve.scalar_tensor_tensor(out=dt[:, :], in0=dt[:, :], scalar=0.0, in1=ab[:, :], op0=ALU.max,
                                                  op1=ALU.add))
                    link(dve.tensor_scalar(ab[:, :], dt[:, :], acc[0:16, 0:1], -1.0, ALU.mult, ALU.mult))
                    for c in range(NB):
                        link(dve.tensor_tensor_scan(acs[:, c * P:c * P + P], core.m("ones")[0:16, :],
                                                    ab[:, c * P:c * P + P], 0.0, ALU.mult, ALU.add))
            with core.block() as block:
                @block.scalar
                def _(act):
                    act.activation(dte[:, :], acs[:, 0:P], ACT.Exp, scale=-1.0, bias=acs[:, P - 1:P])
        xdt = sb("xdt", [P, NB, SSD_HEADS, HD])
        xde = sb("xde", [P, SSD_HEADS, HD])
        cols = sb("ssd_cols", [P, 5, 16])
        btok = sb("btok", [P, SSD_GROUPS, P])
        cbm = sb("cbm", [P, SSD_GROUPS * NB, P])
        hst = sb("h_state", [P, SSD_GROUPS, HPG * HD])
        ident = core.m("ident")
        with core.block() as block:
            @block.tensor
            def _(pe):
                for n, src in enumerate([dt[:, 0:P], dt[:, P:2 * P], acs[:, 0:P], acs[:, P:2 * P], dte[:, :]]):
                    pe.transpose(ps[:, 6, 16 * n:16 * n + 16], src, ident[0:16, 0:16])
                for g in range(SSD_GROUPS):
                    pe.transpose(ps[:, 7, g * P:g * P + P], xbc[:, 8 + g, 0:P], ident)
                for c in range(NB):
                    for t in range(DT):
                        n = c * DT + t
                        pe.transpose(ps[:, n // 4, (n % 4) * P:(n % 4) * P + P], xbc[:, t, c * P:c * P + P], ident)
                for g in range(SSD_GROUPS):
                    for c in range(NB):
                        n = g * NB + c
                        pe.matmul(ps[:, 5, n * P:n * P + P], xbc[:, 8 + g, c * P:c * P + P],
                                  xbc[:, 10 + g, c * P:c * P + P], start=True, stop=True)
        with core.block() as block:
            @block.vector
            def _(dve):
                link = core.link("dve", dve)
                link(dve.tensor_copy(cols[:, :, :], ps[:, 6, 0:80].rearrange("p (a b) -> p a b", b=16)))
                for c in range(NB):
                    for q in range(2):
                        link(dve.tensor_tensor(xdt[:, c, 8 * q:8 * q + 8, :],
                                               ps[:, 2 * c + q, :].rearrange("p (h d) -> p h d", d=HD),
                                               bcast(cols[:, c, 8 * q:8 * q + 8].unsqueeze(2), [P, 8, HD]), ALU.mult))
                link(dve.tensor_tensor(xde[:, :, :], xdt[:, 0, :, :],
                                       bcast(cols[:, 4, :].unsqueeze(2), [P, SSD_HEADS, HD]), ALU.mult))
                link(dve.tensor_tensor(cbm[:, :, :], ps[:, 5, :].rearrange("p (a b) -> p a b", b=P),
                                       bcast(core.m("tri_le").unsqueeze(1), [P, 4, P]), ALU.mult))

            @block.scalar
            def _(act):
                act.activation(btok[:, :, :], ps[:, 7, 0:2 * P].rearrange("p (a b) -> p a b", b=P), ACT.Copy)
        with core.block() as block:
            @block.tensor
            def _(pe):
                for g in range(SSD_GROUPS):
                    pe.matmul(ps[:, g, :], btok[:, g, :], xde[:, g * HPG:g * HPG + HPG, :], start=True, stop=True)
        with core.block() as block:
            @block.vector
            def _(dve):
                dve.tensor_copy(hst[:, :, :], ps[:, 0:2, :])
        seg = sb("seg", [P, 2, TOK])
        ex = sb("seg_exp", [P, 2, TOK + P])
        wl = sb("w_local", [P, 2, TOK + P])
        bc_ready, seg_ready, exp_ready, w_ready, y_ready = core.sem_a, core.sem_b, core.sem_c, core.sem_d, core.sem_e
        y_taken, xd = core.sem_f, xbc
        with core.block() as block:
            @block.tensor
            def _(pe):
                def spread(h):
                    if h >= 2:
                        pe.wait_ge(seg_ready.sem, seg_ready.at(h - 1))
                        pe.wait_ge(exp_ready.sem, exp_ready.at(h - 1))
                    pe.matmul(ps[:, h % 2, 0:TOK], bcast(ident[0:16, h:h + 1], [16, P]), acs[:, :], start=True,
                              stop=True).then_inc(bc_ready.sem, 1)
                spread(0)
                for h in range(SSD_HEADS):
                    if h + 1 < SSD_HEADS:
                        spread(h + 1)
                    pe.wait_ge(w_ready.sem, w_ready.at(h + 1))
                    j, o = h // 2, HD * (h % 2)
                    if h % 2 == 0 and j >= 2:
                        pe.wait_ge(y_taken.sem, y_taken.at(j - 1))
                    out = ps[o:o + HD, 2 + j % 2, :]
                    w = wl[:, h % 2, :]
                    pe.matmul(out[:, 0:P], xdt[:, 0, h, :], w[:, 0:P], start=True, stop=True)
                    pe.matmul(out[:, P:TOK], xdt[:, 1, h, :], w[:, P:TOK], start=True, stop=False)
                    pe.matmul(out[:, P:TOK], hst[:, h // HPG, (h % HPG) * HD:(h % HPG) * HD + HD], w[:, TOK:TOK + P],
                              start=False, stop=True).then_inc(y_ready.sem, 1)

            @block.vector
            def _(dve):
                link = core.link("dve", dve)

                def y_out(j):
                    dve.wait_ge(y_ready.sem, y_ready.at(2 * j + 2))
                    link(dve.scalar_tensor_tensor(out=xd[:, j, :], in0=xd[:, j, :], scalar=core.v("ssd_d", j),
                                                  in1=ps[:, 2 + j % 2, 0:TOK], op0=ALU.mult, op1=ALU.add))
                    dve.sem_inc(y_taken.sem, 1)
                    link(dve.tensor_tensor(xd[:, j, :], xd[:, j, :], z[:, j, :], ALU.mult))
                for h in range(SSD_HEADS):
                    dve.wait_ge(bc_ready.sem, bc_ready.at(h + 1))
                    if h >= 2:
                        dve.wait_ge(exp_ready.sem, exp_ready.at(h - 1))
                    for c in range(NB):
                        ins = dve.tensor_scalar(seg[:, h % 2, c * P:c * P + P], ps[:, h % 2, c * P:c * P + P],
                                                cols[:, 2 + c, h:h + 1], 0.0, ALU.subtract, ALU.min)
                    ins.then_inc(seg_ready.sem, 1)
                    if h >= 3 and h % 2 == 1:
                        y_out((h - 3) // 2)
                y_out(SSD_HEADS // 2 - 1)

            @block.scalar
            def _(act):
                for h in range(SSD_HEADS):
                    act.wait_ge(seg_ready.sem, seg_ready.at(h + 1))
                    if h >= 2:
                        act.wait_ge(w_ready.sem, w_ready.at(h - 1))
                    act.activation(ex[:, h % 2, 0:TOK], seg[:, h % 2, :], ACT.Exp)
                    act.activation(ex[:, h % 2, TOK:TOK + P], ps[:, h % 2, P:TOK], ACT.Exp).then_inc(exp_ready.sem, 1)

            @block.gpsimd
            def _(pool):
                for h in range(SSD_HEADS):
                    g = h // HPG
                    pool.wait_ge(exp_ready.sem, exp_ready.at(h + 1))
                    if h >= 2:
                        pool.wait_ge(y_ready.sem, y_ready.at(h - 1))
                    pool.tensor_tensor(wl[:, h % 2, 0:TOK], ex[:, h % 2, 0:TOK],
                                       cbm[:, g * NB:g * NB + NB, :].rearrange("p a b -> p (a b)"), ALU.mult)
                    pool.tensor_tensor(wl[:, h % 2, TOK:TOK + P], ex[:, h % 2, TOK:TOK + P],
                                       xbc[:, 10 + g, P:TOK], ALU.mult).then_inc(w_ready.sem, 1)
        for sig in (bc_ready, seg_ready, exp_ready, w_ready, y_ready):
            sig.close(SSD_HEADS)
        y_taken.close(SSD_HEADS // 2)
        with core.block() as block:
            @block.scalar
            def _(act):
                act.activation(z[:, :, :], xd[:, 0:DT, :], ACT.Square)
        column_sums(core, [(ps[:, 4 + g, 0:TOK], core.m("ones"), [z[:, 4 * g + k, :] for k in range(4)])
                           for g in range(SSD_GROUPS)])
        rstd = seg[:, :, :]
        rstd_of(core, ps[:, 4:6, 0:TOK], rstd, 1.0 / (SSD_HEADS * HD // SSD_GROUPS), 1e-5)
        with core.block() as block:
            @block.vector
            def _(dve):
                for t in range(DT):
                    dve.scalar_tensor_tensor(out=xd[:, t, :], in0=xd[:, t, :], scalar=core.v("ssd_norm", t),
                                             in1=rstd[:, t // 4, :], op0=ALU.mult, op1=ALU.mult)
        linear(core, "w_out", lambda k: xd[:, k, :] if k < DT else y_sc[:, k - DT, :], residual_tiles(core, ALPHA))
    layer_norm(core, "ln_mix_g", "ln_mix_b", 0)


def to_token_major(core, srcs, dst):
    ps, ident = core.ps, core.m("ident")
    jobs = [(t, b) for t in range(len(srcs)) for b in range(NB)]
    for first in range(0, len(jobs), 16):
        part = jobs[first:first + 16]
        with core.block() as block:
            @block.tensor
            def _(pe):
                for n, (t, b) in enumerate(part):
                    pe.transpose(ps[:, n // 4, (n % 4) * P:(n % 4) * P + P], srcs[t][:, b * P:b * P + P],
                                 ident).then_inc(core.sem_a.sem, 1)

            @block.scalar
            def _(act):
                for n, (t, b) in enumerate(part):
                    if n // 4 % 2 == 0:
                        act.wait_ge(core.sem_a.sem, core.sem_a.at(min(len(part), n // 4 * 4 + 4)))
                        act.activation(dst(t, b), ps[:, n // 4, (n % 4) * P:(n % 4) * P + P], ACT.Copy)

            @block.vector
            def _(dve):
                for n, (t, b) in enumerate(part):
                    if n // 4 % 2 == 1:
                        dve.wait_ge(core.sem_a.sem, core.sem_a.at(min(len(part), n // 4 * 4 + 4)))
                        dve.tensor_copy(dst(t, b), ps[:, n // 4, (n % 4) * P:(n % 4) * P + P])
        core.sem_a.close(len(part))


def softmax_attention(core, name, heads, q, k, v, mask, scale, take, sinks=None):
    nc, ps, ident = core.nc, core.ps, core.m("ident")
    scored, shifted, exped, normed, turned, copied, summed = (
        core.sem_a, core.sem_b, core.sem_c, core.sem_d, core.sem_e, core.sem_f, core.sem_g)
    H, W = len(heads), 3 * P
    with ExitStack() as s:
        prob = s.enter_context(nc.sbuf_tensor(f"{name}_prob", [P, 3, W], F32))
        pt = s.enter_context(nc.sbuf_tensor(f"{name}_pt", [P, 2, W], F32))
        st = s.enter_context(nc.sbuf_tensor(f"{name}_st", [P, 3, 8], F32))
        spans, score_bank = [(0, P), (P, W)], (0, 1, 6)

        with core.block() as block:
            @block.tensor
            def _(pe):
                def scores(i):
                    if i >= 3:
                        pe.wait_ge(shifted.sem, shifted.at(i - 2))
                    h = heads[i]
                    pe.matmul(ps[:, score_bank[i % 3], 0:P], q(h)[:, 0:P], k(h)[:, 0:P], start=True, stop=True)
                    pe.matmul(ps[:, score_bank[i % 3], P:W], q(h)[:, P:TOK], k(h), start=True,
                              stop=True).then_inc(scored.sem, 1)

                def turn(i):
                    pe.wait_ge(normed.sem, normed.at(i + 1))
                    if i >= 2:
                        pe.wait_ge(copied.sem, copied.at(i - 1))
                    for n in range(3):
                        t = pe.transpose(ps[:, 2 + i % 2, n * P:n * P + P], prob[:, i % 3, n * P:n * P + P], ident)
                    t.then_inc(turned.sem, 1)

                def weigh(i):
                    pe.wait_ge(copied.sem, copied.at(i + 1))
                    if i % 2 == 0 and i >= 4:
                        pe.wait_ge(core.dve_evac.sem, core.dve_evac.at(i // 2 - 1))
                    o = HD * (i % 2)
                    out = ps[o:o + HD, 4 + i // 2 % 2, :]
                    p = pt[:, i % 2, :]
                    pe.matmul(out[:, 0:P], v(heads[i], 0), p[:, 0:P], start=True, stop=True)
                    pe.matmul(out[:, P:TOK], v(heads[i], 0), p[:, P:2 * P], start=True, stop=False)
                    pe.matmul(out[:, P:TOK], v(heads[i], 1), p[:, 2 * P:W], start=False, stop=True).then_inc(summed.sem, 1)
                for i in range(3):
                    scores(i)
                for i in range(H + 1):
                    if i < H:
                        turn(i)
                    if i + 3 < H:
                        scores(i + 3)
                    if i >= 1:
                        weigh(i - 1)

            @block.vector
            def _(dve):
                link = core.link("dve", dve)

                def shift(i):
                    pr, t = prob[:, i % 3, :], st[:, i % 3, :]
                    dve.wait_ge(scored.sem, scored.at(i + 1))
                    if i >= 3:
                        dve.wait_ge(turned.sem, turned.at(i - 2))
                    link(dve.scalar_tensor_tensor(out=pr, in0=ps[:, score_bank[i % 3], 0:W], scalar=scale, in1=core.m(mask, 0, W),
                                                  op0=ALU.mult, op1=ALU.add))
                    for b, (lo, hi) in enumerate(spans):
                        link(dve.tensor_reduce(t[:, b:b + 1], pr[:, lo:hi], AX, ALU.max))
                    if sinks is None:
                        ins = dve.tensor_scalar(t[:, 2:4], t[:, 0:2], -1.0, None, ALU.mult)
                    else:
                        ins = dve.tensor_scalar(t[:, 2:4], t[:, 0:2], sinks(heads[i]), -1.0, ALU.max, ALU.mult)
                    ins.then_inc(shifted.sem, 1)

                def normalise(i):
                    pr, t = prob[:, i % 3, :], st[:, i % 3, :]
                    dve.wait_ge(exped.sem, exped.at(i + 1))
                    if sinks is not None:
                        link(dve.tensor_tensor(t[:, 4:6], t[:, 4:6], t[:, 6:8], ALU.add))
                    link(dve.reciprocal(t[:, 4:6], t[:, 4:6]))
                    for b, (lo, hi) in enumerate(spans):
                        ins = dve.tensor_scalar(pr[:, lo:hi], pr[:, lo:hi], t[:, 4 + b:5 + b], None, ALU.mult)
                    ins.then_inc(normed.sem, 1)

                def store(j):
                    dve.wait_ge(summed.sem, summed.at(2 * j + 2))
                    take(dve, j, ps[:, 4 + j % 2, 0:TOK]).then_inc(core.dve_evac.sem, 1)
                for i in range(H + 3):
                    if i < H:
                        shift(i)
                    if 1 <= i <= H:
                        normalise(i - 1)
                    if i >= 4 and i % 2 == 0:
                        store((i - 4) // 2)

            @block.scalar
            def _(act):
                def exponentials(i):
                    pr, t = prob[:, i % 3, :], st[:, i % 3, :]
                    act.wait_ge(shifted.sem, shifted.at(i + 1))
                    for b, (lo, hi) in enumerate(spans):
                        ins = act.activation(pr[:, lo:hi], pr[:, lo:hi], ACT.Exp, bias=t[:, 2 + b:3 + b],
                                             accum_out=t[:, 4 + b:5 + b])
                    if sinks is not None:
                        ins = act.activation(t[:, 6:8], t[:, 2:4], ACT.Exp, bias=sinks(heads[i]))
                    ins.then_inc(exped.sem, 1)

                def copy(i):
                    act.wait_ge(turned.sem, turned.at(i + 1))
                    if i >= 2:
                        act.wait_ge(summed.sem, summed.at(i - 1))
                    act.activation(pt[:, i % 2, :], ps[:, 2 + i % 2, 0:W], ACT.Copy).then_inc(copied.sem, 1)
                for i in range(H + 1):
                    if i < H:
                        exponentials(i)
                    if i >= 1:
                        copy(i - 1)
        for sig in (scored, shifted, exped, normed, turned, copied, summed):
            sig.close(H)
        core.dve_evac.close(H // 2)


def attention_layer(core):
    nc = core.nc
    with ExitStack() as s:
        qkv = s.enter_context(nc.sbuf_tensor("swa_qkv", [P, 12, TOK], F32))
        vt = s.enter_context(nc.sbuf_tensor("swa_v", [P, NB, 2 * P], F32))
        o = s.enter_context(nc.sbuf_tensor("swa_o", [P, DT, TOK], F32))
        take = copy_tiles(core, lambda m: qkv[:, m, :], bias=lambda m: core.v("b_qkv", m))
        linear(core, "qkv", lambda k: core.x[:, k, :], [("act", take(m), None) for m in range(12)])
        to_token_major(core, [qkv[:, 10 + t, :] for t in range(2)], lambda t, b: vt[:, b, t * P:t * P + P])

        def kv_of(u):
            return 2 * (u // 2 // 4) + u % 2

        def half(u):
            return slice(HD * (u % 2), HD * (u % 2) + HD)

        def sink(u):
            return core.v("sinks", 8 * (u // 8) + 4 * (u % 2) + u // 2 % 4)
        softmax_attention(core, "swa", range(16), lambda u: qkv[half(u), u // 2, :],
                          lambda u: qkv[half(u), 8 + u // 8, :],
                          lambda u, b: vt[:, b, HD * kv_of(u):HD * kv_of(u) + HD], "band", HD ** -0.5,
                          lambda e, j, p: e.tensor_copy(o[:, j, :], p), sink)
        tiles = []
        for m in range(DT):
            def take(e, p, m=m):
                return e.scalar_tensor_tensor(out=o2[:, m, :], in0=core.x[:, m, :], scalar=ALPHA, in1=p, op0=ALU.mult, op1=ALU.add)

            def after(e, link, wait_tile, m=m):
                wait_tile(e, m)
                link(e.tensor_scalar(core.x[:, m, :], o2[:, m, :], core.v("b_o", m), None, ALU.add))
            tiles.append(("dve", take, after))
        o2 = qkv
        linear(core, "w_o", lambda k: o[:, k, :], tiles)
    layer_norm(core, "ln_mix_g", "ln_mix_b", 1)


def start_modulation(core, s):
    core.cond = s.enter_context(core.nc.sbuf_tensor("cond", [P, 2, DT, 63], F32))
    with core.block() as block:
        @block.vector
        def _(dve):
            dve.memset(core.cond[:, :, :, :], 0.0)
    with core.block() as block:
        @block.scalar
        def _(act):
            for i, c in enumerate(("c_2", "c_3")):
                act.activation(core.cond[:, i, :, 31], core.vs(c), ACT.Silu)


def modulation_side(core, which, count):
    def side(pe, j, w):
        for k in range(DT):
            t = k % 4
            mm = pe.matmul(core.ps[32 * t:32 * t + 32, 7, 0:PANEL], core.cond[:, which, k, 31 - j:63 - j],
                           w[:, k * PANEL:k * PANEL + PANEL], start=(j == 0 and k < 4), stop=(j == count - 1 and k >= 4))
        return mm
    return side


def finish_modulation(core, name, out, bias):
    ps, n = core.ps, out.shape[-1] // 2
    with ExitStack() as s:
        rows = s.enter_context(core.nc.sbuf_tensor(f"{name}_rows", [P, PANEL], F32))
        with core.block() as block:
            @block.vector
            def _(dve):
                dve.tensor_copy(rows[:, :], ps[:, 7, 0:PANEL])
        with core.block() as block:
            @block.tensor
            def _(pe):
                for c in range(2):
                    pe.matmul(ps[:, 6, c * 32:c * 32 + 32], rows[:, c * P:c * P + P], core.m("fold"), start=True, stop=True)
        with core.block() as block:
            @block.vector
            def _(dve):
                for c in range(2):
                    dve.tensor_tensor(out[:, c::2], ps[:, 6, c * 32:c * 32 + n], bias[:, c::2], ALU.add)


def rms_modulate(core, name, out, g, scale, shift):
    x = core.x
    with ExitStack() as s:
        rs = s.enter_context(core.nc.sbuf_tensor(f"{name}_rs", [P, TOK], F32))
        gs = s.enter_context(core.nc.sbuf_tensor(f"{name}_gs", [P, DT], F32))
        with core.block() as block:
            @block.scalar
            def _(act):
                for k in range(DT):
                    act.activation(out[:, k, :], x[:, k, :], ACT.Square).then_inc(core.sem_a.sem, 1)

            @block.tensor
            def _(pe):
                for k in range(DT):
                    pe.wait_ge(core.sem_a.sem, core.sem_a.at(k + 1))
                    pe.matmul(core.ps[:, 4, 0:TOK], core.m("ones"), out[:, k, :], start=(k == 0), stop=(k == DT - 1))

            @block.vector
            def _(dve):
                dve.scalar_tensor_tensor(out=gs[:, :], in0=scale, scalar=1.0, in1=g, op0=ALU.add, op1=ALU.mult)
        core.sem_a.close(DT)
        rstd_of(core, core.ps[:, 4, 0:TOK], rs[:, :], 1.0 / D, RMS_EPS)
        with core.block() as block:
            @block.vector
            def _(dve):
                for k in range(DT):
                    dve.scalar_tensor_tensor(out=out[:, k, :], in0=x[:, k, :], scalar=gs[:, k:k + 1], in1=rs[:, :],
                                             op0=ALU.mult, op1=ALU.mult).then_inc(core.sem_a.sem, 1)

            @block.scalar
            def _(act):
                for k in range(DT):
                    act.wait_ge(core.sem_a.sem, core.sem_a.at(k + 1))
                    act.activation(out[:, k, :], out[:, k, :], ACT.Identity, bias=shift[:, k:k + 1])
        core.sem_a.close(DT)


def head_sums(core, bank, src, tiles):
    column_sums(core, [(core.ps[:, bank + t // 2, (t % 2) * TOK:(t % 2) * TOK + TOK], core.m("head_ones"), [src[:, t, :]])
                       for t in range(tiles)])
    return core.ps[:, bank:bank + (tiles + 1) // 2, :].rearrange("p a (b n) -> p (a b) n", n=TOK)


def stick_breaking(core, q, k, v, o):
    nc, ps = core.nc, core.ps
    H, W = 8, 3 * P
    scale = HD ** -0.5
    with ExitStack() as s:
        def sb(name, shape):
            return s.enter_context(nc.sbuf_tensor("stick_" + name, shape, F32))
        sq, vt = sb("sq", [P, 8, TOK]), sb("vt", [P, NB, 4 * P])
        for half, (t, g) in enumerate(((q, "q_norm"), (k, "k_norm"))):
            part = sq[:, 4 * half:4 * half + 4, :]
            with core.block() as block:
                @block.scalar
                def _(act):
                    act.activation(part, t, ACT.Square)
            sums = head_sums(core, 2 * half, part, 4)
            rstd_of(core, sums, part, 1.0 / HD, RMS_EPS)
            with core.block() as block:
                @block.vector
                def _(dve):
                    dve.scalar_tensor_tensor(out=t, in0=t, scalar=core.v(g), in1=part, op0=ALU.mult, op1=ALU.mult)
        to_token_major(core, [v[:, t, :] for t in range(4)], lambda t, b: vt[:, b, t * P:t * P + P])
        lg, ln, lk = sb("logit", [P, H, W]), sb("log", [P, H, W]), sb("keep", [P, H, W])
        mask = sb("mask", [P, W])
        scored, logged, kept, masked, between, weight, exped, final = (
            core.sem_a, core.sem_b, core.sem_c, core.sem_d, core.sem_e, core.sem_f, core.sem_g, core.sem_h)
        done, scaled = core.act_evac, core.chain["pe"]
        score_bank = (0, 1, 6, 7)
        with core.block() as block:
            @block.vector
            def _(dve):
                dve.tensor_copy(mask[:, 0:P], core.m("tri_lt"))
                dve.tensor_copy(mask[:, P:2 * P], core.m("ones"))
                dve.tensor_copy(mask[:, 2 * P:W], core.m("tri_lt"))
        with core.block() as block:
            def rows_of(h):
                return slice(HD * (h % 2), HD * (h % 2) + HD)

            @block.tensor
            def _(pe):
                def score(h):
                    if h >= 4:
                        pe.wait_ge(scaled.sem, scaled.at(h - 3))
                    r, t = rows_of(h), h // 2
                    pe.matmul(ps[:, score_bank[h % 4], 0:TOK], k[r, t, 0:P], q[r, t, :], start=True, stop=True)
                    pe.matmul(ps[:, score_bank[h % 4], TOK:W], k[r, t, P:TOK], q[r, t, P:TOK], start=True,
                              stop=True).then_inc(scored.sem, 1)

                def suffix(h):
                    pe.wait_ge(masked.sem, masked.at(h + 1))
                    if h >= 2:
                        pe.wait_ge(weight.sem, weight.at(h - 1))
                    out = ps[:, 2 + h % 2, :]
                    pe.matmul(out[:, 0:TOK], core.m("tri_gt"), lk[:, h, 0:TOK], start=True, stop=False)
                    pe.matmul(out[:, P:TOK], core.m("ones"), lk[:, h, TOK:W], start=False, stop=True)
                    pe.matmul(out[:, TOK:W], core.m("tri_gt"), lk[:, h, TOK:W], start=True, stop=True).then_inc(between.sem, 1)

                def weigh(h):
                    pe.wait_ge(final.sem, final.at(h + 1))
                    if h % 2 == 0 and h >= 4:
                        pe.wait_ge(core.dve_evac.sem, core.dve_evac.at(h // 2 - 1))
                    out = ps[HD * (h % 2):HD * (h % 2) + HD, 4 + h // 2 % 2, :]
                    pe.matmul(out[:, 0:TOK], vt[:, 0, HD * h:HD * h + HD], ln[:, h, 0:TOK], start=True, stop=False)
                    pe.matmul(out[:, P:TOK], vt[:, 1, HD * h:HD * h + HD], ln[:, h, TOK:W], start=False,
                              stop=True).then_inc(done.sem, 1)
                for h in range(H):
                    score(h)
                for h in range(H):
                    suffix(h)
                for h in range(H):
                    weigh(h)

            @block.scalar
            def _(act):
                for h in range(H):
                    act.wait_ge(scored.sem, scored.at(h + 1))
                    act.activation(lg[:, h, :], ps[:, score_bank[h % 4], 0:W], ACT.Copy, scale=scale).then_inc(scaled.sem, 1)
                for h in range(H):
                    act.wait_ge(logged.sem, logged.at(h + 1))
                    act.activation(ln[:, h, :], ln[:, h, :], ACT.Exp).then_inc(core.chain["act"].sem, 1)
                for h in range(H):
                    act.wait_ge(core.chain["act"].sem, core.chain["act"].at(h + 1))
                    act.activation(ln[:, h, :], ln[:, h, :], ACT.Ln, bias=1.0).then_inc(kept.sem, 1)
                for h in range(H):
                    act.wait_ge(weight.sem, weight.at(h + 1))
                    act.activation(ln[:, h, :], ln[:, h, :], ACT.Exp).then_inc(exped.sem, 1)

            @block.vector
            def _(dve):
                link = core.link("dve", dve)
                for h in range(H):
                    dve.wait_ge(scaled.sem, scaled.at(h + 1))
                    dve.scalar_tensor_tensor(out=ln[:, h, :], in0=lg[:, h, :], scalar=-1.0, in1=lg[:, h, :], op0=ALU.mult,
                                             op1=ALU.min).then_inc(logged.sem, 1)

                def keep(h):
                    dve.wait_ge(kept.sem, kept.at(h + 1))
                    link(dve.scalar_tensor_tensor(out=ln[:, h, :], in0=lg[:, h, :], scalar=0.0, in1=ln[:, h, :],
                                                  op0=ALU.min, op1=ALU.subtract))
                    link(dve.tensor_tensor(lk[:, h, :], ln[:, h, :], lg[:, h, :], ALU.subtract))
                    dve.tensor_tensor(lk[:, h, :], lk[:, h, :], mask[:, :], ALU.mult).then_inc(masked.sem, 1)

                def exponent(h):
                    dve.wait_ge(between.sem, between.at(h + 1))
                    dve.tensor_tensor(ln[:, h, :], ln[:, h, :], ps[:, 2 + h % 2, 0:W], ALU.add).then_inc(weight.sem, 1)
                for i in range(H + 1):
                    if i < H:
                        keep(i)
                    if i >= 1:
                        exponent(i - 1)
                for j in range(H // 2):
                    dve.wait_ge(done.sem, done.at(2 * j + 2))
                    dve.tensor_copy(o[:, j, :], ps[:, 4 + j % 2, 0:TOK]).then_inc(core.dve_evac.sem, 1)

            @block.gpsimd
            def _(pool):
                for h in range(H):
                    pool.wait_ge(exped.sem, exped.at(h + 1))
                    pool.tensor_tensor(ln[:, h, :], ln[:, h, :], mask[:, :], ALU.mult).then_inc(final.sem, 1)
        for sig in (scored, logged, kept, masked, between, weight, exped, final, done, scaled, core.chain["act"]):
            sig.close(H)
        core.dve_evac.close(H // 2)
        part = sq[:, 0:4, :]
        with core.block() as block:
            @block.scalar
            def _(act):
                act.activation(part, o, ACT.Square)
        sums = head_sums(core, 0, part, 4)
        rstd_of(core, sums, part, 1.0 / HD, RMS_EPS)
        with core.block() as block:
            @block.vector
            def _(dve):
                for t in range(4):
                    dve.scalar_tensor_tensor(out=o[:, t, :], in0=o[:, t, :], scalar=core.v("sb_out", t),
                                             in1=part[:, t, :], op0=ALU.mult, op1=ALU.mult)


def rwkv_mix(core, z, lora, y):
    nc, ps = core.nc, core.ps
    T4, NC = 4, TOK // CHUNK
    with ExitStack() as s:
        def sb(name, shape):
            return s.enter_context(nc.sbuf_tensor("rwkv_" + name, shape, F32))
        r, k, v = z[:, 0:4, 1:], z[:, 4:8, 1:], z[:, 8:12, 1:]
        a, gate, bonus = (sb(n, [P, T4, TOK]) for n in ("a", "g", "bonus"))
        qq = sb("qq", [P, T4, 2, TOK])
        cm, fac = sb("mid", [P, T4, NC]), sb("fac", [P, T4, NC])
        vt, kt, btt = (sb(n, [P, NB, 4 * P]) for n in ("vt", "kt", "btt"))
        H = 8
        NP_ = H * NB
        mm_ = sb("mm", [P, NP_, 2, 2, P])
        early = s.enter_context(ExitStack())
        kk, lw, bt, en = (early.enter_context(nc.sbuf_tensor("rwkv_" + n, [P, T4, TOK], F32)) for n in ("kk", "lw", "b", "en"))
        with core.block() as block:
            @block.scalar
            def _(act):
                act.activation(z[0:HD, 12, 1:], z[0:HD, 12, 1:], ACT.Tanh)
                act.activation(z[:, 13, 1:], z[:, 13, 1:], ACT.Sigmoid)
        with core.block() as block:
            @block.tensor
            def _(pe):
                for t in range(T4):
                    c = slice((t % 2) * TOK, (t % 2) * TOK + TOK)
                    w = slice(t * P, t * P + P)
                    pe.matmul(ps[:, t // 2, c], lora[0:HD, w], z[0:HD, 12, 1:], start=True, stop=True)
                    pe.matmul(ps[:, 2 + t // 2, c], lora[HD:P, w], z[HD:P, 12, 1:], start=True, stop=True)
                    pe.matmul(ps[:, 4 + t // 2, c], lora[:, 512 + t * P:512 + t * P + P], z[:, 13, 1:], start=True,
                              stop=True)

            @block.vector
            def _(dve):
                link = core.link("dve", dve)
                for t in range(T4):
                    link(dve.tensor_scalar(kk[:, t, :], k[:, t, :], core.v("k_k", t), None, ALU.mult))
                link(dve.tensor_tensor(en[:, :, :], kk[:, :, :], kk[:, :, :], ALU.mult))
        with core.block() as block:
            @block.scalar
            def _(act):
                for t in range(T4):
                    c = slice((t % 2) * TOK, (t % 2) * TOK + TOK)
                    act.activation(lw[:, t, :], ps[:, t // 2, c], ACT.Sigmoid, bias=core.v("decay_w0", t))
                    act.activation(a[:, t, :], ps[:, 2 + t // 2, c], ACT.Sigmoid, bias=core.v("iclr_a0", t))
                    act.activation(gate[:, t, :], ps[:, 4 + t // 2, c], ACT.Copy)
        sums = head_sums(core, 6, en, T4)
        with core.block() as block:
            @block.scalar
            def _(act):
                act.activation(en[:, :, :], sums, ACT.Sqrt)

            @block.vector
            def _(dve):
                link = core.link("dve", dve)
                link(dve.tensor_scalar(lw[:, :, :], lw[:, :, :], -float(np.exp(-0.5)), None, ALU.mult))
                for t in range(T4):
                    link(dve.tensor_tensor_scan(bt[:, t, :], core.m("scan_keep", 0, TOK), lw[:, t, :], 0.0, ALU.mult, ALU.add))
                mid = bt[:, :, :].rearrange("p t (c n) -> p t c n", n=CHUNK)
                link(dve.tensor_copy(cm[:, :, :], mid[:, :, :, CHUNK // 2 - 1]))
                for t in range(T4):
                    link(dve.tensor_tensor(mid[:, t], mid[:, t], bcast(cm[:, t, :].unsqueeze(2), [P, NC, CHUNK]), ALU.subtract))
                link(dve.tensor_copy(fac[:, :, :], mid[:, :, :, CHUNK - 1]))
                link(dve.tensor_tensor(fac[:, :, 0:NC - 1], fac[:, :, 0:NC - 1], cm[:, :, 1:NC], ALU.add))
                link(dve.tensor_tensor(lw[:, :, :], bt[:, :, :], lw[:, :, :], ALU.subtract))
        with core.block() as block:
            @block.vector
            def _(dve):
                link = core.link("dve", dve)
                link(dve.tensor_scalar(en[:, :, :], en[:, :, :], 1e-12, None, ALU.max))
                link(dve.reciprocal(en[:, :, :], en[:, :, :]))
                link(dve.tensor_tensor(kk[:, :, :], kk[:, :, :], en[:, :, :], ALU.mult))
                for t in range(T4):
                    link(dve.tensor_scalar(en[:, t, :], a[:, t, :], 1.0, core.v("k_a", t), ALU.subtract, ALU.mult))
                    link(dve.scalar_tensor_tensor(out=k[:, t, :], in0=en[:, t, :], scalar=1.0, in1=k[:, t, :],
                                                  op0=ALU.add, op1=ALU.mult))
                    link(dve.scalar_tensor_tensor(out=bonus[:, t, :], in0=r[:, t, :], scalar=core.v("r_k", t),
                                                  in1=k[:, t, :], op0=ALU.mult, op1=ALU.mult))

            @block.scalar
            def _(act):
                act.activation(qq[:, :, 0, :], lw[:, :, :], ACT.Exp)
                act.activation(qq[:, :, 1, :], bt[:, :, :], ACT.Exp)
                act.activation(fac[:, :, :], fac[:, :, :], ACT.Exp)
        sums = head_sums(core, 6, bonus, T4)
        with core.block() as block:
            @block.scalar
            def _(act):
                act.activation(en[:, :, :], bt[:, :, :], ACT.Exp, scale=-1.0).then_inc(core.sem_a.sem, 1)

            @block.vector
            def _(dve):
                link = core.link("dve", dve)
                link(dve.tensor_tensor(bonus[:, :, :], v, sums, ALU.mult))
                link(dve.tensor_tensor(qq[:, :, 0, :], qq[:, :, 0, :], kk[:, :, :], ALU.mult))
                link(dve.tensor_tensor(qq[:, :, 1, :], qq[:, :, 1, :], r, ALU.mult))
                dve.wait_ge(core.sem_a.sem, core.sem_a.at(1))
                link(dve.tensor_tensor(bt[:, :, :], kk[:, :, :], a[:, :, :], ALU.mult))
                link(dve.tensor_tensor(bt[:, :, :], bt[:, :, :], en[:, :, :], ALU.mult))
                link(dve.tensor_tensor(k, k, en[:, :, :], ALU.mult))
        core.sem_a.close(1)
        for src, dst in ((v, vt), (k, kt), (bt, btt)):
            to_token_major(core, [src[:, t, :] for t in range(T4)], lambda t, b: dst[:, b, t * P:t * P + P])
        with core.block() as block:
            @block.tensor
            def _(pe):
                for n in range(NP_):
                    h, b = n // NB, n % NB
                    rr = slice(HD * (h % 2), HD * (h % 2) + HD)
                    if n >= 4:
                        pe.wait_ge(core.dve_evac.sem, core.dve_evac.at(n - 3))
                    for i, src in enumerate((k, bt)):
                        x = pe.matmul(ps[:, n % 4, i * TOK:i * TOK + TOK], src[rr, h // 2, b * P:b * P + P],
                                      qq[rr, h // 2, :, b * P:b * P + P], start=True, stop=True)
                    x.then_inc(core.sem_a.sem, 1)

            @block.vector
            def _(dve):
                both = core.m("lt64", 0, 2 * P)
                for n in range(NP_):
                    dve.wait_ge(core.sem_a.sem, core.sem_a.at(n + 1))
                    dve.tensor_tensor(mm_[:, n].rearrange("p i j t -> p i (j t)"),
                                      ps[:, n % 4, :].rearrange("p (i t) -> p i t", i=2),
                                      bcast(both.unsqueeze(1), [P, 2, 2 * P]), ALU.mult).then_inc(core.dve_evac.sem, 1)
        core.sem_a.close(NP_)
        core.dve_evac.close(NP_)
        early.close()
        tt, tn, xx, nl = (sb(n, [P, NP_, P]) for n in ("tt", "tn", "xx", "nl"))
        ident = core.m("ident")
        with core.block() as block:
            @block.vector
            def _(dve):
                for g in range(4):
                    gs = slice(4 * g, 4 * g + 4)
                    dve.tensor_tensor(nl[:, gs, :], mm_[:, gs, 1, 0, :], bcast(core.m("level", 0, P).unsqueeze(1), [P, 4, P]),
                                      ALU.mult).then_inc(core.sem_a.sem, 1)
                for g in range(4):
                    gs = slice(4 * g, 4 * g + 4)
                    dve.wait_ge(core.sem_a.sem, core.sem_a.at(g + 1))
                    dve.tensor_tensor(tt[:, gs, :], bcast(ident.unsqueeze(1), [P, 4, P]), nl[:, gs, :], ALU.subtract)
                    dve.wait_ge(core.sem_b.sem, core.sem_b.at(g + 1))
                    dve.tensor_tensor(tn[:, gs, :], bcast(ident.unsqueeze(1), [P, 4, P]),
                                      ps[:, g, :].rearrange("p (i t) -> p i t", t=P), ALU.subtract)

            @block.tensor
            def _(pe):
                for n in range(NP_):
                    pe.wait_ge(core.sem_a.sem, core.sem_a.at(n // 4 + 1))
                    x = pe.transpose(ps[:, n // 4, n % 4 * P:n % 4 * P + P], nl[:, n, :], ident)
                    if n % 4 == 3:
                        x.then_inc(core.sem_b.sem, 1)
        core.sem_a.close(4)
        core.sem_b.close(4)
        for lev in range(1, 6):
            last = lev == 5
            with core.block() as block:
                @block.gpsimd
                def _(pool):
                    for g in range(4):
                        gs = slice(4 * g, 4 * g + 4)
                        pool.tensor_tensor(nl[:, gs, :], mm_[:, gs, 1, 0, :],
                                           bcast(core.m("level", lev, P).unsqueeze(1), [P, 4, P]),
                                           ALU.mult).then_inc(core.sem_a.sem, 1)

                @block.tensor
                def _(pe):
                    for g in range(5):
                        if g < 4:
                            pe.wait_ge(core.sem_a.sem, core.sem_a.at(g + 1))
                            for i in range(4):
                                n = 4 * g + i
                                x = pe.matmul(ps[:, g, i * P:i * P + P], nl[:, n, :], tn[:, n, :], start=True, stop=True)
                            x.then_inc(core.sem_b.sem, 1)
                        if g >= 1:
                            g1 = g - 1
                            pe.wait_ge(core.sem_c.sem, core.sem_c.at(g1 + 1))
                            if g1 >= 2:
                                pe.wait_ge(core.sem_e.sem, core.sem_e.at(g1 - 1))
                            for i in range(4):
                                n = 4 * g1 + i
                                if not last:
                                    pe.matmul(ps[:, 4 + 2 * (g1 % 2), i * P:i * P + P], tt[:, n, :], xx[:, n, :],
                                              start=True, stop=True)
                                x = pe.matmul(ps[:, 5 + 2 * (g1 % 2), i * P:i * P + P], xx[:, n, :], tt[:, n, :],
                                              start=True, stop=True)
                            x.then_inc(core.sem_d.sem, 1)

                @block.scalar
                def _(act):
                    for g in range(4):
                        act.wait_ge(core.sem_b.sem, core.sem_b.at(g + 1))
                        act.activation(xx[:, 4 * g:4 * g + 4, :], ps[:, g, :].rearrange("p (i t) -> p i t", t=P),
                                       ACT.Copy).then_inc(core.sem_c.sem, 1)

                @block.vector
                def _(dve):
                    for g in range(4):
                        gs = slice(4 * g, 4 * g + 4)
                        dve.wait_ge(core.sem_d.sem, core.sem_d.at(g + 1))
                        if not last:
                            dve.tensor_tensor(tn[:, gs, :], tn[:, gs, :],
                                              ps[:, 4 + 2 * (g % 2), :].rearrange("p (i t) -> p i t", t=P), ALU.subtract)
                        dve.tensor_tensor(tt[:, gs, :], tt[:, gs, :],
                                          ps[:, 5 + 2 * (g % 2), :].rearrange("p (i t) -> p i t", t=P),
                                          ALU.subtract).then_inc(core.sem_e.sem, 1)
            for sig in (core.sem_a, core.sem_b, core.sem_c, core.sem_d, core.sem_e):
                sig.close(4)
        st = sb("state", [P, NC, T4, HD])
        rs, un = sb("rhs", [P, NB, 2, T4, HD]), sb("neg_u", [P, NB, 2, T4, HD])
        for c in range(NC):
            b, off = c // 2, HD * (c % 2)
            po = slice(off, off + HD)
            with core.block() as block:
                @block.tensor
                def _(pe):
                    for par in range(2):
                        rr = slice(HD * par, HD * par + HD)
                        for t in range(T4):
                            h = 2 * t + par
                            n = h * NB + b
                            out = ps[po, par, t * HD:t * HD + HD]
                            x = pe.matmul(out, mm_[:, n, 0, 0, po], vt[:, b, h * HD:h * HD + HD], start=True, stop=(c == 0))
                            if c > 0:
                                x = pe.matmul(out, qq[rr, t, 0, c * CHUNK:c * CHUNK + CHUNK], st[rr, c, t, :], start=False,
                                              stop=True)
                        x.then_inc(core.sem_a.sem, 1)
                    for par in range(2):
                        pe.wait_ge(core.sem_b.sem, core.sem_b.at(par + 1))
                        for t in range(T4):
                            h = 2 * t + par
                            x = pe.matmul(ps[po, 2 + par, t * HD:t * HD + HD], tt[po, h * NB + b, po], rs[po, b, par, t, :],
                                          start=True, stop=True)
                        x.then_inc(core.sem_c.sem, 1)
                    if c < NC - 1:
                        for par in range(2):
                            pe.wait_ge(core.sem_d.sem, core.sem_d.at(par + 1))
                            for t in range(T4):
                                h = 2 * t + par
                                hs = slice(h * HD, h * HD + HD)
                                out = ps[HD * par:HD * par + HD, 4, t * HD:t * HD + HD]
                                pe.matmul(out, kt[po, b, hs], vt[po, b, hs], start=True, stop=False)
                                x = pe.matmul(out, btt[po, b, hs], un[po, b, par, t, :], start=False, stop=True)
                        x.then_inc(core.sem_e.sem, 1)

                @block.vector
                def _(dve):
                    link = core.link("dve", dve)
                    for par in range(2):
                        dve.wait_ge(core.sem_a.sem, core.sem_a.at(par + 1))
                        dve.tensor_copy(rs[po, b, par], ps[po, par, 0:T4 * HD].rearrange("p (t v) -> p t v", v=HD)
                                        ).then_inc(core.sem_b.sem, 1)
                    if c < NC - 1:
                        dve.wait_ge(core.sem_e.sem, core.sem_e.at(1))
                        nxt = st[:, c + 1]
                        new = ps[:, 4, 0:T4 * HD].rearrange("p (t v) -> p t v", v=HD)
                        f = bcast(fac[:, :, c:c + 1], [P, T4, HD])
                        if c == 0:
                            link(dve.tensor_tensor(nxt, new, f, ALU.mult))
                        else:
                            link(dve.tensor_tensor(nxt, st[:, c], new, ALU.add))
                            link(dve.tensor_tensor(nxt, nxt, f, ALU.mult))

                @block.scalar
                def _(act):
                    for par in range(2):
                        act.wait_ge(core.sem_c.sem, core.sem_c.at(par + 1))
                        act.activation(un[po, b, par], ps[po, 2 + par, 0:T4 * HD].rearrange("p (t v) -> p t v", v=HD),
                                       ACT.Copy, scale=-1.0).then_inc(core.sem_d.sem, 1)
            for sig in (core.sem_a, core.sem_b, core.sem_c, core.sem_d):
                sig.close(2)
            if c < NC - 1:
                core.sem_e.close(1)
        with core.block() as block:
            @block.tensor
            def _(pe):
                for par in range(2):
                    rr = slice(HD * par, HD * par + HD)
                    for t in range(T4):
                        h = 2 * t + par
                        for b in range(NB):
                            n = h * NB + b
                            out = ps[rr, 2 * par + t // 2, (t % 2) * TOK + b * P:(t % 2) * TOK + b * P + P]
                            pe.matmul(out, vt[:, b, h * HD:h * HD + HD], mm_[:, n, 0, 1, :], start=True, stop=False)
                            pe.matmul(out, un[:, b, par, t, :], mm_[:, n, 1, 1, :], start=False, stop=False)
                            for c in (2 * b, 2 * b + 1):
                                if c > 0:
                                    half = out[:, (c % 2) * CHUNK:(c % 2) * CHUNK + CHUNK]
                                    pe.matmul(half, st[rr, c, t, :], qq[rr, t, 1, c * CHUNK:c * CHUNK + CHUNK],
                                              start=False, stop=(c % 2 == 1))
        with core.block() as block:
            @block.vector
            def _(dve):
                for par in range(2):
                    rr = slice(HD * par, HD * par + HD)
                    dve.tensor_copy(y[rr, :, :], ps[rr, 2 * par:2 * par + 2, :].rearrange("p a (b n) -> p (a b) n", n=TOK))
        sums = head_sums(core, 4, y, T4)
        with core.block() as block:
            @block.vector
            def _(dve):
                link = core.link("dve", dve)
                link(dve.scalar_tensor_tensor(out=y[:, :, :], in0=sums, scalar=-1.0 / HD, in1=y[:, :, :], op0=ALU.mult, op1=ALU.add))
                link(dve.tensor_tensor(a[:, :, :], y[:, :, :], y[:, :, :], ALU.mult))
        sums = head_sums(core, 6, a, T4)
        rstd_of(core, sums, a[:, :, :], 1.0 / HD, 1e-5 * HD)
        with core.block() as block:
            @block.vector
            def _(dve):
                link = core.link("dve", dve)
                link(dve.tensor_tensor(y[:, :, :], y[:, :, :], a[:, :, :], ALU.mult))
                for t in range(T4):
                    link(dve.tensor_scalar(y[:, t, :], y[:, t, :], core.v("lnx_w", t), core.v("lnx_b", t), ALU.mult, ALU.add))
                link(dve.tensor_tensor(y[:, :, :], y[:, :, :], bonus[:, :, :], ALU.add))
                link(dve.tensor_tensor(y[:, :, :], y[:, :, :], gate[:, :, :], ALU.mult))


def gated_residual(core, gate):
    def take(m):
        return lambda eng, ps: eng.scalar_tensor_tensor(out=core.x[:, m, :], in0=ps, scalar=gate[:, m:m + 1],
                                                        in1=core.x[:, m, :], op0=ALU.mult, op1=ALU.add)
    return [("dve", take(m), None) for m in range(DT)]


def second_block(core):
    nc = core.nc
    mod = core.mod2
    shift1, scale1, gate1, shift2, scale2, gate2 = (mod[:, 8 * i:8 * i + 8] for i in range(6))
    with ExitStack() as s:
        y = s.enter_context(nc.sbuf_tensor("mix2_y", [P, DT, TOK], F32))
        z = s.enter_context(nc.sbuf_tensor("mix2_z", [P, C_RWKV_T, TOK + 1], F32))
        lora = s.enter_context(nc.sbuf_tensor("lora_w", [P, 1024], F32))
        with ExitStack() as s2:
            qkv = s2.enter_context(nc.sbuf_tensor("stick_qkv", [P, 12, TOK], F32))
            with ExitStack() as s3:
                h = s3.enter_context(nc.sbuf_tensor("mix2_h", [P, DT, TOK], F32))
                tmp = s3.enter_context(nc.sbuf_tensor("shift_tmp", [P, TOK], F32))
                rms_modulate(core, "mix2", h, core.vs("norm1"), scale1, shift1)
                with core.block() as block:
                    @block.vector
                    def _(dve):
                        dve.memset(z[:, :, 0:1], 0.0)

                    @block.scalar
                    def _(act):
                        act.dma_start(lora[:, :], core.a["lora"]).then_inc(core.const_loaded.sem, 16)
                        act.wait_ge(core.const_loaded.sem, core.const_loaded.at(16))
                core.const_loaded.close(16)
                tiles = [("act", copy_tiles(core, lambda m: z[:, m, 1:])(m), None) for m in range(C_RWKV_T)]
                tiles += [("act", copy_tiles(core, lambda m: qkv[:, m - C_RWKV_T, :])(m), None)
                          for m in range(C_RWKV_T, 26)]

                def token_shift(dve, link):
                    for t in range(C_RWKV_T):
                        dve.wait_ge(core.act_evac.sem, core.act_evac.at(t + 1))
                        link(dve.tensor_tensor(tmp[:, :], z[:, t, 0:TOK], z[:, t, 1:], ALU.subtract))
                        link(dve.scalar_tensor_tensor(out=z[:, t, 1:], in0=tmp[:, :], scalar=core.v("mu", t),
                                                      in1=z[:, t, 1:], op0=ALU.mult, op1=ALU.add))
                linear(core, "w_in2", lambda k: h[:, k, :], tiles, head=token_shift)
            stick_breaking(core, qkv[:, 0:4, :], qkv[:, 4:8, :], qkv[:, 8:12, :], y[:, 4:8, :])
        rwkv_mix(core, z, lora, y[:, 0:4, :])
        bias = s.enter_context(nc.sbuf_tensor("bias_parts", [BIAS_PARTS * N_EXPERTS, N_BIAS], BF16))
        rest = s.enter_context(nc.sbuf_tensor("bias_rest", [BIAS_PARTS * N_EXPERTS, N_BIAS], F32))
        with core.block() as block:
            @block.sync
            def _(sp):
                for i in range(BIAS_PARTS):
                    sp.dma_start(rest[i * N_EXPERTS:(i + 1) * N_EXPERTS, :], core.a["eb"]).then_inc(core.const_loaded.sem, 16)
        casts, rests = split_biases(core, bias, rest)
        linear(core, "w_out2", lambda k: y[:, k, :], gated_residual(core, gate1), act_work=casts, pool_work=rests)
        core.const_loaded.close(16 * BIAS_PARTS)
        core.sem_a.close(2)
        core.sem_b.close(2)
        moe_layer(core, bias)


class LoopChain:

    def __init__(self, sig, eng, u, per_turn):
        self.sig, self.eng, self.u, self.per_turn, self.n = sig, eng, u, per_turn, 0

    def __call__(self, ins):
        self.n += 1
        ins.then_inc(self.sig.sem, 1)
        self.eng.wait_ge(self.sig.sem, self.u * self.per_turn + self.n)

    def done(self):
        assert self.n == self.per_turn, self.n


BIAS_PARTS, N_BIAS = 3, 3 * D


def split_biases(core, bias, rest):
    E = N_EXPERTS
    cast, left = core.sem_a, core.sem_b

    def casts(act):
        act.wait_ge(core.const_loaded.sem, core.const_loaded.at(16 * BIAS_PARTS))
        act.activation(bias[:, :], rest[:, :], ACT.Copy).then_inc(cast.sem, 1)
        act.wait_ge(left.sem, left.at(1))
        act.activation(bias[E:2 * E, :], rest[E:2 * E, :], ACT.Copy)
        act.activation(bias[2 * E:, :], rest[2 * E:, :], ACT.Copy).then_inc(cast.sem, 1)
        act.wait_ge(left.sem, left.at(2))
        act.activation(bias[2 * E:, :], rest[2 * E:, :], ACT.Copy)

    def rests(pool):
        pool.wait_ge(cast.sem, cast.at(1))
        pool.tensor_tensor(rest[:, :], rest[:, :], bias[:, :], ALU.subtract).then_inc(left.sem, 1)
        pool.wait_ge(cast.sem, cast.at(2))
        pool.tensor_tensor(rest[2 * E:, :], rest[2 * E:, :], bias[2 * E:, :], ALU.subtract).then_inc(left.sem, 1)
    return casts, rests


def mixture_of_experts(core, h, acc, bias):
    nc, ps = core.nc, core.ps
    E, S = N_EXPERTS, UNIT
    with ExitStack() as s:
        def sb(name, shape, dt=F32):
            return s.enter_context(nc.sbuf_tensor("moe_" + name, shape, dt))
        ht = sb("ht", [P, NB, D])
        table = sb("table", [P, UNITS, 2, NB])
        expert_of = sb("expert_of", [3 * E, UNITS])
        unit_int = sb("unit_int", [1, MAX_UNITS + 1], I32)
        selt, ytok = sb("selt", [P, 2 * TOK]), sb("ytok", [P, D // 2])
        to_token_major(core, [h[:, t, :] for t in range(DT)], lambda t, b: ht[:, b, t * P:t * P + P])
        with ExitStack() as s2:
            def sb2(name, shape, dt=F32):
                return s2.enter_context(nc.sbuf_tensor("route_" + name, shape, dt))
            rw = sb2("rw", [P, DT, E])
            lg, m, g, r = (sb2(n, [P, NB, E]) for n in ("lg", "m", "g", "r"))
            mx, ix, ixf = sb2("mx", [P, NB, 8]), sb2("ix", [P, NB, 8], U32), sb2("ixf", [P, NB, 8])
            sm = sb2("sm", [P, NB, 2])
            cnt, units, cum, first = (sb2(n, [P, E]) for n in ("cnt", "units", "cum", "first"))
            ecol, onehot = sb2("ecol", [BIAS_PARTS * E, 2]), sb2("onehot", [3 * E, UNITS])
            cf = sb2("cf", [1, 2, 3, E])
            rt, gt = sb2("rt", [E, TOK]), sb2("gt", [E, TOK])
            row = sb2("row", [1, MAX_UNITS + 1])
            with core.block() as block:
                @block.scalar
                def _(act):
                    act.dma_start(rw[:, :, :], core.a["router"]).then_inc(core.const_loaded.sem, 16)

                @block.gpsimd
                def _(pool):
                    pool.memset(acc[:, :, :], 0.0)
                    pool.memset(ytok[:, :], 0.0)
                    pool.memset(selt[:, :], 0.0).then_inc(core.sem_a.sem, 1)

                @block.tensor
                def _(pe):
                    pe.wait_ge(core.const_loaded.sem, core.const_loaded.at(16))
                    for b in range(NB):
                        for k in range(DT):
                            pe.matmul(ps[:, 0, b * E:b * E + E], h[:, k, b * P:b * P + P], rw[:, k, :], start=(k == 0),
                                      stop=(k == DT - 1))
            core.const_loaded.close(16)
            with core.block() as block:
                @block.vector
                def _(dve):
                    link = core.link("dve", dve)
                    link(dve.tensor_tensor(lg[:, :, :], ps[:, 0, 0:NB * E].rearrange("p (b e) -> p b e", e=E),
                                           bcast(core.vs("router_b").unsqueeze(1), [P, NB, E]), ALU.add))
                    for b in range(NB):
                        link(dve.max(mx[:, b, :], lg[:, b, :]))
                        link(dve.max_index(ix[:, b, :], mx[:, b, :], lg[:, b, :]))
                    link(dve.tensor_copy(ixf[:, :, :], ix[:, :, :]))
                    for b in range(NB):
                        link(dve.tensor_scalar(m[:, b, :], core.m("iota_e"), ixf[:, b, 0:1], None, ALU.is_equal))
                        for j in range(1, TOP_K):
                            link(dve.scalar_tensor_tensor(out=m[:, b, :], in0=core.m("iota_e"), scalar=ixf[:, b, j:j + 1],
                                                          in1=m[:, b, :], op0=ALU.is_equal, op1=ALU.add))
                    link(dve.tensor_scalar(sm[:, :, 0], mx[:, :, 0], -1.0, None, ALU.mult))
            with core.block() as block:
                @block.scalar
                def _(act):
                    for b in range(NB):
                        act.activation(g[:, b, :], lg[:, b, :], ACT.Exp, bias=sm[:, b, 0:1])

                @block.tensor
                def _(pe):
                    pe.matmul(ps[:, 1, 0:E], core.m("tri_lt"), m[:, 0, :], start=True, stop=True)
                    pe.matmul(ps[:, 1, E:2 * E], core.m("tri_lt"), m[:, 1, :], start=True, stop=False)
                    pe.matmul(ps[:, 1, E:2 * E], core.m("ones"), m[:, 0, :], start=False, stop=True)
                    for b in range(NB):
                        pe.matmul(ps[:, 2, 0:E], core.m("ones"), m[:, b, :], start=(b == 0), stop=(b == NB - 1))
            with core.block() as block:
                @block.vector
                def _(dve):
                    link = core.link("dve", dve)
                    link(dve.tensor_tensor(g[:, :, :], g[:, :, :], m[:, :, :], ALU.mult))
                    link(dve.tensor_reduce(sm[:, :, 1], g[:, :, :], AX, ALU.add))
                    link(dve.reciprocal(sm[:, :, 1], sm[:, :, 1]))
                    link(dve.tensor_tensor(g[:, :, :], g[:, :, :], bcast(sm[:, :, 1:2], [P, NB, E]), ALU.mult))
                    link(dve.tensor_copy(cnt[:, :], ps[:, 2, 0:E]))
                    link(dve.tensor_scalar(units[:, :], cnt[:, :], 0.0, None, ALU.is_gt))
                    for j in range(1, TOK // S):
                        link(dve.scalar_tensor_tensor(out=units[:, :], in0=cnt[:, :], scalar=float(j * S),
                                                      in1=units[:, :], op0=ALU.is_gt, op1=ALU.add))
                    link(dve.tensor_tensor_scan(cum[:, :], core.m("ones")[:, 0:E], units[:, :], 0.0, ALU.mult, ALU.add))
                    link(dve.tensor_tensor(first[:, :], cum[:, :], units[:, :], ALU.subtract))
                    link(dve.tensor_copy(cf[:, 0], bcast(cum[0:1, :].unsqueeze(1), [1, 3, E])))
                    link(dve.tensor_copy(cf[:, 1], bcast(first[0:1, :].unsqueeze(1), [1, 3, E])))
                    link(dve.scalar_tensor_tensor(out=r[:, :, :], in0=ps[:, 1, 0:NB * E].rearrange("p (b e) -> p b e", e=E),
                                                  scalar=1000.0, in1=m[:, :, :], op0=ALU.add, op1=ALU.mult))
                    link(dve.tensor_scalar(cnt[:, :], first[:, :], float(S), -1000.0, ALU.mult, ALU.add))
                    link(dve.tensor_tensor(r[:, :, :], r[:, :, :], bcast(cnt[:, :].unsqueeze(1), [P, NB, E]), ALU.add))
            with core.block() as block:
                @block.tensor
                def _(pe):
                    ident = core.m("ident")
                    for i in range(2):
                        pe.matmul(ps[0:3 * E, 0, i:i + 1], cf[:, i].rearrange("p a e -> p (a e)"), core.m("ones")[0:1, 0:1],
                                  start=True, stop=True)
                    for b in range(NB):
                        pe.transpose(ps[0:E, 1, b * P:b * P + P], r[:, b, :], ident)
                        pe.transpose(ps[0:E, 2, b * P:b * P + P], g[:, b, :], ident)
            with core.block() as block:
                @block.vector
                def _(dve):
                    link = core.link("dve", dve)
                    link(dve.tensor_copy(ecol[:, :], ps[0:3 * E, 0, 0:2]))
                    link(dve.tensor_copy(rt[:, :], ps[0:E, 1, 0:TOK]))
                    link(dve.tensor_copy(gt[:, :], ps[0:E, 2, 0:TOK]))
                    iu = core.m("iota_u")[0:3 * E, :]
                    link(dve.tensor_scalar(onehot[:, :], iu, ecol[:, 0:1], None, ALU.is_lt))
                    link(dve.scalar_tensor_tensor(out=onehot[:, :], in0=iu, scalar=ecol[:, 1:2], in1=onehot[:, :],
                                                  op0=ALU.is_ge, op1=ALU.mult))
                    link(dve.tensor_copy(expert_of[:, :], onehot[:, :]))
            with core.block() as block:
                @block.tensor
                def _(pe):
                    for b in range(NB):
                        pe.matmul(ps[:, 0, b * S:b * S + UNITS], rt[:, b * P:b * P + P], onehot[0:E, :], start=True, stop=True)
                        pe.matmul(ps[:, 1, b * S:b * S + UNITS], gt[:, b * P:b * P + P], onehot[0:E, :], start=True, stop=True)
                    pe.matmul(ps[0:1, 2, 0:UNITS], core.m("col_e")[0:E, :], onehot[0:E, :], start=True, stop=True)
            with core.block() as block:
                @block.vector
                def _(dve):
                    link = core.link("dve", dve)
                    link(dve.tensor_copy(row[:, 0:MAX_UNITS], ps[0:1, 2, 0:MAX_UNITS]))
                    link(dve.tensor_copy(row[:, MAX_UNITS:], cum[0:1, E - 1:E]))
                    link(dve.tensor_copy(unit_int[:, :], row[:, :]))
                    for b in range(NB):
                        link(dve.scalar_tensor_tensor(out=table[:, :, 0, b], in0=core.m("iota_u"), scalar=-float(S),
                                                      in1=ps[:, 0, b * S:b * S + UNITS], op0=ALU.mult, op1=ALU.add))
                        link(dve.tensor_copy(table[:, :, 1, b], ps[:, 1, b * S:b * S + UNITS]))

        cur = sb("cur", [P, 2, 2, NB])
        sel, selg = sb("sel", [P, NB, 2 * S]), sb("selg", [P, NB, 2 * S])
        pick = sb("pick", [BIAS_PARTS * E, S], BF16)
        xg, hidt = sb("xg", [P, DT, 2 * S]), sb("hidt", [P, D // 2])
        glu, lin, sg = sb("glu", [P, D // 2]), sb("lin", [P, D // 2]), sb("sg", [P, D // 2])
        loaded = [core.counter(f"expert_panel{i}") for i in range(RING)]
        names = ("expert_panel_used", "picked", "gates_picked", "expert_picked", "gathered", "gathered_copied",
                 "gates_turned", "gates_copied", "hidden", "glu_ready", "sigmoid_ready", "hidden_ready", "hidden_turned",
                 "hidden_copied", "bias_used", "expert_out", "out_copied", "scattered", "added", "dve_turn")
        (used, picked, gates_picked, expert_picked, gathered, xg_ready, gates_turned, gates_copied, hidden, glu_ready,
         sig_ready, hid_ready, hid_turned, hid_copied, bias_used, outs, copied, scattered, added, turn) = (
            core.counter(n) for n in names)
        PANELS = 12
        scatter_banks = (5, 3, 2, 4)
        with core.block() as block:
            @block.tensor
            def _(pe):
                pe.wait_ge(core.sem_a.sem, core.sem_a.at(1))
                pe.sem_inc(used.sem, RING)
                pe.sem_inc(added.sem, 1)
        added.close(1)
        core.sem_a.close(1)

        def unit_count(eng):
            return eng.value_load(unit_int[0:1, MAX_UNITS:MAX_UNITS + 1], min_val=1, max_val=MAX_UNITS)

        def pick_tokens(dve, link, u):
            link(dve.tensor_copy(cur[:, 0], table[:, bass.ds(u, 1)].rearrange("p a i b -> p (a i) b")))
            for b in range(NB):
                ins = dve.tensor_scalar(sel[:, b, :], core.m("iota_slot"), cur[:, 0, 0, b:b + 1], None, ALU.is_equal)
            ins.then_inc(picked.sem, 1)

        def pick_gates(dve, link, u):
            link(dve.tensor_copy(cur[:, 1], table[:, bass.ds(u, 1)].rearrange("p a i b -> p (a i) b")))
            for b in range(NB):
                ins = dve.tensor_scalar(selg[:, b, :], core.m("iota_slot"), cur[:, 1, 0, b:b + 1], cur[:, 1, 1, b:b + 1],
                                        ALU.is_equal, ALU.mult)
            ins.then_inc(gates_picked.sem, 1)

        def pick_expert(dve, u):
            dve.tensor_copy(pick[:, :], bcast(expert_of[:, bass.ds(u, 1)], [BIAS_PARTS * E, S])).then_inc(expert_picked.sem, 1)

        def copy_gathered(dve):
            for i in range(2):
                ins = dve.tensor_copy(xg[:, 4 * i:4 * i + 4, :], ps[:, 6 + i, :].rearrange("p (k n) -> p k n", n=2 * S))
            ins.then_inc(xg_ready.sem, 1)

        def gather(pe):
            for k in range(DT):
                for b in range(NB):
                    mm = pe.matmul(ps[:, 6 + k // 4, k % 4 * 2 * S:k % 4 * 2 * S + 2 * S], ht[:, b, k * P:k * P + P], sel[:, b, :],
                                   start=(b == 0), stop=(b == NB - 1))
            mm.then_inc(gathered.sem, 1)

        def scatter(pe, u):
            pe.wait_ge(copied.sem, copied.at(u))
            pe.wait_ge(gates_copied.sem, gates_copied.at(u))
            pe.wait_ge(added.sem, added.at(u * 4))
            for t, bank in enumerate(scatter_banks):
                pe.matmul(ps[:, bank, :], ytok[:, t * P:t * P + P], selt[:, :], start=True, stop=True).then_inc(scattered.sem, 1)

        def add(dve, u):
            for t, bank in enumerate(scatter_banks):
                dve.wait_ge(scattered.sem, scattered.at(u * 4 + (t + 1)))
                dve.tensor_tensor(acc[:, t::4, :], acc[:, t::4, :],
                                  ps[:, bank, :].rearrange("p (k n) -> p k n", n=TOK), ALU.add).then_inc(added.sem, 1)

        with core.block() as block:
            @block.sync
            def _(sp):
                n = unit_count(sp)
                with sp.Fori(0, n) as u:
                    e = sp.value_load(unit_int[0:1, bass.ds(u, 1)], min_val=0, max_val=E - 1)
                    for j in range(PANELS):
                        sp.wait_ge(used.sem, used.at(u * PANELS + (j + 1)))
                        if j < 8:
                            src = core.a["w1"][bass.ds(e * 8 + j, 1)].rearrange("a p n -> p (a n)")
                            dst = core.ring[:, j % RING, :]
                        else:
                            src = core.a["w2"][bass.ds(e * 4 + (j - 8), 1)].rearrange("a (k p) n -> p (a k) n", p=P)
                            dst = core.ring[:, j % RING, :].rearrange("p (k n) -> p k n", n=D)
                        sp.dma_start(dst, src).then_inc(loaded[j % RING].sem, 16)

            @block.tensor
            def _(pe):
                n = unit_count(pe)
                ident = core.m("ident")
                pe.wait_ge(picked.sem, picked.at(1))
                gather(pe)
                halves = [(slice(0, S), 0), (slice(S, P), D // 2)]
                with pe.Fori(0, n) as u:
                    def panel(j):
                        pe.wait_ge(loaded[j % RING].sem, loaded[j % RING].at(u * (16 * PANELS // RING) + 16 * (j // RING + 1)))
                        return core.ring[:, j % RING, :]
                    pe.wait_ge(expert_picked.sem, expert_picked.at(u + 1))
                    pe.wait_ge(xg_ready.sem, xg_ready.at(u + 1))
                    for bank in range(2):
                        for out, at in halves:
                            pe.matmul(ps[out, bank, :], pick[:, :], bias[:, bank * D + at:bank * D + at + 512], start=True, stop=False)
                    for j in range(8):
                        w = panel(j)
                        for bank in range(2):
                            for out, at in halves:
                                mm = pe.matmul(ps[out, bank, :], xg[:, j, 0:S], w[:, bank * D + at:bank * D + at + 512],
                                               start=False, stop=(j == 7))
                        mm.then_inc(used.sem, 1)
                    pe.sem_inc(hidden.sem, 1)
                    scatter(pe, u)
                    pe.wait_ge(picked.sem, picked.at(u + 2))
                    gather(pe)
                    pe.wait_ge(gates_picked.sem, gates_picked.at(u + 1))
                    pe.wait_ge(added.sem, added.at(u * 4 + 4))
                    for b in range(NB):
                        mm = pe.transpose(ps[:, 5, b * P:b * P + P], selg[:, b, :], ident)
                    mm.then_inc(gates_turned.sem, 1)
                    pe.wait_ge(hid_ready.sem, hid_ready.at(u + 1))
                    for c in range(4):
                        mm = pe.transpose(ps[:, 3, c * P:c * P + P], lin[:, c * P:c * P + P], ident)
                    mm.then_inc(hid_turned.sem, 1)
                    for out, at in halves:
                        mm = pe.matmul(ps[out, 2, :], pick[:, :], bias[:, 2 * D + at:2 * D + at + 512], start=True, stop=False)
                    mm.then_inc(bias_used.sem, 1)
                    pe.wait_ge(hid_copied.sem, hid_copied.at(u + 1))
                    for q in range(4):
                        w = panel(8 + q)
                        for i in range(2):
                            k = 2 * q + i
                            at_k = k % 4 * P + k // 4 * S
                            for out, at in halves:
                                mm = pe.matmul(ps[out, 2, :], hidt[:, at_k:at_k + S], w[:, i * D + at:i * D + at + 512],
                                               start=False, stop=(k == DT - 1))
                        mm.then_inc(used.sem, 1)
                    pe.sem_inc(outs.sem, 1)
                scatter(pe, n)

            @block.scalar
            def _(act):
                n = unit_count(act)
                with act.Fori(0, n) as u:
                    act.wait_ge(glu_ready.sem, glu_ready.at(u + 1))
                    act.activation(sg[:, :], glu[:, :], ACT.Sigmoid, scale=SWIGLU_ALPHA).then_inc(sig_ready.sem, 1)

            @block.vector
            def _(dve):
                n = unit_count(dve)
                link = core.link("dve", dve)
                pick_tokens(dve, link, 0)
                pick_gates(dve, link, 0)
                pick_expert(dve, 0)
                dve.wait_ge(gathered.sem, gathered.at(1))
                copy_gathered(dve)
                with dve.Fori(0, n) as u:
                    link = LoopChain(turn, dve, u, 5)
                    dve.wait_ge(gathered.sem, gathered.at(u + 1))
                    pick_tokens(dve, link, u + 1)
                    dve.wait_ge(used.sem, used.at(u * PANELS + (RING + 8)))
                    dve.tensor_scalar(glu[:, :], ps[:, 0, :], SWIGLU_LIMIT, None, ALU.min).then_inc(glu_ready.sem, 1)
                    link(dve.tensor_scalar(lin[:, :], ps[:, 1, :], SWIGLU_LIMIT, -SWIGLU_LIMIT, ALU.min, ALU.max))
                    dve.wait_ge(glu_ready.sem, glu_ready.at(u + 1))
                    link(dve.scalar_tensor_tensor(out=lin[:, :], in0=lin[:, :], scalar=1.0, in1=glu[:, :], op0=ALU.add,
                                                  op1=ALU.mult))
                    dve.wait_ge(sig_ready.sem, sig_ready.at(u + 1))
                    link(dve.tensor_tensor(lin[:, :], lin[:, :], sg[:, :], ALU.mult))
                    dve.sem_inc(hid_ready.sem, 1)
                    add(dve, u)
                    dve.wait_ge(gathered.sem, gathered.at(u + 2))
                    copy_gathered(dve)
                    dve.wait_ge(gates_turned.sem, gates_turned.at(u + 1))
                    dve.tensor_copy(selt[0:S, 0:TOK], ps[0:S, 5, 0:TOK])
                    dve.tensor_copy(selt[S:P, TOK:], ps[S:P, 5, 0:TOK]).then_inc(gates_copied.sem, 1)
                    dve.wait_ge(hid_turned.sem, hid_turned.at(u + 1))
                    dve.tensor_copy(hidt[:, :], ps[:, 3, :]).then_inc(hid_copied.sem, 1)
                    pick_gates(dve, link, u + 1)
                    dve.wait_ge(bias_used.sem, bias_used.at(u + 1))
                    pick_expert(dve, u + 1)
                    dve.wait_ge(used.sem, used.at(u * PANELS + (RING + 12)))
                    dve.tensor_copy(ytok[:, :], ps[:, 2, :]).then_inc(copied.sem, 1)
                    link.done()
                add(dve, n)


def moe_layer(core, bias):
    nc = core.nc
    with ExitStack() as s:
        h = s.enter_context(nc.sbuf_tensor("moe_h", [P, DT, TOK], F32))
        acc = s.enter_context(nc.sbuf_tensor("moe_acc", [P, DT, TOK], F32))
        mod = core.mod2
        rms_modulate(core, "moe", h, core.vs("norm2"), mod[:, 32:40], mod[:, 24:32])
        mixture_of_experts(core, h, acc, bias)
        with core.block() as block:
            @block.vector
            def _(dve):
                for k in range(DT):
                    dve.scalar_tensor_tensor(out=core.x[:, k, :], in0=acc[:, k, :], scalar=mod[:, 40 + k:41 + k],
                                             in1=core.x[:, k, :], op0=ALU.mult, op1=ALU.add)


def switch_stream(core, stream):
    assert core.issued == core.used == len(core.stream)
    for slot in range(RING):
        core.panel_loaded[slot].close(16 * len(range(slot, len(core.stream), RING)))
    core.panel_used.close(len(core.stream))
    core.stream, core.issued, core.used = panels_of(stream), 0, 0


def rms_tiles(core, name, t, g, width):
    n = width // P
    with ExitStack() as s:
        sq = s.enter_context(core.nc.sbuf_tensor(f"{name}_sq", [P, n, TOK], F32))
        rs = s.enter_context(core.nc.sbuf_tensor(f"{name}_rs", [P, TOK], F32))
        with core.block() as block:
            @block.scalar
            def _(act):
                act.activation(sq[:, :, :], t, ACT.Square)
        column_sums(core, [(core.ps[:, 4, 0:TOK], core.m("ones"), [sq[:, k, :] for k in range(n)])])
        rstd_of(core, core.ps[:, 4, 0:TOK], rs[:, :], 1.0 / width, RMS_EPS)
        with core.block() as block:
            @block.vector
            def _(dve):
                for k in range(n):
                    dve.scalar_tensor_tensor(out=t[:, k, :], in0=t[:, k, :], scalar=core.v(g, k), in1=rs[:, :],
                                             op0=ALU.mult, op1=ALU.mult)


TWO_PI_PARTS = (6.28125, 1.935303211212158e-03, 2.535181590533e-09)
ROUND = 1.5 * 2.0 ** 23
HALF_PI = float(np.float32(np.pi / 2))
PI = float(np.nextafter(np.float32(np.pi), np.float32(0)))


def rope_tables(core, pos, tables):
    nc = core.nc
    with ExitStack() as s:
        ang = s.enter_context(nc.sbuf_tensor("rope_angle", [P, TOK], F32))
        turns = s.enter_context(nc.sbuf_tensor("rope_turns", [P, TOK], F32))
        with core.block() as block:
            @block.vector
            def _(dve):
                link = core.link("dve", dve)
                for invf, cos, sin in tables:
                    for out, lead in ((sin, 0.0), (cos, HALF_PI)):
                        link(dve.tensor_scalar(ang[:, :], pos, core.m(invf), None, ALU.mult))
                        link(dve.tensor_scalar(turns[:, :], ang[:, :], 1.0 / (2 * np.pi), lead / (2 * np.pi), ALU.mult, ALU.add))
                        link(dve.tensor_scalar(turns[:, :], turns[:, :], ROUND, None, ALU.add))
                        link(dve.tensor_scalar(turns[:, :], turns[:, :], ROUND, None, ALU.subtract))
                        for c in TWO_PI_PARTS:
                            link(dve.scalar_tensor_tensor(out=ang[:, :], in0=turns[:, :], scalar=-c, in1=ang[:, :],
                                                          op0=ALU.mult, op1=ALU.add))
                        if lead:
                            link(dve.tensor_scalar(ang[:, :], ang[:, :], lead, None, ALU.add))
                        link(dve.tensor_scalar(out, ang[:, :], PI, -PI, ALU.min, ALU.max))
        with core.block() as block:
            @block.scalar
            def _(act):
                for _, cos, sin in tables:
                    act.activation(cos, cos, ACT.Sin)
                    act.activation(sin, sin, ACT.Sin)


def rope(core, name, tiles, rot, cos, sin):
    nc, ps = core.nc, core.ps
    with ExitStack() as s:
        part = s.enter_context(nc.sbuf_tensor(f"{name}_part", [P, 2, TOK], F32))
        swapped, done = core.sem_a, core.sem_b
        with core.block() as block:
            @block.tensor
            def _(pe):
                for i, t in enumerate(tiles):
                    if i >= 4:
                        pe.wait_ge(done.sem, done.at(i - 3))
                    pe.matmul(ps[:, i % 4, 0:TOK], core.m(rot), t, start=True, stop=True).then_inc(swapped.sem, 1)

            @block.vector
            def _(dve):
                link = core.link("dve", dve)
                for i, t in enumerate(tiles):
                    dve.wait_ge(swapped.sem, swapped.at(i + 1))
                    dve.tensor_tensor(part[:, i % 2, :], ps[:, i % 4, 0:TOK], sin, ALU.mult).then_inc(done.sem, 1)
                    link(dve.tensor_tensor(t, t, cos, ALU.mult))
                    dve.wait_ge(done.sem, done.at(i + 1))
                    link(dve.tensor_tensor(t, t, part[:, i % 2, :], ALU.add))
        swapped.close(len(tiles))
        done.close(len(tiles))


def third_block(core):
    nc, x = core.nc, core.x
    switch_stream(core, STREAM_2)
    with ExitStack() as s:
        def sb(name, shape, dt=F32):
            return s.enter_context(nc.sbuf_tensor("third_" + name, shape, dt))
        pos_int, pos = sb("pos_int", [P, TOK], I32), sb("pos", [P, TOK])
        tab = sb("tab", [P, 4, TOK])
        cos32, sin32, cos64, sin64 = (tab[:, i, :] for i in range(4))
        with core.block() as block:
            @block.sync
            def _(sp):
                issue_panels(core, sp, RING)

            @block.scalar
            def _(act):
                act.dma_start(pos_int[:, :], core.a["positions"]).then_inc(core.const_loaded.sem, 16)

            @block.vector
            def _(dve):
                dve.wait_ge(core.const_loaded.sem, core.const_loaded.at(16))
                dve.tensor_copy(pos[:, :], pos_int[:, :])
        core.const_loaded.close(16)
        rope_tables(core, pos[:, :], [("invf32", cos32, sin32), ("invf64", cos64, sin64)])
        shift, scale, gate = (core.mod3[:, 8 * i:8 * i + 8] for i in range(3))
        n_lat, n_z, n_mb = 4, 4, 12
        lat = sb("lat", [P, n_lat, TOK])
        z_mla, z_mb = sb("z_mla", [P, n_z, TOK]), sb("z_mb", [P, n_z, TOK])
        mb = sb("moba_qkv", [P, n_mb, TOK])
        merge = sb("merge", [P, 2 * DT, TOK])
        h = sb("h", [P, DT, TOK])
        rms_modulate(core, "third", h, core.vs("g_pre"), scale, shift)

        def plain(dst):
            return [("act", copy_tiles(core, lambda m: dst[:, m, :])(m), None) for m in range(dst.shape[1])]

        def silu(dst):
            return [("act", copy_tiles(core, lambda m: dst[:, m, :], func=ACT.Silu)(m), None) for m in range(n_z)]
        gates = [("act", copy_tiles(core, lambda m: merge[:, m, :], func=ACT.Sigmoid,
                                    bias=lambda m: core.v("b_merge", m))(m), None) for m in range(2 * DT)]
        linear(core, "w_in3", lambda k: h[:, k, :], plain(lat) + silu(z_mla) + plain(mb) + silu(z_mb) + gates)

        o = sb("o", [P, n_z, TOK])
        vt = sb("vt", [P, NB, 4 * P])
        with ExitStack() as s2:
            q = s2.enter_context(nc.sbuf_tensor("mla_q", [P, DT, TOK], F32))
            kv = s2.enter_context(nc.sbuf_tensor("mla_kv", [P, DT + 4, TOK], F32))
            rms_tiles(core, "q_lat", lat[:, 0:2, :], "g_q_lat", 2 * P)
            rms_tiles(core, "kv_lat", lat[:, 2:3, :], "g_kv_lat", P)
            linear(core, "w_uq", lambda k: lat[:, k, :], plain(q))
            linear(core, "w_ukv", lambda k: lat[:, 2, :], plain(kv))
            rope(core, "mla", [q[:, t, :] for t in range(DT)] + [lat[:, 3, :]], "rot32", cos32, sin32)
            with core.block() as block:
                @block.vector
                def _(dve):
                    for t in range(DT):
                        dve.tensor_copy(kv[64:96, t, :], lat[64:96, 3, :])
            to_token_major(core, [kv[:, DT + t, :] for t in range(4)], lambda t, b: vt[:, b, t * P:t * P + P])
            softmax_attention(core, "mla", range(8), lambda u: q[:, u, :], lambda u: kv[:, u, :],
                              lambda u, b: vt[:, b, HD * u:HD * u + HD], "causal", 96 ** -0.5,
                              lambda e, j, p: e.tensor_tensor(o[:, j, :], p, z_mla[:, j, :], ALU.mult))
        y = h
        tiles = []
        for m in range(DT):
            def take_a(e, p, m=m):
                return e.tensor_tensor(y[:, m, :], p, merge[:, m, :], ALU.mult)
            tiles.append(("dve", take_a, None))
        linear(core, "w_om", lambda k: o[:, k, :], tiles)

        rope(core, "moba", [mb[:, t, :] for t in range(8)], "rot64", cos64, sin64)
        to_token_major(core, [mb[:, 8 + t, :] for t in range(4)], lambda t, b: vt[:, b, t * P:t * P + P])

        def half(u):
            return slice(HD * (u % 2), HD * (u % 2) + HD)
        softmax_attention(core, "moba", range(8), lambda u: mb[half(u), u // 2, :], lambda u: mb[half(u), 4 + u // 2, :],
                          lambda u, b: vt[:, b, HD * u:HD * u + HD], "causal", HD ** -0.5,
                          lambda e, j, p: e.tensor_tensor(o[:, j, :], p, z_mb[:, j, :], ALU.mult))
        tiles = []
        for m in range(DT):
            def take_b(e, p, m=m):
                return e.tensor_tensor(merge[:, DT + m, :], p, merge[:, DT + m, :], ALU.mult)

            def after(e, link, wait_tile, m=m):
                wait_tile(e, m)
                link(e.tensor_tensor(y[:, m, :], y[:, m, :], merge[:, DT + m, :], ALU.add))
            tiles.append(("dve", take_b, after))
        linear(core, "w_ob", lambda k: o[:, k, :], tiles)

        out = merge[:, 0:DT, :]
        linear(core, "w_out3", lambda k: y[:, k, :], plain(out))
        sq, rs, gg = merge[:, DT:, :], sb("out_rs", [P, TOK]), sb("gg", [P, DT])
        with core.block() as block:
            @block.scalar
            def _(act):
                for k in range(DT):
                    act.activation(sq[:, k, :], out[:, k, :], ACT.Square).then_inc(core.sem_a.sem, 1)

            @block.tensor
            def _(pe):
                for k in range(DT):
                    pe.wait_ge(core.sem_a.sem, core.sem_a.at(k + 1))
                    pe.matmul(core.ps[:, 4, 0:TOK], core.m("ones"), sq[:, k, :], start=(k == 0), stop=(k == DT - 1))

            @block.vector
            def _(dve):
                dve.tensor_tensor(gg[:, :], gate, core.vs("g_post"), ALU.mult)
        core.sem_a.close(DT)
        rstd_of(core, core.ps[:, 4, 0:TOK], rs[:, :], 1.0 / D, RMS_EPS)
        with core.block() as block:
            @block.vector
            def _(dve):
                link = core.link("dve", dve)
                for k in range(DT):
                    link(dve.scalar_tensor_tensor(out=out[:, k, :], in0=out[:, k, :], scalar=gg[:, k:k + 1], in1=rs[:, :],
                                                  op0=ALU.mult, op1=ALU.mult))
                    link(dve.tensor_tensor(x[:, k, :], x[:, k, :], out[:, k, :], ALU.add))


def start(core):
    with core.block() as block:
        @block.scalar
        def _(act):
            act.dma_start(core.x[:, :, :], core.a["x"]).then_inc(core.const_loaded.sem, 16)
            act.dma_start(core.vec[:, :], core.a["vectors"]).then_inc(core.const_loaded.sem, 16)
            act.dma_start(core.mat[:, :], core.a["matrices"]).then_inc(core.const_loaded.sem, 16)
            act.wait_ge(core.const_loaded.sem, core.const_loaded.at(48))

        @block.sync
        def _(sp):
            sp.wait_ge(core.const_loaded.sem, core.const_loaded.at(48))
            issue_panels(core, sp, RING)
    core.const_loaded.close(48)


def finish(core):
    with core.block() as block:
        @block.scalar
        def _(act):
            act.dma_start(core.a["out"], core.x[:, :, :]).then_inc(core.const_loaded.sem, 16)
            act.wait_ge(core.const_loaded.sem, core.const_loaded.at(16))
    core.const_loaded.close(16)


def blocks_kernel(nc, a):
    with ExitStack() as ctx:
        core = Core(nc, a, ctx)
        start(core)
        with ExitStack() as s:
            start_modulation(core, s)
            ssd_layer(core)
            ffn(core, 0)
            per_layer_embedding(core, 0)
            attention_layer(core)
            ffn(core, 1)
            per_layer_embedding(core, 1)
        second_block(core)
        third_block(core)
        finish(core)


def tokens_last(x):
    return np.ascontiguousarray(x.reshape(x.shape[0], -1, P).transpose(2, 1, 0))


def column(v):
    return v.reshape(-1, P).T


def panels(w, width=PANEL):
    k, n = w.shape
    return np.ascontiguousarray(w.reshape(k // P, P, n // width, width).transpose(2, 1, 0, 3)).reshape(n // width, P, -1)


def short(v):
    out = np.zeros((P, 1), np.float32)
    out[:v.size, 0] = v.ravel()
    return out


def rows(v, n=None):
    return np.broadcast_to(v.reshape(1, -1), (P, v.size))


def head_order(first):
    order = []
    for t in range(8):
        pair = t // 4
        for half in range(2):
            h = 8 * pair + 4 * half + t % 4
            order += [first + HD * h + i for i in range(HD)]
    return order


def layout(i):
    f = {k: np.asarray(v) for k, v in i.items()}
    a = {"x": tokens_last(f["x"][0]), "p": np.stack([tokens_last(f["p"][l, 0]) for l in range(DEPTH)])}
    w = f["w_in_mix"][0]
    z, xbc, dt, sc = np.split(w, [1024, 2560, 2576], axis=1)
    sb, sc_c, sc_h = np.split(sc, 3, axis=1)
    a["w_in"] = panels(np.concatenate([xbc, sc_c, sc_h, sb, z], axis=1))
    a["w_dt"] = np.ascontiguousarray(dt.reshape(DT, P, 16).transpose(1, 0, 2))
    a["w_out"] = panels(f["w_out_mix"][0])
    for l in range(DEPTH):
        g, u = f["w_ffn_gate"][l].reshape(D, FF_T, P), f["w_ffn_up"][l].reshape(D, FF_T, P)
        a[f"ffn_up{l}"] = panels(np.stack([g, u], axis=2).reshape(D, 2 * D_FF))
        a[f"ffn_dn{l}"] = panels(f["w_ffn_down"][l])
        a[f"ple_g{l}"] = panels(f["w_ple_gate"][l])
        a[f"ple_p{l}"] = panels(f["w_ple"][l])
    qo = head_order(0)
    perm = np.array(qo + list(range(D, 1536)))
    a["qkv"] = panels(f["w_qkv"][0][:, perm])
    a["w_o"] = panels(f["w_o"][0][np.array(qo), :])
    vec = {
        "dt_bias": short(f["ssd_dt_bias"]), "a_log": short(f["ssd_a_log"]),
        "conv_w": column(f["ssd_conv_w"][0]), "conv_b": column(f["ssd_conv_b"][0]), "sc_w": column(f["sc_conv_w"][0]),
        "ssd_d": column(np.repeat(f["ssd_d"][0], HD)), "ssd_norm": column(f["ssd_norm_w"][0]),
        "ln_mix_g": column(f["ln_mix_g"]), "ln_mix_b": column(f["ln_mix_b"]),
        "ln_ffn_g": column(f["ln_ffn_g"]), "ln_ffn_b": column(f["ln_ffn_b"]), "b_ple": column(f["b_ple_gate"]),
        "b_qkv": column(f["b_qkv"][0][perm]), "b_o": column(f["b_o"]), "sinks": rows(f["attn_sinks"][0]),
        "c_2": column(f["c_2"]), "norm1": column(f["norm1_g_2"]), "norm2": column(f["norm2_g_2"]),
        "ada_b_2": column(f["ada_b_2"]), "mu": column(f["shift_mu_2"]), "decay_w0": column(f["decay_w0_2"]),
        "iclr_a0": column(f["iclr_a0_2"]), "k_k": column(f["k_k_2"]), "k_a": column(f["k_a_2"]),
        "r_k": column(f["r_k_2"]), "lnx_w": column(f["lnx_w_2"]), "lnx_b": column(f["lnx_b_2"]),
        "q_norm": np.tile(f["q_norm_g_2"].reshape(HD, 1), (2, 1)), "k_norm": np.tile(f["k_norm_g_2"].reshape(HD, 1), (2, 1)),
        "sb_out": column(f["sb_out_g_2"]), "router_b": rows(f["router_b_2"]),
        "c_3": column(f["c_3"]), "b_ada_3": column(f["b_ada_3"]), "g_pre": column(f["g_pre_3"]),
        "g_post": column(f["g_post_3"]), "g_q_lat": column(f["g_q_lat_3"]), "g_kv_lat": column(f["g_kv_lat_3"]),
        "b_merge": column(f["b_merge_3"]),
    }
    assert all(vec[n].shape == (P, w) for n, w in VECTORS), [n for n, w in VECTORS if vec[n].shape != (P, w)]
    a["vectors"] = np.ascontiguousarray(np.concatenate([vec[n] for n, _ in VECTORS], axis=1))
    a["matrices"] = constant_matrices()
    a["ada2"] = panels(f["ada_w_2"][0])
    a["w_in2"] = panels(f["w_in_2"][0])
    a["w_out2"] = panels(f["w_out_2"][0])
    a["lora"] = np.ascontiguousarray(np.concatenate([
        np.concatenate([f["decay_up_2"][0], f["iclr_up_2"][0]], axis=0), f["gate_up_2"][0]], axis=1))
    a["router"] = np.ascontiguousarray(f["router_w_2"][0].reshape(DT, P, N_EXPERTS).transpose(1, 0, 2))
    a["w1"] = f["exp_w1_2"][0].reshape(N_EXPERTS * 8, P, SLOT)
    a["w2"] = f["exp_w2_2"][0].reshape(N_EXPERTS * 4, 2 * P, D)
    a["eb"] = np.ascontiguousarray(np.concatenate([f["exp_b1_2"][0], f["exp_b2_2"][0]], axis=1))
    w = f["w_in_3"][0]
    q_lat, kv_lat, k_rope, z_mla, q_mb, k_mb, v_mb, z_mb, merge = np.split(
        w, np.cumsum([256, 128, 32, 512, 512, 512, 512, 512]), axis=1)
    a["w_in3"] = panels(np.concatenate([q_lat, kv_lat, np.tile(k_rope, (1, 4)), z_mla, q_mb, k_mb, v_mb, z_mb, merge], axis=1))
    a["ada3"] = panels(f["w_ada_3"][0])
    uq = f["w_uq_3"][0].reshape(256, 8, 96)
    a["w_uq"] = panels(np.pad(uq, ((0, 0), (0, 0), (0, 32))).reshape(256, 1024))
    ukv = f["w_ukv_3"][0].reshape(128, 8, 2, 64)
    k_nope = np.pad(ukv[:, :, 0], ((0, 0), (0, 0), (0, 64))).reshape(128, 1024)
    a["w_ukv"] = panels(np.concatenate([k_nope, ukv[:, :, 1].reshape(128, 512)], axis=1))
    a["w_om"] = panels(f["w_o_mla_3"][0])
    a["w_ob"] = panels(f["w_o_moba_3"][0])
    a["w_out3"] = panels(f["w_out_3"][0])
    a["positions"] = np.ascontiguousarray(np.broadcast_to(f["positions_3"].astype(np.int32).reshape(1, TOK), (P, TOK)))
    return a


def kernel(**inputs):
    import concourse.bacc as bacc
    from concourse.bass_utils import run_bass_kernel_spmd

    nc = bacc.Bacc("TRN2", target_bir_lowering=False, num_devices=1)
    arrays = layout(inputs)
    a = {n: nc.dram_tensor(f"{n}_dram", v.shape, mybir.dt.from_np(v.dtype), kind="ExternalInput").ap()
         for n, v in arrays.items()}
    a["out"] = nc.dram_tensor("out_dram", (P, DT, TOK), F32, kind="ExternalOutput").ap()
    blocks_kernel(nc, a)
    r = run_bass_kernel_spmd(nc, [{f"{n}_dram": v for n, v in arrays.items()}], core_ids=[0])
    out = r.results[0]["out_dram"]
    return np.ascontiguousarray(out.transpose(2, 1, 0)).reshape(1, TOK, D)
```

```python
import numpy as np
from contextlib import ExitStack

import concourse.bass as bass
from concourse import mybir

F32 = mybir.dt.float32
I32 = mybir.dt.int32
BF16 = mybir.dt.bfloat16
U32 = mybir.dt.uint32
ALU = mybir.AluOpType
ACT = mybir.ActivationFunctionType
AX = mybir.AxisListType.X

P = 128
TOK = 256
NB = TOK // P
D = 1024
DT = D // P
DEPTH = 2
PANEL = 256
KG = 8
RING = 6
SLOT = KG * PANEL
ALPHA = (2 * DEPTH) ** 0.25
LN_EPS = 1e-5

SSD_HEADS, SSD_CHUNK, SSD_CONV, SC_CONV = 16, 128, 4, 3
SSD_GROUPS, HPG = 2, 8
XBC_T = 12
D_FF = 2816
FF_T = D_FF // P
HD = 64

C_RWKV_T, CHUNK = 14, 64
N_EXPERTS, TOP_K = 32, 4
UNIT = 64
MAX_UNITS = N_EXPERTS + TOK * TOP_K // UNIT
UNITS = MAX_UNITS + 1
SWIGLU_ALPHA, SWIGLU_LIMIT = 1.702, 7.0
RMS_EPS = 1e-6
BIG = 1.0e30


VECTORS = [
    ("junk", 1), ("dt_bias", 1), ("a_log", 1), ("conv_w", SSD_CONV * XBC_T), ("conv_b", XBC_T), ("sc_w", SC_CONV * DT),
    ("ssd_d", DT), ("ssd_norm", DT),
    ("ln_mix_g", 2 * DT), ("ln_mix_b", 2 * DT), ("ln_ffn_g", 2 * DT), ("ln_ffn_b", 2 * DT), ("b_ple", 2 * DT),
    ("b_qkv", 12), ("b_o", DT), ("sinks", 16),
    ("c_2", DT), ("norm1", DT), ("norm2", DT), ("ada_b_2", 48), ("mu", C_RWKV_T), ("decay_w0", 4), ("iclr_a0", 4),
    ("k_k", 4), ("k_a", 4), ("r_k", 4), ("lnx_w", 4), ("lnx_b", 4), ("q_norm", 1), ("k_norm", 1), ("sb_out", 4),
    ("router_b", N_EXPERTS),
    ("c_3", DT), ("b_ada_3", 24), ("g_pre", DT), ("g_post", DT), ("g_q_lat", 2), ("g_kv_lat", 1), ("b_merge", 16),
]
MATRICES = [
    ("ident", P), ("fold", 32), ("head_cols", 32), ("spread", 4 * P), ("ones", P), ("head_ones", P), ("tri_le", P), ("tri_lt", P), ("tri_gt", P),
    ("lt64", P), ("le64", P), ("level", 6 * P), ("rot64", P), ("rot32", P), ("band", 3 * P), ("causal", 3 * P),
    ("iota_slot", 2 * UNIT), ("iota_e", N_EXPERTS), ("iota_u", UNITS), ("col_e", 1), ("invf64", 1), ("invf32", 1),
    ("scan_keep", TOK), ("halves", 2),
]


def offsets(table):
    at, out = 0, {}
    for name, n in table:
        out[name] = (at, n)
        at += n
    return out, at


def constant_matrices():
    r = np.arange(P)[:, None]
    c = np.arange(P)[None, :]
    c2 = np.arange(2 * P)[None, :]
    m = {
        "ident": r == c, "fold": r % 32 == c[:, :32], "ones": np.ones((P, P)), "head_ones": r // HD == c // HD,
        "tri_le": r <= c, "tri_lt": r < c, "tri_gt": r > c,
        "lt64": (r // CHUNK == c // CHUNK) & (r < c), "le64": (r // CHUNK == c // CHUNK) & (r <= c),
    }
    m["head_cols"] = r // HD == c[:, :32] // 16
    m["spread"] = np.concatenate([(r // 32 == t) & (r % 32 // 16 == c // HD) for t in range(4)], axis=1) / 16.0
    m["level"] = np.concatenate([
        (r // (2 * b) == c // (2 * b)) & ((c // b) % 2 == 1) & ((r // b) % 2 == 0) for b in (1, 2, 4, 8, 16, 32)], axis=1)

    def rotation(width):
        half = width // 2
        low = c % width < half
        return np.where(low, -1.0 * (r == c + half), 1.0 * (r == c - half))

    m["rot64"] = rotation(64)
    rotated = (c >= 64) & (c < 96)
    m["rot32"] = rotation(32) * rotated
    rel = r + P - c2
    for name, ok in (("band", (rel >= 0) & (rel < 128)), ("causal", rel >= 0)):
        full = np.where(ok, 0.0, -BIG)
        m[name] = np.concatenate([full[:, P:], full], axis=1)
    m["iota_slot"] = np.broadcast_to(np.arange(2 * UNIT) % UNIT, (P, 2 * UNIT))
    m["iota_e"] = np.broadcast_to(np.arange(N_EXPERTS), (P, N_EXPERTS))
    m["iota_u"] = np.broadcast_to(np.arange(UNITS), (P, UNITS))
    m["col_e"] = r % N_EXPERTS
    m["invf64"] = np.float32(10000.0) ** (-(np.arange(P) % 32).astype(np.float32) / np.float32(32))[:, None]
    m["invf32"] = np.float32(10000.0) ** (-(np.arange(P) % 16).astype(np.float32) / np.float32(16))[:, None] * rotated.T
    m["halves"] = np.concatenate([r < HD, r >= HD], axis=1)
    m["scan_keep"] = np.broadcast_to((np.arange(TOK) % CHUNK != 0), (P, TOK))
    return np.concatenate([np.asarray(m[n], np.float32).reshape(P, w) for n, w in MATRICES], axis=1)


STREAM_1 = [
    ("w_in", 22, 8, 256), ("w_out", 4, 16, 256),
    ("ffn_up0", 22, 8, 256, ("ada2", 24)), ("ffn_dn0", 4, 22, 256), ("ple_g0", 4, 8, 256), ("ple_p0", 4, 2, 256),
    ("qkv", 6, 8, 256), ("w_o", 4, 8, 256),
    ("ffn_up1", 22, 8, 256, ("ada3", 12)), ("ffn_dn1", 4, 22, 256), ("ple_g1", 4, 8, 256), ("ple_p1", 4, 2, 256),
    ("w_in2", 13, 8, 256), ("w_out2", 4, 8, 256),
]
STREAM_2 = [
    ("w_in3", 20, 8, 256), ("w_uq", 4, 2, 256), ("w_ukv", 6, 1, 256),
    ("w_om", 4, 4, 256), ("w_ob", 4, 4, 256), ("w_out3", 4, 8, 256),
]


def panels_of(stream):
    out = []
    for name, n, kt, _, *side in stream:
        side = [(side[0][0], j, 0, KG) for j in range(side[0][1])] if side else []
        for j in range(n):
            for k0 in range(0, kt, KG):
                out.append((name, j, k0, min(KG, kt - k0)))
            out += side[:1]
            side = side[1:]
        out += side
    return out


class Signal:

    def __init__(self, sem):
        self.sem, self.base = sem, 0

    def at(self, n):
        return self.base + n

    def close(self, n):
        self.base += n


class Core:

    def __init__(self, nc, a, ctx):
        self.nc, self.a, self.ctx = nc, a, ctx
        self.v_at, nv = offsets(VECTORS)
        self.m_at, nm = offsets(MATRICES)
        self.vec = self.sb("vec", [P, nv])
        self.mat = self.sb("mat", [P, nm])
        self.x = self.sb("x_res", [P, DT, TOK])
        self.ring = self.sb("ring", [P, RING, SLOT])
        self.ps = ctx.enter_context(nc.psum_tensor("ps", [P, 8, 512], F32))
        self.panel_loaded = [self.counter(f"panel_loaded{s}") for s in range(RING)]
        self.panel_used = self.counter("panel_used")
        self.act_evac = self.counter("act_evac")
        self.dve_evac = self.counter("dve_evac")
        self.const_loaded = self.counter("const_loaded")
        self.chain = {e: self.counter(f"{e}_chain") for e in ("pe", "act", "dve", "pool")}
        self.sem_a, self.sem_b, self.sem_c, self.sem_d, self.sem_e = (
            self.counter(n) for n in ("stage_in", "stage_mid", "stage_exp", "stage_mul", "stage_out"))
        self.sem_f, self.sem_g, self.sem_h = self.counter("stage_aux"), self.counter("stage_aux2"), self.counter("stage_end")
        self.junk = self.sb("junk", [P, 1])
        self.rstd, self.gain = self.sb("norm_rstd", [P, TOK]), self.sb("norm_gain", [P, DT])
        small = self.sb("modulations", [P, 48 + 24])
        self.mod2, self.mod3 = small[:, 0:48], small[:, 48:72]
        self.stream, self.issued, self.used = panels_of(STREAM_1), 0, 0

    def sb(self, name, shape, dt=F32):
        return self.ctx.enter_context(self.nc.sbuf_tensor(name, shape, dt))

    def counter(self, name):
        return Signal(self.ctx.enter_context(self.nc.semaphore(name)))

    def v(self, name, i=0, parts=P):
        at, n = self.v_at[name]
        return self.vec[0:parts, at + i:at + i + 1]

    def vs(self, name):
        at, n = self.v_at[name]
        return self.vec[:, at:at + n]

    def m(self, name, i=0, w=None):
        at, n = self.m_at[name]
        w = w or min(n, P)
        return self.mat[:, at + i * w:at + i * w + w]

    def load_table(self, act, func):
        act.activation(self.junk[:, :], self.v("junk"), func)

    def block(self):
        return self.nc.Block(no_gpsimd_drain=True)

    def link(self, which, eng):
        sig = self.chain[which]

        def link(ins):
            sig.base += 1
            ins.then_inc(sig.sem, 1)
            eng.wait_ge(sig.sem, sig.base)
        return link


def issue_panels(core, sp, upto):
    while core.issued < min(upto, len(core.stream)):
        i = core.issued
        name, j, k0, kn = core.stream[i]
        slot = i % RING
        if i >= RING:
            sp.wait_ge(core.panel_used.sem, core.panel_used.at(i - RING + 1))
        w = core.a[name][j, :, k0 * PANEL:(k0 + kn) * PANEL]
        sp.dma_start(core.ring[:, slot, 0:kn * PANEL], w).then_inc(core.panel_loaded[slot].sem, 16)
        core.issued += 1


class NormTail:

    def __init__(self, core, out, src, gain, shift):
        self.core, self.out, self.src, self.gain, self.shift_of = core, out, src, gain, shift
        self.scaled, self.ready = core.sem_g, core.sem_h

    def scale(self, dve):
        for k in range(DT):
            dve.scalar_tensor_tensor(out=self.out[:, k, :], in0=self.src[:, k, :], scalar=self.gain(k), in1=self.core.rstd[:, :],
                                     op0=ALU.mult, op1=ALU.mult).then_inc(self.scaled.sem, 1)

    def shift(self, act):
        for k in range(DT):
            act.wait_ge(self.scaled.sem, self.scaled.at(k + 1))
            act.activation(self.out[:, k, :], self.out[:, k, :], ACT.Identity, bias=self.shift_of(k)).then_inc(self.ready.sem, 1)

    def wait(self, pe, k):
        pe.wait_ge(self.ready.sem, self.ready.at(k + 1))

    def close(self):
        self.scaled.close(DT)
        self.ready.close(DT)

    def run(self):
        with self.core.block() as block:
            @block.vector
            def _(dve):
                self.scale(dve)

            @block.scalar
            def _(act):
                self.shift(act)
        self.close()


def linear(core, name, src, tiles, head=None, side=None, act_work=None, pool_work=None, sum_x=False, pe_work=None, source=None):
    nc = core.nc
    mine = []
    i = core.used
    while i < len(core.stream) and (core.stream[i][0] == name or side and core.stream[i][0].startswith("ada")):
        mine.append(i)
        i += 1
    assert mine, name
    own = [i for i in mine if core.stream[i][0] == name]
    kt = max(core.stream[i][2] + core.stream[i][3] for i in own)
    last_panel = {core.stream[i][1]: i for i in own}
    order = {}
    counts = {"act": 0, "dve": 0}
    for i, t in enumerate(tiles):
        counts[t[0]] += 1
        order[i] = (t[0], counts[t[0]])
    evac = {"act": core.act_evac, "dve": core.dve_evac}
    BANKS = 4

    def wait_tile(eng, i):
        which, n = order[i]
        eng.wait_ge(evac[which].sem, evac[which].at(n))

    def column_sum(pe, t):
        wait_tile(pe, t)
        pe.matmul(core.ps[:, 4, 0:TOK], core.m("ones"), core.x[:, t, :], start=(t == 0), stop=(t == DT - 1))

    with core.block() as block:
        @block.sync
        def _(sp):
            issue_panels(core, sp, mine[-1] + 1 + RING)

        @block.tensor
        def _(pe):
            for i in mine:
                panel, j, k0, kn = core.stream[i]
                slot = i % RING
                pe.wait_ge(core.panel_loaded[slot].sem, core.panel_loaded[slot].at(16 * (i // RING + 1)))
                if panel != name:
                    side(pe, j, core.ring[:, slot, :]).then_inc(core.panel_used.sem, 1)
                    continue
                for c in range(2):
                    t = 2 * j + c
                    if k0 == 0 and t >= BANKS:
                        wait_tile(pe, t - BANKS)
                    for k in range(kn):
                        if source is not None and i == mine[0] and c == 0:
                            source.wait(pe, k)
                        mm = pe.matmul(core.ps[:, t % BANKS, 0:TOK],
                                       core.ring[:, slot, k * PANEL + c * P:k * PANEL + c * P + P],
                                       src(k0 + k), start=(k0 + k == 0), stop=(k0 + k == kt - 1))
                mm.then_inc(core.panel_used.sem, 1)
                if pe_work is not None and k0 + kn == kt:
                    pe_work(pe, j, wait_tile)
                if sum_x and k0 + kn == kt and j > 0:
                    column_sum(pe, 2 * j - 2)
                    column_sum(pe, 2 * j - 1)
            if sum_x:
                column_sum(pe, DT - 2)
                column_sum(pe, DT - 1)

        def evacuations(eng, which):
            link = core.link(which, eng)
            for i, (e, take, after) in enumerate(tiles):
                if e != which:
                    continue
                eng.wait_ge(core.panel_used.sem, core.panel_used.at(last_panel[i // 2] + 1))
                take(eng, core.ps[:, i % BANKS, 0:TOK]).then_inc(evac[which].sem, 1)
                if after is not None:
                    after(eng, link, wait_tile)

        @block.scalar
        def _(act):
            if source is not None:
                source.shift(act)
            if act_work is not None:
                act_work(act)
            evacuations(act, "act")

        @block.vector
        def _(dve):
            if source is not None:
                source.scale(dve)
            if head is not None:
                head(dve, core.link("dve", dve))
            evacuations(dve, "dve")

        @block.gpsimd
        def _(pool):
            if pool_work is not None:
                pool_work(pool)
    core.used = mine[-1] + 1
    if source is not None:
        source.close()
    core.act_evac.close(counts["act"])
    core.dve_evac.close(counts["dve"])


def bcast(ap, shape):
    return ap.to_broadcast(shape)


def column_sums(core, jobs, then=None):
    with core.block() as block:
        @block.scalar
        def _(act):
            if then is not None:
                core.load_table(act, then)

        @block.tensor
        def _(pe):
            for out, mat, srcs in jobs:
                for n, s in enumerate(srcs):
                    pe.matmul(out, mat, s, start=(n == 0), stop=(n == len(srcs) - 1))


def rstd_of(core, ps, out, scale, eps):
    with core.block() as block:
        @block.vector
        def _(dve):
            dve.tensor_scalar(out, ps, scale, eps, ALU.mult, ALU.add).then_inc(core.sem_a.sem, 1)
            dve.wait_ge(core.sem_b.sem, core.sem_b.at(1))
            dve.reciprocal(out, out)

        @block.scalar
        def _(act):
            act.wait_ge(core.sem_a.sem, core.sem_a.at(1))
            act.activation(out, out, ACT.Sqrt).then_inc(core.sem_b.sem, 1)
    core.sem_a.close(1)
    core.sem_b.close(1)


def layer_norm(core, g, b, layer):
    x = core.x
    with ExitStack() as s:
        sq = s.enter_context(core.nc.sbuf_tensor(f"ln_sq_{g}{layer}", [P, DT, TOK], F32))
        with core.block() as block:
            @block.vector
            def _(dve):
                for h in range(2):
                    part = x[:, 4 * h:4 * h + 4, :]
                    dve.scalar_tensor_tensor(out=part, in0=bcast(core.ps[:, 4:5, 0:TOK], [P, 4, TOK]), scalar=-1.0 / D,
                                             in1=part, op0=ALU.mult, op1=ALU.add).then_inc(core.sem_a.sem, 1)

            @block.scalar
            def _(act):
                core.load_table(act, ACT.Sqrt)
                for h in range(2):
                    act.wait_ge(core.sem_a.sem, core.sem_a.at(h + 1))
                    for k in range(4 * h, 4 * h + 4, 2):
                        act.activation(sq[:, k:k + 2, :], x[:, k:k + 2, :], ACT.Square).then_inc(core.sem_b.sem, 1)

            @block.tensor
            def _(pe):
                for k in range(DT):
                    pe.wait_ge(core.sem_b.sem, core.sem_b.at(k // 2 + 1))
                    pe.matmul(core.ps[:, 5, 0:TOK], core.m("ones"), sq[:, k, :], start=(k == 0), stop=(k == DT - 1))
        core.sem_a.close(2)
        core.sem_b.close(4)
        rstd_of(core, core.ps[:, 5, 0:TOK], core.rstd[:, :], 1.0 / D, LN_EPS)
    return NormTail(core, x, x, lambda k: core.v(g, layer * DT + k), lambda k: core.v(b, layer * DT + k))


def residual_tiles(core, scale):
    def take(m):
        return lambda eng, ps: eng.scalar_tensor_tensor(out=core.x[:, m, :], in0=core.x[:, m, :], scalar=scale, in1=ps,
                                                        op0=ALU.mult, op1=ALU.add)
    return [("dve", take(m), None) for m in range(DT)]


def copy_tiles(core, dst, eng="act", func=None, bias=None, scale=1.0):
    def take(m):
        if eng == "dve":
            return lambda e, ps: e.tensor_copy(dst(m), ps)
        if bias is None:
            return lambda e, ps: e.activation(dst(m), ps, func or ACT.Copy, scale=scale)
        return lambda e, ps: e.activation(dst(m), ps, func or ACT.Identity, bias=bias(m), scale=scale)
    return take


def ffn(core, layer, norm=None):
    with ExitStack() as s:
        h = s.enter_context(core.nc.sbuf_tensor(f"ffn_h{layer}", [P, FF_T, TOK], F32))
        tiles = []
        for j in range(FF_T):
            def gate(e, ps, j=j):
                return e.activation(h[:, j, :], ps, ACT.Silu)

            def up(e, ps, j=j):
                e.wait_ge(core.act_evac.sem, core.act_evac.at(j + 1))
                return e.tensor_tensor(h[:, j, :], h[:, j, :], ps, ALU.mult)
            tiles += [("act", gate, None), ("dve", up, None)]
        name, out, bias = (("ada2", core.mod2, "ada_b_2"), ("ada3", core.mod3, "b_ada_3"))[layer]
        linear(core, f"ffn_up{layer}", lambda k: core.x[:, k, :], tiles,
               side=modulation_side(core, layer, out.shape[-1] // 2), source=norm)
        finish_modulation(core, name, out, core.vs(bias))
        linear(core, f"ffn_dn{layer}", lambda k: h[:, k, :], residual_tiles(core, ALPHA), sum_x=True)
    return layer_norm(core, "ln_ffn_g", "ln_ffn_b", layer)


def per_layer_embedding(core, layer, norm=None):
    nc = core.nc
    with ExitStack() as s:
        gate = s.enter_context(nc.sbuf_tensor(f"ple_gate{layer}", [P, DT, TOK], F32))
        pt = s.enter_context(nc.sbuf_tensor(f"ple_p{layer}_sb", [P, 2, TOK], F32))
        take = copy_tiles(core, lambda m: gate[:, m, :], func=ACT.Sigmoid, bias=lambda m: core.v("b_ple", layer * DT + m))
        with core.block() as block:
            @block.scalar
            def _(act):
                act.dma_start(pt[:, :, :], core.a["p"][layer]).then_inc(core.const_loaded.sem, 16)
        linear(core, f"ple_g{layer}", lambda k: core.x[:, k, :], [("act", take(m), None) for m in range(DT)],
               source=norm)
        with core.block() as block:
            @block.scalar
            def _(act):
                act.wait_ge(core.const_loaded.sem, core.const_loaded.at(16))
        core.const_loaded.close(16)
        tiles = []
        for m in range(DT):
            def take(e, ps, m=m):
                return e.tensor_tensor(gate[:, m, :], gate[:, m, :], ps, ALU.mult)

            def after(e, link, wait_tile, m=m):
                wait_tile(e, m)
                link(e.tensor_tensor(core.x[:, m, :], core.x[:, m, :], gate[:, m, :], ALU.add))
            tiles.append(("dve", take, after))
        linear(core, f"ple_p{layer}", lambda k: pt[:, k, :], tiles)


def ssd_layer(core):
    nc, ps = core.nc, core.ps
    with ExitStack() as s:
        def sb(name, shape):
            return s.enter_context(nc.sbuf_tensor(name, shape, F32))
        y_sc = sb("y_sc", [P, DT, TOK])
        z = sb("z_gate", [P, DT, TOK])
        xbc = sb("xbc", [P, XBC_T, TOK])
        dt = sb("dt16", [16, TOK])
        acs = sb("acs16", [16, TOK])
        dte = sb("dte16", [16, SSD_CHUNK])
        with ExitStack() as s2:
            xbp = s2.enter_context(nc.sbuf_tensor("xbc_pad", [P, 2, TOK + 4], F32))
            scp = s2.enter_context(nc.sbuf_tensor("sc_pad", [P, DT, TOK + 4], F32))
            dtw = s2.enter_context(nc.sbuf_tensor("dt_w", [P, DT, 16], F32))
            acc = s2.enter_context(nc.sbuf_tensor("conv_acc", [P, TOK], F32))
            ab = s2.enter_context(nc.sbuf_tensor("dt_abs", [16, TOK], F32))
            with core.block() as block:
                @block.scalar
                def _(act):
                    act.dma_start(dtw[:, :, :], core.a["w_dt"]).then_inc(core.const_loaded.sem, 16)

                @block.sync
                def _(sp):
                    sp.wait_ge(core.const_loaded.sem, core.const_loaded.at(16))
                    issue_panels(core, sp, RING)

                @block.vector
                def _(dve):
                    dve.memset(xbp[:, :, 0:4], 0.0)
                    dve.memset(scp[:, :, 0:4], 0.0)

                @block.tensor
                def _(pe):
                    pe.wait_ge(core.const_loaded.sem, core.const_loaded.at(16))
                    for k in range(DT):
                        pe.matmul(ps[0:16, 7, 0:TOK], dtw[:, k, :], core.x[:, k, :], start=(k == 0), stop=(k == DT - 1))
            core.const_loaded.close(16)

            tiles = []
            for t in range(XBC_T):
                def take(e, p_, t=t):
                    if t >= 2:
                        e.wait_ge(core.sem_c.sem, core.sem_c.at(t - 1))
                    return e.activation(xbp[:, t % 2, 4:4 + TOK], p_, ACT.Copy)
                tiles.append(("act", take, None))
            for t in range(DT):
                tiles.append(("act", copy_tiles(core, lambda m: scp[:, m, 4:4 + TOK])(t), None))
            for t in range(DT):
                def take(e, p_, t=t):
                    e.wait_ge(core.act_evac.sem, core.act_evac.at(XBC_T + t + 1))
                    return e.tensor_tensor(scp[:, t, 4:4 + TOK], scp[:, t, 4:4 + TOK], p_, ALU.mult)
                tiles.append(("dve", take, None))
            for t in range(DT):
                def take(e, p_, t=t):
                    return e.tensor_tensor(y_sc[:, t, :], y_sc[:, t, :], p_, ALU.mult)
                tiles.append(("dve", take, None))
            for t in range(DT):
                tiles.append(("act", copy_tiles(core, lambda m: z[:, m, :], func=ACT.Silu)(t), None))

            def conv(link, dve, dst, src, w, n, bias=None):
                if bias is None:
                    link(dve.tensor_scalar(dst, src[:, 4:4 + TOK], w(n - 1), None, ALU.mult))
                else:
                    link(dve.tensor_scalar(dst, src[:, 4:4 + TOK], w(n - 1), bias, ALU.mult, ALU.add))
                for i in range(n - 1):
                    lag = n - 1 - i
                    link(dve.scalar_tensor_tensor(out=dst, in0=src[:, 4 - lag:4 - lag + TOK], scalar=w(i), in1=dst,
                                                  op0=ALU.mult, op1=ALU.add))

            def conv_xbc(e, link, t):
                e.wait_ge(core.act_evac.sem, core.act_evac.at(t + 1))
                conv(link, e, xbc[:, t, :], xbp[:, t % 2, :], lambda i: core.v("conv_w", i * XBC_T + t), SSD_CONV,
                     core.v("conv_b", t))

            def conv_sc(e, link, wait_tile, t):
                wait_tile(e, XBC_T + DT + t)
                conv(link, e, y_sc[:, t, :], scp[:, t, :], lambda i: core.v("sc_w", i * DT + t), SC_CONV)
            for t in range(DT):
                i = XBC_T + DT + t
                e_, take_, _ = tiles[i]
                tiles[i] = (e_, take_, lambda e, link, wt, t=t: conv_sc(e, link, wt, t))

            def head(dve, link):
                for t in range(XBC_T):
                    conv_xbc(dve, link, t)
                    dve.sem_inc(core.sem_c.sem, 1)

            dt_done, decay_done = core.sem_e, core.sem_f

            def activations(act, link, wait_tile):
                act.wait_ge(core.sem_c.sem, core.sem_c.at(XBC_T))
                link(act.activation(xbc[:, :, :], xbc[:, :, :], ACT.Silu))
                link(act.activation(dt[:, :], ps[0:16, 7, 0:TOK], ACT.Identity, bias=core.v("dt_bias", 0, 16)))
                link(act.activation(ab[:, :], dt[:, :], ACT.Abs))
                link(act.activation(ab[:, :], ab[:, :], ACT.Exp, scale=-1.0))
                link(act.activation(acc[0:16, 0:1], core.v("a_log", 0, 16), ACT.Exp))
                act.activation(ab[:, :], ab[:, :], ACT.Ln, bias=1.0).then_inc(dt_done.sem, 1)

            def decays(dve, link, wait_tile):
                dve.wait_ge(dt_done.sem, dt_done.at(1))
                link(dve.scalar_tensor_tensor(out=dt[:, :], in0=dt[:, :], scalar=0.0, in1=ab[:, :], op0=ALU.max,
                                              op1=ALU.add))
                link(dve.tensor_scalar(ab[:, :], dt[:, :], acc[0:16, 0:1], -1.0, ALU.mult, ALU.mult))
                for c in range(NB):
                    link(dve.tensor_tensor_scan(acs[:, c * P:c * P + P], core.m("ones")[0:16, :],
                                                ab[:, c * P:c * P + P], 0.0, ALU.mult, ALU.add))
                dve.sem_inc(decay_done.sem, 1)

            def to_end(act, link, wait_tile):
                act.wait_ge(decay_done.sem, decay_done.at(1))
                act.activation(dte[:, :], acs[:, 0:P], ACT.Exp, scale=-1.0, bias=acs[:, P - 1:P])
            for i, after in ((XBC_T + DT - 1, activations), (XBC_T + 3 * DT - 1, decays), (XBC_T + 3 * DT, to_end)):
                assert tiles[i][2] is None
                tiles[i] = (tiles[i][0], tiles[i][1], after)
            linear(core, "w_in", lambda k: core.x[:, k, :], tiles, head=head)
            core.sem_c.close(XBC_T)
            dt_done.close(1)
            decay_done.close(1)
        xdt = sb("xdt", [P, NB, SSD_HEADS, HD])
        xde = sb("xde", [P, SSD_HEADS, HD])
        cols = sb("ssd_cols", [P, 5, 16])
        btok = sb("btok", [P, SSD_GROUPS, P])
        cbm = sb("cbm", [P, SSD_GROUPS * NB, P])
        hst = sb("h_state", [P, SSD_GROUPS, HPG * HD])
        ident = core.m("ident")
        with core.block() as block:
            @block.tensor
            def _(pe):
                for n, src in enumerate([dt[:, 0:P], dt[:, P:2 * P], acs[:, 0:P], acs[:, P:2 * P], dte[:, :]]):
                    pe.transpose(ps[:, 6, 16 * n:16 * n + 16], src, ident[0:16, 0:16])
                for g in range(SSD_GROUPS):
                    pe.transpose(ps[:, 7, g * P:g * P + P], xbc[:, 8 + g, 0:P], ident)
                for c in range(NB):
                    for t in range(DT):
                        n = c * DT + t
                        pe.transpose(ps[:, n // 4, (n % 4) * P:(n % 4) * P + P], xbc[:, t, c * P:c * P + P], ident)
                for g in range(SSD_GROUPS):
                    for c in range(NB):
                        n = g * NB + c
                        pe.matmul(ps[:, 5, n * P:n * P + P], xbc[:, 8 + g, c * P:c * P + P],
                                  xbc[:, 10 + g, c * P:c * P + P], start=True, stop=True)
        with core.block() as block:
            @block.vector
            def _(dve):
                link = core.link("dve", dve)
                link(dve.tensor_copy(cols[:, :, :], ps[:, 6, 0:80].rearrange("p (a b) -> p a b", b=16)))
                for c in range(NB):
                    for q in range(2):
                        link(dve.tensor_tensor(xdt[:, c, 8 * q:8 * q + 8, :],
                                               ps[:, 2 * c + q, :].rearrange("p (h d) -> p h d", d=HD),
                                               bcast(cols[:, c, 8 * q:8 * q + 8].unsqueeze(2), [P, 8, HD]), ALU.mult))
                link(dve.tensor_tensor(xde[:, :, :], xdt[:, 0, :, :],
                                       bcast(cols[:, 4, :].unsqueeze(2), [P, SSD_HEADS, HD]), ALU.mult))
                link(dve.tensor_tensor(cbm[:, :, :], ps[:, 5, :].rearrange("p (a b) -> p a b", b=P),
                                       bcast(core.m("tri_le").unsqueeze(1), [P, 4, P]), ALU.mult))

            @block.scalar
            def _(act):
                act.activation(btok[:, :, :], ps[:, 7, 0:2 * P].rearrange("p (a b) -> p a b", b=P), ACT.Copy)
        with core.block() as block:
            @block.tensor
            def _(pe):
                for g in range(SSD_GROUPS):
                    pe.matmul(ps[:, g, :], btok[:, g, :], xde[:, g * HPG:g * HPG + HPG, :], start=True, stop=True)
        with core.block() as block:
            @block.vector
            def _(dve):
                dve.tensor_copy(hst[:, :, :], ps[:, 0:2, :])
        seg = sb("seg", [P, 2, TOK])
        ex = sb("seg_exp", [P, 2, TOK + P])
        wl = sb("w_local", [P, 2, TOK + P])
        bc_ready, seg_ready, exp_ready, w_ready, y_ready = core.sem_a, core.sem_b, core.sem_c, core.sem_d, core.sem_e
        y_taken, xd = core.sem_f, xbc
        with core.block() as block:
            @block.tensor
            def _(pe):
                def spread(h):
                    if h >= 2:
                        pe.wait_ge(seg_ready.sem, seg_ready.at(h - 1))
                        pe.wait_ge(exp_ready.sem, exp_ready.at(h - 1))
                    pe.matmul(ps[:, h % 2, 0:TOK], bcast(ident[0:16, h:h + 1], [16, P]), acs[:, :], start=True,
                              stop=True).then_inc(bc_ready.sem, 1)
                spread(0)
                for h in range(SSD_HEADS):
                    if h + 1 < SSD_HEADS:
                        spread(h + 1)
                    pe.wait_ge(w_ready.sem, w_ready.at(h + 1))
                    j, o = h // 2, HD * (h % 2)
                    if h % 2 == 0 and j >= 2:
                        pe.wait_ge(y_taken.sem, y_taken.at(j - 1))
                    out = ps[o:o + HD, 2 + j % 2, :]
                    w = wl[:, h % 2, :]
                    pe.matmul(out[:, 0:P], xdt[:, 0, h, :], w[:, 0:P], start=True, stop=True)
                    pe.matmul(out[:, P:TOK], xdt[:, 1, h, :], w[:, P:TOK], start=True, stop=False)
                    pe.matmul(out[:, P:TOK], hst[:, h // HPG, (h % HPG) * HD:(h % HPG) * HD + HD], w[:, TOK:TOK + P],
                              start=False, stop=True).then_inc(y_ready.sem, 1)

            @block.vector
            def _(dve):
                link = core.link("dve", dve)

                def y_out(j):
                    dve.wait_ge(y_ready.sem, y_ready.at(2 * j + 2))
                    link(dve.scalar_tensor_tensor(out=xd[:, j, :], in0=xd[:, j, :], scalar=core.v("ssd_d", j),
                                                  in1=ps[:, 2 + j % 2, 0:TOK], op0=ALU.mult, op1=ALU.add))
                    dve.sem_inc(y_taken.sem, 1)
                    link(dve.tensor_tensor(xd[:, j, :], xd[:, j, :], z[:, j, :], ALU.mult))
                for h in range(SSD_HEADS):
                    dve.wait_ge(bc_ready.sem, bc_ready.at(h + 1))
                    if h >= 2:
                        dve.wait_ge(exp_ready.sem, exp_ready.at(h - 1))
                    for c in range(NB):
                        ins = dve.tensor_scalar(seg[:, h % 2, c * P:c * P + P], ps[:, h % 2, c * P:c * P + P],
                                                cols[:, 2 + c, h:h + 1], 0.0, ALU.subtract, ALU.min)
                    ins.then_inc(seg_ready.sem, 1)
                    if h >= 3 and h % 2 == 1:
                        y_out((h - 3) // 2)
                y_out(SSD_HEADS // 2 - 1)

            @block.scalar
            def _(act):
                for h in range(SSD_HEADS):
                    act.wait_ge(seg_ready.sem, seg_ready.at(h + 1))
                    if h >= 2:
                        act.wait_ge(w_ready.sem, w_ready.at(h - 1))
                    act.activation(ex[:, h % 2, 0:TOK], seg[:, h % 2, :], ACT.Exp)
                    act.activation(ex[:, h % 2, TOK:TOK + P], ps[:, h % 2, P:TOK], ACT.Exp).then_inc(exp_ready.sem, 1)

            @block.gpsimd
            def _(pool):
                for h in range(SSD_HEADS):
                    g = h // HPG
                    pool.wait_ge(exp_ready.sem, exp_ready.at(h + 1))
                    if h >= 2:
                        pool.wait_ge(y_ready.sem, y_ready.at(h - 1))
                    pool.tensor_tensor(wl[:, h % 2, 0:TOK], ex[:, h % 2, 0:TOK],
                                       cbm[:, g * NB:g * NB + NB, :].rearrange("p a b -> p (a b)"), ALU.mult)
                    pool.tensor_tensor(wl[:, h % 2, TOK:TOK + P], ex[:, h % 2, TOK:TOK + P],
                                       xbc[:, 10 + g, P:TOK], ALU.mult).then_inc(w_ready.sem, 1)
        for sig in (bc_ready, seg_ready, exp_ready, w_ready, y_ready):
            sig.close(SSD_HEADS)
        y_taken.close(SSD_HEADS // 2)
        with core.block() as block:
            @block.scalar
            def _(act):
                act.activation(z[:, :, :], xd[:, 0:DT, :], ACT.Square)
        column_sums(core, [(ps[:, 4 + g, 0:TOK], core.m("ones"), [z[:, 4 * g + k, :] for k in range(4)])
                           for g in range(SSD_GROUPS)])
        rstd = seg[:, :, :]
        rstd_of(core, ps[:, 4:6, 0:TOK], rstd, 1.0 / (SSD_HEADS * HD // SSD_GROUPS), 1e-5)
        with core.block() as block:
            @block.vector
            def _(dve):
                for t in range(DT):
                    dve.scalar_tensor_tensor(out=xd[:, t, :], in0=xd[:, t, :], scalar=core.v("ssd_norm", t),
                                             in1=rstd[:, t // 4, :], op0=ALU.mult, op1=ALU.mult)
        linear(core, "w_out", lambda k: xd[:, k, :] if k < DT else y_sc[:, k - DT, :], residual_tiles(core, ALPHA), sum_x=True)
    return layer_norm(core, "ln_mix_g", "ln_mix_b", 0)


def to_token_major(core, srcs, dst):
    ps, ident = core.ps, core.m("ident")
    jobs = [(t, b) for t in range(len(srcs)) for b in range(NB)]
    for first in range(0, len(jobs), 16):
        part = jobs[first:first + 16]
        with core.block() as block:
            @block.tensor
            def _(pe):
                for n, (t, b) in enumerate(part):
                    pe.transpose(ps[:, n // 4, (n % 4) * P:(n % 4) * P + P], srcs[t][:, b * P:b * P + P],
                                 ident).then_inc(core.sem_a.sem, 1)

            @block.scalar
            def _(act):
                for n, (t, b) in enumerate(part):
                    if n // 4 % 2 == 0:
                        act.wait_ge(core.sem_a.sem, core.sem_a.at(min(len(part), n // 4 * 4 + 4)))
                        act.activation(dst(t, b), ps[:, n // 4, (n % 4) * P:(n % 4) * P + P], ACT.Copy)

            @block.vector
            def _(dve):
                for n, (t, b) in enumerate(part):
                    if n // 4 % 2 == 1:
                        dve.wait_ge(core.sem_a.sem, core.sem_a.at(min(len(part), n // 4 * 4 + 4)))
                        dve.tensor_copy(dst(t, b), ps[:, n // 4, (n % 4) * P:(n % 4) * P + P])
        core.sem_a.close(len(part))


def softmax_attention(core, name, heads, q, k, v, mask, scale, take, sinks=None):
    nc, ps, ident = core.nc, core.ps, core.m("ident")
    scored, shifted, exped, normed, turned, copied, summed = (
        core.sem_a, core.sem_b, core.sem_c, core.sem_d, core.sem_e, core.sem_f, core.sem_g)
    inverted, normed_late = core.sem_h, core.chain["pool"]
    H, W = len(heads), 3 * P
    with ExitStack() as s:
        prob = s.enter_context(nc.sbuf_tensor(f"{name}_prob", [P, 3, W], F32))
        pt = s.enter_context(nc.sbuf_tensor(f"{name}_pt", [P, 2, W], F32))
        st = s.enter_context(nc.sbuf_tensor(f"{name}_st", [P, 3, 8], F32))
        spans, score_bank = [(0, P), (P, W)], (0, 1, 6)

        with core.block() as block:
            @block.tensor
            def _(pe):
                def scores(i):
                    if i >= 3:
                        pe.wait_ge(shifted.sem, shifted.at(i - 2))
                    h = heads[i]
                    pe.matmul(ps[:, score_bank[i % 3], 0:P], q(h)[:, 0:P], k(h)[:, 0:P], start=True, stop=True)
                    pe.matmul(ps[:, score_bank[i % 3], P:W], q(h)[:, P:TOK], k(h), start=True,
                              stop=True).then_inc(scored.sem, 1)

                def turn(i):
                    pe.wait_ge(normed.sem, normed.at(i + 1))
                    pe.wait_ge(normed_late.sem, normed_late.at(i + 1))
                    if i >= 2:
                        pe.wait_ge(copied.sem, copied.at(i - 1))
                    for n in range(3):
                        t = pe.transpose(ps[:, 2 + i % 2, n * P:n * P + P], prob[:, i % 3, n * P:n * P + P], ident)
                    t.then_inc(turned.sem, 1)

                def weigh(i):
                    pe.wait_ge(copied.sem, copied.at(i + 1))
                    if i % 2 == 0 and i >= 4:
                        pe.wait_ge(core.dve_evac.sem, core.dve_evac.at(i // 2 - 1))
                    o = HD * (i % 2)
                    out = ps[o:o + HD, 4 + i // 2 % 2, :]
                    p = pt[:, i % 2, :]
                    pe.matmul(out[:, 0:P], v(heads[i], 0), p[:, 0:P], start=True, stop=True)
                    pe.matmul(out[:, P:TOK], v(heads[i], 0), p[:, P:2 * P], start=True, stop=False)
                    pe.matmul(out[:, P:TOK], v(heads[i], 1), p[:, 2 * P:W], start=False, stop=True).then_inc(summed.sem, 1)
                for i in range(3):
                    scores(i)
                for i in range(H + 1):
                    if i < H:
                        turn(i)
                    if i + 3 < H:
                        scores(i + 3)
                    if i >= 1:
                        weigh(i - 1)

            @block.vector
            def _(dve):
                turn = core.chain["dve"]

                def mark(ins):
                    ins.then_inc(turn.sem, 1)
                    turn.base += 1
                    return turn.base

                def step(i):
                    new, old = i < H, i >= 1
                    pr, t = prob[:, i % 3, :], st[:, i % 3, :]
                    pr1, t1 = prob[:, (i - 1) % 3, :], st[:, (i - 1) % 3, :]
                    if new:
                        dve.wait_ge(scored.sem, scored.at(i + 1))
                        if i >= 3:
                            dve.wait_ge(turned.sem, turned.at(i - 2))
                        masked = mark(dve.scalar_tensor_tensor(out=pr, in0=ps[:, score_bank[i % 3], 0:W], scalar=scale,
                                                               in1=core.m(mask, 0, W), op0=ALU.mult, op1=ALU.add))
                        dve.wait_ge(turn.sem, masked)
                        for b, (lo, hi) in enumerate(spans):
                            largest = mark(dve.tensor_reduce(t[:, b:b + 1], pr[:, lo:hi], AX, ALU.max))
                    if old:
                        dve.wait_ge(exped.sem, exped.at(i))
                        if sinks is not None:
                            dve.wait_ge(turn.sem, mark(dve.tensor_tensor(t1[:, 4:6], t1[:, 4:6], t1[:, 6:8], ALU.add)))
                        dve.reciprocal(t1[:, 4:6], t1[:, 4:6]).then_inc(inverted.sem, 1)
                    if new:
                        dve.wait_ge(turn.sem, largest)
                        if sinks is None:
                            ins = dve.tensor_scalar(t[:, 2:4], t[:, 0:2], -1.0, None, ALU.mult)
                        else:
                            ins = dve.tensor_scalar(t[:, 2:4], t[:, 0:2], sinks(heads[i]), -1.0, ALU.max, ALU.mult)
                        ins.then_inc(shifted.sem, 1)
                    if old:
                        dve.wait_ge(inverted.sem, inverted.at(i))
                        lo, hi = spans[1]
                        dve.tensor_scalar(pr1[:, lo:hi], pr1[:, lo:hi], t1[:, 5:6], None, ALU.mult).then_inc(normed_late.sem, 1)

                def store(j):
                    dve.wait_ge(summed.sem, summed.at(2 * j + 2))
                    take(dve, j, ps[:, 4 + j % 2, 0:TOK]).then_inc(core.dve_evac.sem, 1)
                for i in range(H + 3):
                    if i <= H:
                        step(i)
                    if i >= 4 and i % 2 == 0:
                        store((i - 4) // 2)

            @block.scalar
            def _(act):
                def exponentials(i):
                    pr, t = prob[:, i % 3, :], st[:, i % 3, :]
                    act.wait_ge(shifted.sem, shifted.at(i + 1))
                    for b, (lo, hi) in enumerate(spans):
                        ins = act.activation(pr[:, lo:hi], pr[:, lo:hi], ACT.Exp, bias=t[:, 2 + b:3 + b],
                                             accum_out=t[:, 4 + b:5 + b])
                    if sinks is not None:
                        ins = act.activation(t[:, 6:8], t[:, 2:4], ACT.Exp, bias=sinks(heads[i]))
                    ins.then_inc(exped.sem, 1)

                def normalise(i):
                    pr, t = prob[:, i % 3, :], st[:, i % 3, :]
                    act.wait_ge(inverted.sem, inverted.at(i + 1))
                    lo, hi = spans[0]
                    act.activation(pr[:, lo:hi], pr[:, lo:hi], ACT.Copy, scale=t[:, 4:5]).then_inc(normed.sem, 1)

                def copy(i):
                    act.wait_ge(turned.sem, turned.at(i + 1))
                    if i >= 2:
                        act.wait_ge(summed.sem, summed.at(i - 1))
                    act.activation(pt[:, i % 2, :], ps[:, 2 + i % 2, 0:W], ACT.Copy).then_inc(copied.sem, 1)
                for i in range(H + 2):
                    if i < H:
                        exponentials(i)
                    if 1 <= i <= H:
                        normalise(i - 1)
                    if i >= 2:
                        copy(i - 2)
        for sig in (scored, shifted, exped, inverted, normed, normed_late, turned, copied, summed):
            sig.close(H)
        core.dve_evac.close(H // 2)


def pad_keys(core, keys, dst):
    with core.block() as block:
        @block.gpsimd
        def _(pool):
            for half in range(2):
                other = slice(HD * (1 - half), HD * (1 - half) + HD)
                ins = pool.memset(dst[other, half::2, :], 0.0)
            ins.then_inc(core.sem_a.sem, 1)

        @block.vector
        def _(dve):
            dve.wait_ge(core.sem_a.sem, core.sem_a.at(1))

        @block.scalar
        def _(act):
            for half in range(2):
                own = slice(HD * half, HD * half + HD)
                act.activation(dst[own, half::2, :], keys[own, :, :], ACT.Copy)
    core.sem_a.close(1)


def attention_layer(core):
    nc = core.nc
    with ExitStack() as s:
        qkv = s.enter_context(nc.sbuf_tensor("swa_qkv", [P, 12, TOK], F32))
        vt = s.enter_context(nc.sbuf_tensor("swa_v", [P, NB, 2 * P], F32))
        o = s.enter_context(nc.sbuf_tensor("swa_o", [P, DT, TOK], F32))
        kz = s.enter_context(nc.sbuf_tensor("swa_kz", [P, 4, TOK], F32))
        take = copy_tiles(core, lambda m: qkv[:, m, :], bias=lambda m: core.v("b_qkv", m))
        linear(core, "qkv", lambda k: core.x[:, k, :], [("act", take(m), None) for m in range(12)])
        pad_keys(core, qkv[:, 8:10, :], kz)
        to_token_major(core, [qkv[:, 10 + t, :] for t in range(2)], lambda t, b: vt[:, b, t * P:t * P + P])

        def kv_of(u):
            return 2 * (u // 2 // 4) + u % 2

        def sink(u):
            return core.v("sinks", 8 * (u // 8) + 4 * (u % 2) + u // 2 % 4)
        softmax_attention(core, "swa", range(16), lambda u: qkv[:, u // 2, :], lambda u: kz[:, kv_of(u), :],
                          lambda u, b: vt[:, b, HD * kv_of(u):HD * kv_of(u) + HD], "band", HD ** -0.5,
                          lambda e, j, p: e.tensor_copy(o[:, j, :], p), sink)
        tiles = []
        for m in range(DT):
            def take(e, p, m=m):
                return e.tensor_tensor(core.x[:, m, :], core.x[:, m, :], p, ALU.add)
            tiles.append(("dve", take, None))

        def scaled(dve, link):
            for m in range(DT):
                link(dve.tensor_scalar(core.x[:, m, :], core.x[:, m, :], ALPHA, core.v("b_o", m), ALU.mult, ALU.add))
        linear(core, "w_o", lambda k: o[:, k, :], tiles, head=scaled, sum_x=True)
    return layer_norm(core, "ln_mix_g", "ln_mix_b", 1)


def start_modulation(core, s):
    core.cond = s.enter_context(core.nc.sbuf_tensor("cond", [P, 2, DT, 63], F32))
    with core.block() as block:
        @block.vector
        def _(dve):
            dve.memset(core.cond[:, :, :, :], 0.0)
    with core.block() as block:
        @block.scalar
        def _(act):
            for i, c in enumerate(("c_2", "c_3")):
                act.activation(core.cond[:, i, :, 31], core.vs(c), ACT.Silu)


def modulation_side(core, which, count):
    def side(pe, j, w):
        for k in range(DT):
            t = k % 4
            mm = pe.matmul(core.ps[32 * t:32 * t + 32, 7, 0:PANEL], core.cond[:, which, k, 31 - j:63 - j],
                           w[:, k * PANEL:k * PANEL + PANEL], start=(j == 0 and k < 4), stop=(j == count - 1 and k >= 4))
        return mm
    return side


def finish_modulation(core, name, out, bias):
    ps, n = core.ps, out.shape[-1] // 2
    with ExitStack() as s:
        rows = s.enter_context(core.nc.sbuf_tensor(f"{name}_rows", [P, PANEL], F32))
        with core.block() as block:
            @block.vector
            def _(dve):
                dve.tensor_copy(rows[:, :], ps[:, 7, 0:PANEL])
        with core.block() as block:
            @block.tensor
            def _(pe):
                for c in range(2):
                    pe.matmul(ps[:, 6, c * 32:c * 32 + 32], rows[:, c * P:c * P + P], core.m("fold"), start=True, stop=True)
        with core.block() as block:
            @block.vector
            def _(dve):
                for c in range(2):
                    dve.tensor_tensor(out[:, c::2], ps[:, 6, c * 32:c * 32 + n], bias[:, c::2], ALU.add)


def rms_modulate(core, out, g, scale, shift):
    x = core.x
    gs = core.gain
    with core.block() as block:
        @block.scalar
        def _(act):
            core.load_table(act, ACT.Sqrt)
            for k in range(DT):
                act.activation(out[:, k, :], x[:, k, :], ACT.Square).then_inc(core.sem_a.sem, 1)

        @block.tensor
        def _(pe):
            for k in range(DT):
                pe.wait_ge(core.sem_a.sem, core.sem_a.at(k + 1))
                pe.matmul(core.ps[:, 4, 0:TOK], core.m("ones"), out[:, k, :], start=(k == 0), stop=(k == DT - 1))

        @block.vector
        def _(dve):
            dve.scalar_tensor_tensor(out=gs[:, :], in0=scale, scalar=1.0, in1=g, op0=ALU.add, op1=ALU.mult)
    core.sem_a.close(DT)
    rstd_of(core, core.ps[:, 4, 0:TOK], core.rstd[:, :], 1.0 / D, RMS_EPS)
    return NormTail(core, out, x, lambda k: gs[:, k:k + 1], lambda k: shift[:, k:k + 1])


def head_sums(core, bank, src, tiles):
    column_sums(core, [(core.ps[:, bank + t // 2, (t % 2) * TOK:(t % 2) * TOK + TOK], core.m("head_ones"), [src[:, t, :]])
                       for t in range(tiles)])
    return core.ps[:, bank:bank + (tiles + 1) // 2, :].rearrange("p a (b n) -> p (a b) n", n=TOK)


def head_scales(core, name, groups, scale, add, floor=None):
    ps, n = core.ps, len(groups) * TOK
    with ExitStack() as s:
        comp = s.enter_context(core.nc.sbuf_tensor(f"{name}_scales", [P, n], F32))
        with core.block() as block:
            @block.scalar
            def _(act):
                core.load_table(act, ACT.Sqrt)

            @block.tensor
            def _(pe):
                for g, src in enumerate(groups):
                    for t in range(4):
                        pe.matmul(ps[32 * t:32 * t + 32, 4, g * TOK:g * TOK + TOK], core.m("head_cols"), src[:, t, :],
                                  start=True, stop=True)
        if floor is None:
            rstd_of(core, ps[:, 4, 0:n], comp[:, :], scale, add)
        else:
            with core.block() as block:
                @block.scalar
                def _(act):
                    act.activation(comp[:, :], ps[:, 4, 0:n], ACT.Sqrt)
            with core.block() as block:
                @block.vector
                def _(dve):
                    link = core.link("dve", dve)
                    link(dve.tensor_scalar(comp[:, :], comp[:, :], floor, None, ALU.max))
                    link(dve.reciprocal(comp[:, :], comp[:, :]))
        with core.block() as block:
            @block.tensor
            def _(pe):
                for t in range(4):
                    pe.matmul(ps[:, t, 0:n], core.m("spread", t, P), comp[:, :], start=True, stop=True)
    return [ps[:, 0:4, g * TOK:g * TOK + TOK] for g in range(len(groups))]


def stick_breaking(core, q, k, v, o):
    nc, ps = core.nc, core.ps
    H, W = 8, 3 * P
    scale = HD ** -0.5
    with ExitStack() as s:
        def sb(name, shape):
            return s.enter_context(nc.sbuf_tensor("stick_" + name, shape, F32))
        sq, vt = sb("sq", [P, 8, TOK]), sb("vt", [P, NB, 4 * P])
        halves = [sq[:, 0:4, :], sq[:, 4:8, :]]
        with core.block() as block:
            @block.scalar
            def _(act):
                for part, t in zip(halves, (q, k)):
                    act.activation(part, t, ACT.Square)
        scales = head_scales(core, "stick_qk", halves, 1.0 / HD, RMS_EPS)
        with core.block() as block:
            @block.vector
            def _(dve):
                for t, g, rs in zip((q, k), ("q_norm", "k_norm"), scales):
                    dve.scalar_tensor_tensor(out=t, in0=t, scalar=core.v(g), in1=rs, op0=ALU.mult, op1=ALU.mult)
        to_token_major(core, [v[:, t, :] for t in range(4)], lambda t, b: vt[:, b, t * P:t * P + P])
        lg, ln, lk = sb("logit", [P, H, W]), sb("log", [P, H, W]), sb("keep", [P, H, W])
        mask = sb("mask", [P, W])
        scored, logged, kept, masked, between, weight, exped, final = (
            core.sem_a, core.sem_b, core.sem_c, core.sem_d, core.sem_e, core.sem_f, core.sem_g, core.sem_h)
        done, scaled = core.act_evac, core.chain["pe"]
        score_bank = (0, 1, 6, 7)
        with core.block() as block:
            @block.vector
            def _(dve):
                dve.tensor_copy(mask[:, 0:P], core.m("tri_lt"))
                dve.tensor_copy(mask[:, P:2 * P], core.m("ones"))
                dve.tensor_copy(mask[:, 2 * P:W], core.m("tri_lt"))
        with core.block() as block:
            def rows_of(h):
                return slice(HD * (h % 2), HD * (h % 2) + HD)

            @block.tensor
            def _(pe):
                def score(h):
                    if h >= 4:
                        pe.wait_ge(scaled.sem, scaled.at(h - 3))
                    r, t = rows_of(h), h // 2
                    pe.matmul(ps[:, score_bank[h % 4], 0:TOK], k[r, t, 0:P], q[r, t, :], start=True, stop=True)
                    pe.matmul(ps[:, score_bank[h % 4], TOK:W], k[r, t, P:TOK], q[r, t, P:TOK], start=True,
                              stop=True).then_inc(scored.sem, 1)

                def suffix(h):
                    pe.wait_ge(masked.sem, masked.at(h + 1))
                    if h >= 2:
                        pe.wait_ge(weight.sem, weight.at(h - 1))
                    out = ps[:, 2 + h % 2, :]
                    pe.matmul(out[:, 0:TOK], core.m("tri_gt"), lk[:, h, 0:TOK], start=True, stop=False)
                    pe.matmul(out[:, P:TOK], core.m("ones"), lk[:, h, TOK:W], start=False, stop=True)
                    pe.matmul(out[:, TOK:W], core.m("tri_gt"), lk[:, h, TOK:W], start=True, stop=True).then_inc(between.sem, 1)

                def weigh(h):
                    pe.wait_ge(final.sem, final.at(h + 1))
                    if h % 2 == 0 and h >= 4:
                        pe.wait_ge(core.dve_evac.sem, core.dve_evac.at(h // 2 - 1))
                    out = ps[HD * (h % 2):HD * (h % 2) + HD, 4 + h // 2 % 2, :]
                    pe.matmul(out[:, 0:TOK], vt[:, 0, HD * h:HD * h + HD], ln[:, h, 0:TOK], start=True, stop=False)
                    pe.matmul(out[:, P:TOK], vt[:, 1, HD * h:HD * h + HD], ln[:, h, TOK:W], start=False,
                              stop=True).then_inc(done.sem, 1)
                for h in range(H):
                    score(h)
                for h in range(H):
                    suffix(h)
                for h in range(H):
                    weigh(h)

            @block.scalar
            def _(act):
                for h in range(H):
                    act.wait_ge(scored.sem, scored.at(h + 1))
                    act.activation(lg[:, h, :], ps[:, score_bank[h % 4], 0:W], ACT.Copy, scale=scale).then_inc(scaled.sem, 1)
                for h in range(H):
                    act.wait_ge(logged.sem, logged.at(h + 1))
                    act.activation(ln[:, h, :], ln[:, h, :], ACT.Exp).then_inc(core.chain["act"].sem, 1)
                for h in range(H):
                    act.wait_ge(core.chain["act"].sem, core.chain["act"].at(h + 1))
                    act.activation(ln[:, h, :], ln[:, h, :], ACT.Ln, bias=1.0).then_inc(kept.sem, 1)
                for h in range(H):
                    act.wait_ge(weight.sem, weight.at(h + 1))
                    act.activation(ln[:, h, :], ln[:, h, :], ACT.Exp).then_inc(exped.sem, 1)

            @block.vector
            def _(dve):
                link = core.link("dve", dve)
                for h in range(H):
                    dve.wait_ge(scaled.sem, scaled.at(h + 1))
                    dve.scalar_tensor_tensor(out=ln[:, h, :], in0=lg[:, h, :], scalar=-1.0, in1=lg[:, h, :], op0=ALU.mult,
                                             op1=ALU.min).then_inc(logged.sem, 1)

                def keep(h):
                    dve.wait_ge(kept.sem, kept.at(h + 1))
                    link(dve.scalar_tensor_tensor(out=ln[:, h, :], in0=lg[:, h, :], scalar=0.0, in1=ln[:, h, :],
                                                  op0=ALU.min, op1=ALU.subtract))
                    link(dve.tensor_tensor(lk[:, h, :], ln[:, h, :], lg[:, h, :], ALU.subtract))
                    dve.tensor_tensor(lk[:, h, :], lk[:, h, :], mask[:, :], ALU.mult).then_inc(masked.sem, 1)

                def exponent(h):
                    dve.wait_ge(between.sem, between.at(h + 1))
                    dve.tensor_tensor(ln[:, h, :], ln[:, h, :], ps[:, 2 + h % 2, 0:W], ALU.add).then_inc(weight.sem, 1)
                for i in range(H + 1):
                    if i < H:
                        keep(i)
                    if i >= 1:
                        exponent(i - 1)
                for j in range(H // 2):
                    dve.wait_ge(done.sem, done.at(2 * j + 2))
                    dve.tensor_copy(o[:, j, :], ps[:, 4 + j % 2, 0:TOK]).then_inc(core.dve_evac.sem, 1)

            @block.gpsimd
            def _(pool):
                for h in range(H):
                    pool.wait_ge(exped.sem, exped.at(h + 1))
                    pool.tensor_tensor(ln[:, h, :], ln[:, h, :], mask[:, :], ALU.mult).then_inc(final.sem, 1)
        for sig in (scored, logged, kept, masked, between, weight, exped, final, done, scaled, core.chain["act"]):
            sig.close(H)
        core.dve_evac.close(H // 2)
        part = sq[:, 0:4, :]
        with core.block() as block:
            @block.scalar
            def _(act):
                act.activation(part, o, ACT.Square)
        rs, = head_scales(core, "stick_o", [part], 1.0 / HD, RMS_EPS)
        with core.block() as block:
            @block.vector
            def _(dve):
                for t in range(4):
                    dve.scalar_tensor_tensor(out=o[:, t, :], in0=o[:, t, :], scalar=core.v("sb_out", t),
                                             in1=rs[:, t, :], op0=ALU.mult, op1=ALU.mult)


def rwkv_mix(core, z, lora, y):
    nc, ps = core.nc, core.ps
    T4, NC = 4, TOK // CHUNK
    with ExitStack() as s:
        def sb(name, shape):
            return s.enter_context(nc.sbuf_tensor("rwkv_" + name, shape, F32))
        r, k, v = z[:, 0:4, 1:], z[:, 4:8, 1:], z[:, 8:12, 1:]
        a, gate, bonus = (sb(n, [P, T4, TOK]) for n in ("a", "g", "bonus"))
        qq = sb("qq", [P, T4, 2, TOK])
        cm, fac = sb("mid", [P, T4, NC]), sb("fac", [P, T4, NC])
        vt, kt, btt = (sb(n, [P, NB, 4 * P]) for n in ("vt", "kt", "btt"))
        H = 8
        NP_ = H * NB
        mm_ = sb("mm", [P, NP_, 2, 2, P])
        early = s.enter_context(ExitStack())
        kk, lw, bt, en = (early.enter_context(nc.sbuf_tensor("rwkv_" + n, [P, T4, TOK], F32)) for n in ("kk", "lw", "b", "en"))
        with core.block() as block:
            @block.scalar
            def _(act):
                act.activation(z[0:HD, 12, 1:], z[0:HD, 12, 1:], ACT.Tanh)
                act.activation(z[:, 13, 1:], z[:, 13, 1:], ACT.Sigmoid)
        with core.block() as block:
            @block.tensor
            def _(pe):
                for t in range(T4):
                    c = slice((t % 2) * TOK, (t % 2) * TOK + TOK)
                    w = slice(t * P, t * P + P)
                    pe.matmul(ps[:, t // 2, c], lora[0:HD, w], z[0:HD, 12, 1:], start=True, stop=True)
                    pe.matmul(ps[:, 2 + t // 2, c], lora[HD:P, w], z[HD:P, 12, 1:], start=True, stop=True)
                    pe.matmul(ps[:, 4 + t // 2, c], lora[:, 512 + t * P:512 + t * P + P], z[:, 13, 1:], start=True,
                              stop=True)

            @block.vector
            def _(dve):
                link = core.link("dve", dve)
                for t in range(T4):
                    link(dve.tensor_scalar(kk[:, t, :], k[:, t, :], core.v("k_k", t), None, ALU.mult))
                link(dve.tensor_tensor(en[:, :, :], kk[:, :, :], kk[:, :, :], ALU.mult))
        with core.block() as block:
            @block.scalar
            def _(act):
                for t in range(T4):
                    c = slice((t % 2) * TOK, (t % 2) * TOK + TOK)
                    act.activation(lw[:, t, :], ps[:, t // 2, c], ACT.Sigmoid, bias=core.v("decay_w0", t))
                    act.activation(a[:, t, :], ps[:, 2 + t // 2, c], ACT.Sigmoid, bias=core.v("iclr_a0", t))
                    act.activation(gate[:, t, :], ps[:, 4 + t // 2, c], ACT.Copy)
        kk_scale, = head_scales(core, "rwkv_kk", [en], 1.0, 0.0, floor=1e-12)
        with core.block() as block:
            @block.vector
            def _(dve):
                link = core.link("dve", dve)
                link(dve.tensor_scalar(lw[:, :, :], lw[:, :, :], -float(np.exp(-0.5)), None, ALU.mult))
                for t in range(T4):
                    link(dve.tensor_tensor_scan(bt[:, t, :], core.m("scan_keep", 0, TOK), lw[:, t, :], 0.0, ALU.mult, ALU.add))
                mid = bt[:, :, :].rearrange("p t (c n) -> p t c n", n=CHUNK)
                link(dve.tensor_copy(cm[:, :, :], mid[:, :, :, CHUNK // 2 - 1]))
                for t in range(T4):
                    link(dve.tensor_tensor(mid[:, t], mid[:, t], bcast(cm[:, t, :].unsqueeze(2), [P, NC, CHUNK]), ALU.subtract))
                link(dve.tensor_copy(fac[:, :, :], mid[:, :, :, CHUNK - 1]))
                link(dve.tensor_tensor(fac[:, :, 0:NC - 1], fac[:, :, 0:NC - 1], cm[:, :, 1:NC], ALU.add))
                link(dve.tensor_tensor(lw[:, :, :], bt[:, :, :], lw[:, :, :], ALU.subtract))
        with core.block() as block:
            @block.vector
            def _(dve):
                link = core.link("dve", dve)
                link(dve.tensor_tensor(kk[:, :, :], kk[:, :, :], kk_scale, ALU.mult))
                for t in range(T4):
                    link(dve.tensor_scalar(en[:, t, :], a[:, t, :], 1.0, core.v("k_a", t), ALU.subtract, ALU.mult))
                    link(dve.scalar_tensor_tensor(out=k[:, t, :], in0=en[:, t, :], scalar=1.0, in1=k[:, t, :],
                                                  op0=ALU.add, op1=ALU.mult))
                    link(dve.scalar_tensor_tensor(out=bonus[:, t, :], in0=r[:, t, :], scalar=core.v("r_k", t),
                                                  in1=k[:, t, :], op0=ALU.mult, op1=ALU.mult))

            @block.scalar
            def _(act):
                act.activation(qq[:, :, 0, :], lw[:, :, :], ACT.Exp)
                act.activation(qq[:, :, 1, :], bt[:, :, :], ACT.Exp)
                act.activation(fac[:, :, :], fac[:, :, :], ACT.Exp)
        sums = head_sums(core, 6, bonus, T4)
        with core.block() as block:
            @block.scalar
            def _(act):
                act.activation(en[:, :, :], bt[:, :, :], ACT.Exp, scale=-1.0).then_inc(core.sem_a.sem, 1)

            @block.vector
            def _(dve):
                link = core.link("dve", dve)
                link(dve.tensor_tensor(bonus[:, :, :], v, sums, ALU.mult))
                link(dve.tensor_tensor(qq[:, :, 0, :], qq[:, :, 0, :], kk[:, :, :], ALU.mult))
                link(dve.tensor_tensor(qq[:, :, 1, :], qq[:, :, 1, :], r, ALU.mult))
                dve.wait_ge(core.sem_a.sem, core.sem_a.at(1))
                link(dve.tensor_tensor(bt[:, :, :], kk[:, :, :], a[:, :, :], ALU.mult))
                link(dve.tensor_tensor(bt[:, :, :], bt[:, :, :], en[:, :, :], ALU.mult))
                link(dve.tensor_tensor(k, k, en[:, :, :], ALU.mult))
        core.sem_a.close(1)
        for src, dst in ((v, vt), (k, kt), (bt, btt)):
            to_token_major(core, [src[:, t, :] for t in range(T4)], lambda t, b: dst[:, b, t * P:t * P + P])
        padded = {(0, 0): kk, (0, 1): lw, (1, 0): en, (1, 1): a}
        with core.block() as block:
            @block.scalar
            def _(act):
                for half in range(2):
                    act.activation(padded[0, half][:, :, :], k, ACT.Copy, scale=core.m("halves", half, 1))

            @block.vector
            def _(dve):
                for half in range(2):
                    dve.tensor_scalar(padded[1, half][:, :, :], bt[:, :, :], core.m("halves", half, 1), None, ALU.mult)
        with core.block() as block:
            @block.tensor
            def _(pe):
                for n in range(NP_):
                    h, b = n // NB, n % NB
                    if n >= 4:
                        pe.wait_ge(core.dve_evac.sem, core.dve_evac.at(n - 3))
                    for i in range(2):
                        x = pe.matmul(ps[:, n % 4, i * TOK:i * TOK + TOK], padded[i, h % 2][:, h // 2, b * P:b * P + P],
                                      qq[:, h // 2, :, b * P:b * P + P], start=True, stop=True)
                    x.then_inc(core.sem_a.sem, 1)

            @block.vector
            def _(dve):
                both = core.m("lt64", 0, 2 * P)
                for n in range(NP_):
                    dve.wait_ge(core.sem_a.sem, core.sem_a.at(n + 1))
                    dve.tensor_tensor(mm_[:, n].rearrange("p i j t -> p i (j t)"),
                                      ps[:, n % 4, :].rearrange("p (i t) -> p i t", i=2),
                                      bcast(both.unsqueeze(1), [P, 2, 2 * P]), ALU.mult).then_inc(core.dve_evac.sem, 1)
        core.sem_a.close(NP_)
        core.dve_evac.close(NP_)
        early.close()
        tt = sb("tt", [P, NP_, P])
        levels = s.enter_context(ExitStack())
        tn, xx, nl = (levels.enter_context(nc.sbuf_tensor("rwkv_" + n, [P, NP_, P], F32)) for n in ("tn", "xx", "nl"))
        ident = core.m("ident")
        with core.block() as block:
            @block.vector
            def _(dve):
                for g in range(4):
                    gs = slice(4 * g, 4 * g + 4)
                    dve.tensor_tensor(nl[:, gs, :], mm_[:, gs, 1, 0, :], bcast(core.m("level", 0, P).unsqueeze(1), [P, 4, P]),
                                      ALU.mult).then_inc(core.sem_a.sem, 1)
                for g in range(4):
                    gs = slice(4 * g, 4 * g + 4)
                    dve.wait_ge(core.sem_a.sem, core.sem_a.at(g + 1))
                    dve.tensor_tensor(tt[:, gs, :], bcast(ident.unsqueeze(1), [P, 4, P]), nl[:, gs, :], ALU.subtract)
                    dve.wait_ge(core.sem_b.sem, core.sem_b.at(g + 1))
                    dve.tensor_tensor(tn[:, gs, :], bcast(ident.unsqueeze(1), [P, 4, P]),
                                      ps[:, g, :].rearrange("p (i t) -> p i t", t=P), ALU.subtract)

            @block.tensor
            def _(pe):
                for n in range(NP_):
                    pe.wait_ge(core.sem_a.sem, core.sem_a.at(n // 4 + 1))
                    x = pe.transpose(ps[:, n // 4, n % 4 * P:n % 4 * P + P], nl[:, n, :], ident)
                    if n % 4 == 3:
                        x.then_inc(core.sem_b.sem, 1)
        core.sem_a.close(4)
        core.sem_b.close(4)
        steps = [(lev, g) for lev in range(1, 6) for g in range(4)]
        picked, first, moved, second, updated = core.sem_a, core.sem_b, core.sem_c, core.sem_d, core.sem_e
        with core.block() as block:
            @block.gpsimd
            def _(pool):
                for i, (lev, g) in enumerate(steps):
                    if i >= 4:
                        pool.wait_ge(first.sem, first.at(i - 3))
                    gs = slice(4 * g, 4 * g + 4)
                    pool.tensor_tensor(nl[:, gs, :], mm_[:, gs, 1, 0, :], bcast(core.m("level", lev, P).unsqueeze(1), [P, 4, P]),
                                       ALU.mult).then_inc(picked.sem, 1)

            @block.tensor
            def _(pe):
                def products(i):
                    lev, g = steps[i]
                    pe.wait_ge(picked.sem, picked.at(i + 1))
                    if i >= 4:
                        pe.wait_ge(updated.sem, updated.at(i - 3))
                    for n in range(4 * g, 4 * g + 4):
                        x = pe.matmul(ps[:, g, n % 4 * P:n % 4 * P + P], nl[:, n, :], tn[:, n, :], start=True, stop=True)
                    x.then_inc(first.sem, 1)

                def corrections(i):
                    lev, g = steps[i]
                    pe.wait_ge(moved.sem, moved.at(i + 1))
                    if i >= 2:
                        pe.wait_ge(updated.sem, updated.at(i - 1))
                    for n in range(4 * g, 4 * g + 4):
                        at = slice(n % 4 * P, n % 4 * P + P)
                        if lev < 5:
                            pe.matmul(ps[:, 4 + 2 * (g % 2), at], tt[:, n, :], xx[:, n, :], start=True, stop=True)
                        x = pe.matmul(ps[:, 5 + 2 * (g % 2), at], xx[:, n, :], tt[:, n, :], start=True, stop=True)
                    x.then_inc(second.sem, 1)
                for i in range(len(steps) + 1):
                    if i < len(steps):
                        products(i)
                    if i >= 1:
                        corrections(i - 1)

            @block.scalar
            def _(act):
                for i, (lev, g) in enumerate(steps):
                    act.wait_ge(first.sem, first.at(i + 1))
                    act.activation(xx[:, 4 * g:4 * g + 4, :], ps[:, g, :].rearrange("p (i t) -> p i t", t=P),
                                   ACT.Copy).then_inc(moved.sem, 1)

            @block.vector
            def _(dve):
                for i, (lev, g) in enumerate(steps):
                    gs = slice(4 * g, 4 * g + 4)
                    dve.wait_ge(second.sem, second.at(i + 1))
                    if lev < 5:
                        dve.tensor_tensor(tn[:, gs, :], tn[:, gs, :],
                                          ps[:, 4 + 2 * (g % 2), :].rearrange("p (i t) -> p i t", t=P), ALU.subtract)
                    dve.tensor_tensor(tt[:, gs, :], tt[:, gs, :],
                                      ps[:, 5 + 2 * (g % 2), :].rearrange("p (i t) -> p i t", t=P),
                                      ALU.subtract).then_inc(updated.sem, 1)
        for sig in (picked, first, moved, second, updated):
            sig.close(len(steps))
        levels.close()
        st = sb("state", [P, NC, T4, HD])
        rs, un = sb("rhs", [P, NB, 2, T4, HD]), sb("neg_u", [P, NB, 2, T4, HD])
        for c in range(NC):
            b, off = c // 2, HD * (c % 2)
            po = slice(off, off + HD)
            with core.block() as block:
                @block.tensor
                def _(pe):
                    for par in range(2):
                        rr = slice(HD * par, HD * par + HD)
                        for t in range(T4):
                            h = 2 * t + par
                            n = h * NB + b
                            out = ps[po, par, t * HD:t * HD + HD]
                            x = pe.matmul(out, mm_[:, n, 0, 0, po], vt[:, b, h * HD:h * HD + HD], start=True, stop=(c == 0))
                            if c > 0:
                                x = pe.matmul(out, qq[rr, t, 0, c * CHUNK:c * CHUNK + CHUNK], st[rr, c, t, :], start=False,
                                              stop=True)
                        x.then_inc(core.sem_a.sem, 1)
                    for par in range(2):
                        pe.wait_ge(core.sem_b.sem, core.sem_b.at(par + 1))
                        for t in range(T4):
                            h = 2 * t + par
                            x = pe.matmul(ps[po, 2 + par, t * HD:t * HD + HD], tt[po, h * NB + b, po], rs[po, b, par, t, :],
                                          start=True, stop=True)
                        x.then_inc(core.sem_c.sem, 1)
                    if c < NC - 1:
                        for par in range(2):
                            pe.wait_ge(core.sem_d.sem, core.sem_d.at(par + 1))
                            for t in range(T4):
                                h = 2 * t + par
                                hs = slice(h * HD, h * HD + HD)
                                out = ps[HD * par:HD * par + HD, 4, t * HD:t * HD + HD]
                                pe.matmul(out, kt[po, b, hs], vt[po, b, hs], start=True, stop=False)
                                x = pe.matmul(out, btt[po, b, hs], un[po, b, par, t, :], start=False, stop=True)
                        x.then_inc(core.sem_e.sem, 1)

                @block.vector
                def _(dve):
                    link = core.link("dve", dve)
                    for par in range(2):
                        dve.wait_ge(core.sem_a.sem, core.sem_a.at(par + 1))
                        dve.tensor_copy(rs[po, b, par], ps[po, par, 0:T4 * HD].rearrange("p (t v) -> p t v", v=HD)
                                        ).then_inc(core.sem_b.sem, 1)
                    if c < NC - 1:
                        dve.wait_ge(core.sem_e.sem, core.sem_e.at(1))
                        nxt = st[:, c + 1]
                        new = ps[:, 4, 0:T4 * HD].rearrange("p (t v) -> p t v", v=HD)
                        f = bcast(fac[:, :, c:c + 1], [P, T4, HD])
                        if c == 0:
                            link(dve.tensor_tensor(nxt, new, f, ALU.mult))
                        else:
                            link(dve.tensor_tensor(nxt, st[:, c], new, ALU.add))
                            link(dve.tensor_tensor(nxt, nxt, f, ALU.mult))

                @block.scalar
                def _(act):
                    for par in range(2):
                        act.wait_ge(core.sem_c.sem, core.sem_c.at(par + 1))
                        act.activation(un[po, b, par], ps[po, 2 + par, 0:T4 * HD].rearrange("p (t v) -> p t v", v=HD),
                                       ACT.Copy, scale=-1.0).then_inc(core.sem_d.sem, 1)
            for sig in (core.sem_a, core.sem_b, core.sem_c, core.sem_d):
                sig.close(2)
            if c < NC - 1:
                core.sem_e.close(1)
        with core.block() as block:
            @block.tensor
            def _(pe):
                for par in range(2):
                    rr = slice(HD * par, HD * par + HD)
                    for t in range(T4):
                        h = 2 * t + par
                        for b in range(NB):
                            n = h * NB + b
                            out = ps[rr, 2 * par + t // 2, (t % 2) * TOK + b * P:(t % 2) * TOK + b * P + P]
                            pe.matmul(out, vt[:, b, h * HD:h * HD + HD], mm_[:, n, 0, 1, :], start=True, stop=False)
                            pe.matmul(out, un[:, b, par, t, :], mm_[:, n, 1, 1, :], start=False, stop=False)
                            for c in (2 * b, 2 * b + 1):
                                if c > 0:
                                    half = out[:, (c % 2) * CHUNK:(c % 2) * CHUNK + CHUNK]
                                    pe.matmul(half, st[rr, c, t, :], qq[rr, t, 1, c * CHUNK:c * CHUNK + CHUNK],
                                              start=False, stop=(c % 2 == 1))
        with core.block() as block:
            @block.vector
            def _(dve):
                for par in range(2):
                    rr = slice(HD * par, HD * par + HD)
                    dve.tensor_copy(y[rr, :, :], ps[rr, 2 * par:2 * par + 2, :].rearrange("p a (b n) -> p (a b) n", n=TOK))
        sums = head_sums(core, 4, y, T4)
        with core.block() as block:
            @block.vector
            def _(dve):
                link = core.link("dve", dve)
                link(dve.scalar_tensor_tensor(out=y[:, :, :], in0=sums, scalar=-1.0 / HD, in1=y[:, :, :], op0=ALU.mult, op1=ALU.add))
                link(dve.tensor_tensor(a[:, :, :], y[:, :, :], y[:, :, :], ALU.mult))
        rs, = head_scales(core, "rwkv_y", [a], 1.0 / HD, 1e-5 * HD)
        with core.block() as block:
            @block.vector
            def _(dve):
                link = core.link("dve", dve)
                link(dve.tensor_tensor(y[:, :, :], y[:, :, :], rs, ALU.mult))
                for t in range(T4):
                    link(dve.tensor_scalar(y[:, t, :], y[:, t, :], core.v("lnx_w", t), core.v("lnx_b", t), ALU.mult, ALU.add))
                link(dve.tensor_tensor(y[:, :, :], y[:, :, :], bonus[:, :, :], ALU.add))
                link(dve.tensor_tensor(y[:, :, :], y[:, :, :], gate[:, :, :], ALU.mult))


def gated_residual(core, gate):
    def take(m):
        return lambda eng, ps: eng.scalar_tensor_tensor(out=core.x[:, m, :], in0=ps, scalar=gate[:, m:m + 1],
                                                        in1=core.x[:, m, :], op0=ALU.mult, op1=ALU.add)
    return [("dve", take(m), None) for m in range(DT)]


def second_block(core):
    nc = core.nc
    mod = core.mod2
    shift1, scale1, gate1, shift2, scale2, gate2 = (mod[:, 8 * i:8 * i + 8] for i in range(6))
    with ExitStack() as s:
        y = s.enter_context(nc.sbuf_tensor("mix2_y", [P, DT, TOK], F32))
        z = s.enter_context(nc.sbuf_tensor("mix2_z", [P, C_RWKV_T, TOK + 1], F32))
        lora = s.enter_context(nc.sbuf_tensor("lora_w", [P, 1024], F32))
        with ExitStack() as s2:
            qkv = s2.enter_context(nc.sbuf_tensor("stick_qkv", [P, 12, TOK], F32))
            with ExitStack() as s3:
                h = s3.enter_context(nc.sbuf_tensor("mix2_h", [P, DT, TOK], F32))
                tmp = s3.enter_context(nc.sbuf_tensor("shift_tmp", [P, TOK], F32))
                norm = rms_modulate(core, h, core.vs("norm1"), scale1, shift1)
                with core.block() as block:
                    @block.vector
                    def _(dve):
                        dve.memset(z[:, :, 0:1], 0.0)

                    @block.scalar
                    def _(act):
                        act.dma_start(lora[:, :], core.a["lora"]).then_inc(core.const_loaded.sem, 16)
                tiles = [("act", copy_tiles(core, lambda m: z[:, m, 1:])(m), None) for m in range(C_RWKV_T)]
                tiles += [("act", copy_tiles(core, lambda m: qkv[:, m - C_RWKV_T, :])(m), None)
                          for m in range(C_RWKV_T, 26)]

                def token_shift(dve, link):
                    for t in range(C_RWKV_T):
                        dve.wait_ge(core.act_evac.sem, core.act_evac.at(t + 1))
                        link(dve.tensor_tensor(tmp[:, :], z[:, t, 0:TOK], z[:, t, 1:], ALU.subtract))
                        link(dve.scalar_tensor_tensor(out=z[:, t, 1:], in0=tmp[:, :], scalar=core.v("mu", t),
                                                      in1=z[:, t, 1:], op0=ALU.mult, op1=ALU.add))
                linear(core, "w_in2", lambda k: h[:, k, :], tiles, head=token_shift, source=norm)
            with core.block() as block:
                @block.scalar
                def _(act):
                    act.wait_ge(core.const_loaded.sem, core.const_loaded.at(16))
            core.const_loaded.close(16)
            stick_breaking(core, qkv[:, 0:4, :], qkv[:, 4:8, :], qkv[:, 8:12, :], y[:, 4:8, :])
        rwkv_mix(core, z, lora, y[:, 0:4, :])
        bias = s.enter_context(nc.sbuf_tensor("bias_parts", [BIAS_PARTS * N_EXPERTS, N_BIAS], BF16))
        rest = s.enter_context(nc.sbuf_tensor("bias_rest", [BIAS_PARTS * N_EXPERTS, N_BIAS], F32))
        with core.block() as block:
            @block.sync
            def _(sp):
                for i in range(BIAS_PARTS):
                    sp.dma_start(rest[i * N_EXPERTS:(i + 1) * N_EXPERTS, :], core.a["eb"]).then_inc(core.const_loaded.sem, 16)
        casts, rests = split_biases(core, bias, rest)
        linear(core, "w_out2", lambda k: y[:, k, :], gated_residual(core, gate1), act_work=casts, pool_work=rests)
        core.const_loaded.close(16 * BIAS_PARTS)
        core.sem_a.close(2)
        core.sem_b.close(2)
        moe_layer(core, bias)


class LoopChain:

    def __init__(self, sig, eng, u, per_turn):
        self.sig, self.eng, self.u, self.per_turn, self.n = sig, eng, u, per_turn, 0

    def __call__(self, ins):
        self.n += 1
        ins.then_inc(self.sig.sem, 1)
        self.eng.wait_ge(self.sig.sem, self.u * self.per_turn + self.n)

    def done(self):
        assert self.n == self.per_turn, self.n


BIAS_PARTS, N_BIAS = 3, 3 * D


def split_biases(core, bias, rest):
    E = N_EXPERTS
    cast, left = core.sem_a, core.sem_b

    def casts(act):
        act.wait_ge(core.const_loaded.sem, core.const_loaded.at(16 * BIAS_PARTS))
        act.activation(bias[:, :], rest[:, :], ACT.Copy).then_inc(cast.sem, 1)
        act.wait_ge(left.sem, left.at(1))
        act.activation(bias[E:2 * E, :], rest[E:2 * E, :], ACT.Copy)
        act.activation(bias[2 * E:, :], rest[2 * E:, :], ACT.Copy).then_inc(cast.sem, 1)
        act.wait_ge(left.sem, left.at(2))
        act.activation(bias[2 * E:, :], rest[2 * E:, :], ACT.Copy)

    def rests(pool):
        pool.wait_ge(cast.sem, cast.at(1))
        pool.tensor_tensor(rest[:, :], rest[:, :], bias[:, :], ALU.subtract).then_inc(left.sem, 1)
        pool.wait_ge(cast.sem, cast.at(2))
        pool.tensor_tensor(rest[2 * E:, :], rest[2 * E:, :], bias[2 * E:, :], ALU.subtract).then_inc(left.sem, 1)
    return casts, rests


def mixture_of_experts(core, h, acc, bias):
    nc, ps = core.nc, core.ps
    E, S = N_EXPERTS, UNIT
    with ExitStack() as s:
        def sb(name, shape, dt=F32):
            return s.enter_context(nc.sbuf_tensor("moe_" + name, shape, dt))
        ht = sb("ht", [P, NB, D])
        table = sb("table", [P, UNITS, 2, NB])
        expert_of = sb("expert_of", [3 * E, UNITS])
        unit_int = sb("unit_int", [1, MAX_UNITS + 1], I32)
        selt, ytok = sb("selt", [P, 2 * TOK]), sb("ytok", [P, D // 2])
        to_token_major(core, [h[:, t, :] for t in range(DT)], lambda t, b: ht[:, b, t * P:t * P + P])
        with ExitStack() as s2:
            def sb2(name, shape, dt=F32):
                return s2.enter_context(nc.sbuf_tensor("route_" + name, shape, dt))
            rw = sb2("rw", [P, DT, E])
            lg, m, g, r = (sb2(n, [P, NB, E]) for n in ("lg", "m", "g", "r"))
            mx, ix, ixf = sb2("mx", [P, NB, 8]), sb2("ix", [P, NB, 8], U32), sb2("ixf", [P, NB, 8])
            sm = sb2("sm", [P, NB, 2])
            cnt, units, cum, first = (sb2(n, [P, E]) for n in ("cnt", "units", "cum", "first"))
            ecol, onehot = sb2("ecol", [BIAS_PARTS * E, 2]), sb2("onehot", [3 * E, UNITS])
            cf = sb2("cf", [1, 2, 3, E])
            rt, gt = sb2("rt", [E, TOK]), sb2("gt", [E, TOK])
            row = sb2("row", [1, MAX_UNITS + 1])
            with core.block() as block:
                @block.scalar
                def _(act):
                    act.dma_start(rw[:, :, :], core.a["router"]).then_inc(core.const_loaded.sem, 16)

                @block.gpsimd
                def _(pool):
                    pool.memset(acc[:, :, :], 0.0)
                    pool.memset(ytok[:, :], 0.0)
                    pool.memset(selt[:, :], 0.0).then_inc(core.sem_a.sem, 1)

                @block.tensor
                def _(pe):
                    pe.wait_ge(core.const_loaded.sem, core.const_loaded.at(16))
                    for b in range(NB):
                        for k in range(DT):
                            pe.matmul(ps[:, 0, b * E:b * E + E], h[:, k, b * P:b * P + P], rw[:, k, :], start=(k == 0),
                                      stop=(k == DT - 1))
            core.const_loaded.close(16)
            with core.block() as block:
                @block.vector
                def _(dve):
                    link = core.link("dve", dve)
                    link(dve.tensor_tensor(lg[:, :, :], ps[:, 0, 0:NB * E].rearrange("p (b e) -> p b e", e=E),
                                           bcast(core.vs("router_b").unsqueeze(1), [P, NB, E]), ALU.add))
                    for b in range(NB):
                        link(dve.max(mx[:, b, :], lg[:, b, :]))
                        link(dve.max_index(ix[:, b, :], mx[:, b, :], lg[:, b, :]))
                    link(dve.tensor_copy(ixf[:, :, :], ix[:, :, :]))
                    for b in range(NB):
                        link(dve.tensor_scalar(m[:, b, :], core.m("iota_e"), ixf[:, b, 0:1], None, ALU.is_equal))
                        for j in range(1, TOP_K):
                            link(dve.scalar_tensor_tensor(out=m[:, b, :], in0=core.m("iota_e"), scalar=ixf[:, b, j:j + 1],
                                                          in1=m[:, b, :], op0=ALU.is_equal, op1=ALU.add))
                    link(dve.tensor_scalar(sm[:, :, 0], mx[:, :, 0], -1.0, None, ALU.mult))
            with core.block() as block:
                @block.scalar
                def _(act):
                    for b in range(NB):
                        act.activation(g[:, b, :], lg[:, b, :], ACT.Exp, bias=sm[:, b, 0:1])

                @block.tensor
                def _(pe):
                    pe.matmul(ps[:, 1, 0:E], core.m("tri_lt"), m[:, 0, :], start=True, stop=True)
                    pe.matmul(ps[:, 1, E:2 * E], core.m("tri_lt"), m[:, 1, :], start=True, stop=False)
                    pe.matmul(ps[:, 1, E:2 * E], core.m("ones"), m[:, 0, :], start=False, stop=True)
                    for b in range(NB):
                        pe.matmul(ps[:, 2, 0:E], core.m("ones"), m[:, b, :], start=(b == 0), stop=(b == NB - 1))
            with core.block() as block:
                @block.vector
                def _(dve):
                    link = core.link("dve", dve)
                    link(dve.tensor_tensor(g[:, :, :], g[:, :, :], m[:, :, :], ALU.mult))
                    link(dve.tensor_reduce(sm[:, :, 1], g[:, :, :], AX, ALU.add))
                    link(dve.reciprocal(sm[:, :, 1], sm[:, :, 1]))
                    link(dve.tensor_tensor(g[:, :, :], g[:, :, :], bcast(sm[:, :, 1:2], [P, NB, E]), ALU.mult))
                    link(dve.tensor_copy(cnt[:, :], ps[:, 2, 0:E]))
                    link(dve.tensor_scalar(units[:, :], cnt[:, :], 0.0, None, ALU.is_gt))
                    for j in range(1, TOK // S):
                        link(dve.scalar_tensor_tensor(out=units[:, :], in0=cnt[:, :], scalar=float(j * S),
                                                      in1=units[:, :], op0=ALU.is_gt, op1=ALU.add))
                    link(dve.tensor_tensor_scan(cum[:, :], core.m("ones")[:, 0:E], units[:, :], 0.0, ALU.mult, ALU.add))
                    link(dve.tensor_tensor(first[:, :], cum[:, :], units[:, :], ALU.subtract))
                    link(dve.tensor_copy(cf[:, 0], bcast(cum[0:1, :].unsqueeze(1), [1, 3, E])))
                    link(dve.tensor_copy(cf[:, 1], bcast(first[0:1, :].unsqueeze(1), [1, 3, E])))
                    link(dve.scalar_tensor_tensor(out=r[:, :, :], in0=ps[:, 1, 0:NB * E].rearrange("p (b e) -> p b e", e=E),
                                                  scalar=1000.0, in1=m[:, :, :], op0=ALU.add, op1=ALU.mult))
                    link(dve.tensor_scalar(cnt[:, :], first[:, :], float(S), -1000.0, ALU.mult, ALU.add))
                    link(dve.tensor_tensor(r[:, :, :], r[:, :, :], bcast(cnt[:, :].unsqueeze(1), [P, NB, E]), ALU.add))
            with core.block() as block:
                @block.tensor
                def _(pe):
                    ident = core.m("ident")
                    for i in range(2):
                        pe.matmul(ps[0:3 * E, 0, i:i + 1], cf[:, i].rearrange("p a e -> p (a e)"), core.m("ones")[0:1, 0:1],
                                  start=True, stop=True)
                    for b in range(NB):
                        pe.transpose(ps[0:E, 1, b * P:b * P + P], r[:, b, :], ident)
                        pe.transpose(ps[0:E, 2, b * P:b * P + P], g[:, b, :], ident)
            with core.block() as block:
                @block.vector
                def _(dve):
                    link = core.link("dve", dve)
                    link(dve.tensor_copy(ecol[:, :], ps[0:3 * E, 0, 0:2]))
                    link(dve.tensor_copy(rt[:, :], ps[0:E, 1, 0:TOK]))
                    link(dve.tensor_copy(gt[:, :], ps[0:E, 2, 0:TOK]))
                    iu = core.m("iota_u")[0:3 * E, :]
                    link(dve.tensor_scalar(onehot[:, :], iu, ecol[:, 0:1], None, ALU.is_lt))
                    link(dve.scalar_tensor_tensor(out=onehot[:, :], in0=iu, scalar=ecol[:, 1:2], in1=onehot[:, :],
                                                  op0=ALU.is_ge, op1=ALU.mult))
                    link(dve.tensor_copy(expert_of[:, :], onehot[:, :]))
            with core.block() as block:
                @block.tensor
                def _(pe):
                    for b in range(NB):
                        pe.matmul(ps[:, 0, b * S:b * S + UNITS], rt[:, b * P:b * P + P], onehot[0:E, :], start=True, stop=True)
                        pe.matmul(ps[:, 1, b * S:b * S + UNITS], gt[:, b * P:b * P + P], onehot[0:E, :], start=True, stop=True)
                    pe.matmul(ps[0:1, 2, 0:UNITS], core.m("col_e")[0:E, :], onehot[0:E, :], start=True, stop=True)
            with core.block() as block:
                @block.vector
                def _(dve):
                    link = core.link("dve", dve)
                    link(dve.tensor_copy(row[:, 0:MAX_UNITS], ps[0:1, 2, 0:MAX_UNITS]))
                    link(dve.tensor_copy(row[:, MAX_UNITS:], cum[0:1, E - 1:E]))
                    link(dve.tensor_copy(unit_int[:, :], row[:, :]))
                    for b in range(NB):
                        link(dve.scalar_tensor_tensor(out=table[:, :, 0, b], in0=core.m("iota_u"), scalar=-float(S),
                                                      in1=ps[:, 0, b * S:b * S + UNITS], op0=ALU.mult, op1=ALU.add))
                        link(dve.tensor_copy(table[:, :, 1, b], ps[:, 1, b * S:b * S + UNITS]))

        cur = sb("cur", [P, 2, 2, NB])
        sel, selg = sb("sel", [P, NB, 2 * S]), sb("selg", [P, NB, 2 * S])
        pick = sb("pick", [BIAS_PARTS * E, S], BF16)
        xg, hidt = sb("xg", [P, DT, 2 * S]), sb("hidt", [P, D // 2])
        glu, lin, sg = sb("glu", [P, D // 2]), sb("lin", [P, D // 2]), sb("sg", [P, D // 2])
        loaded = [core.counter(f"expert_panel{i}") for i in range(RING)]
        names = ("expert_panel_used", "picked", "gates_picked", "expert_picked", "gathered", "gathered_copied",
                 "gates_turned", "gates_copied", "hidden", "glu_ready", "sigmoid_ready", "hidden_ready", "hidden_turned",
                 "hidden_copied", "bias_used", "expert_out", "out_copied", "scattered", "added", "dve_turn")
        (used, picked, gates_picked, expert_picked, gathered, xg_ready, gates_turned, gates_copied, hidden, glu_ready,
         sig_ready, hid_ready, hid_turned, hid_copied, bias_used, outs, copied, scattered, added, turn) = (
            core.counter(n) for n in names)
        PANELS = 12
        scatter_banks = (5, 3, 2, 4)
        with core.block() as block:
            @block.tensor
            def _(pe):
                pe.wait_ge(core.sem_a.sem, core.sem_a.at(1))
                pe.sem_inc(used.sem, RING)
                pe.sem_inc(added.sem, 1)
        added.close(1)
        core.sem_a.close(1)

        def unit_count(eng):
            return eng.value_load(unit_int[0:1, MAX_UNITS:MAX_UNITS + 1], min_val=1, max_val=MAX_UNITS)

        def pick_tokens(dve, link, u):
            link(dve.tensor_copy(cur[:, 0], table[:, bass.ds(u, 1)].rearrange("p a i b -> p (a i) b")))
            for b in range(NB):
                ins = dve.tensor_scalar(sel[:, b, :], core.m("iota_slot"), cur[:, 0, 0, b:b + 1], None, ALU.is_equal)
            ins.then_inc(picked.sem, 1)

        def pick_gates(dve, link, u):
            link(dve.tensor_copy(cur[:, 1], table[:, bass.ds(u, 1)].rearrange("p a i b -> p (a i) b")))
            for b in range(NB):
                ins = dve.tensor_scalar(selg[:, b, :], core.m("iota_slot"), cur[:, 1, 0, b:b + 1], cur[:, 1, 1, b:b + 1],
                                        ALU.is_equal, ALU.mult)
            ins.then_inc(gates_picked.sem, 1)

        def pick_expert(dve, u):
            dve.tensor_copy(pick[:, :], bcast(expert_of[:, bass.ds(u, 1)], [BIAS_PARTS * E, S])).then_inc(expert_picked.sem, 1)

        def copy_gathered(dve):
            for i in range(2):
                ins = dve.tensor_copy(xg[:, 4 * i:4 * i + 4, :], ps[:, 6 + i, :].rearrange("p (k n) -> p k n", n=2 * S))
            ins.then_inc(xg_ready.sem, 1)

        def gather(pe):
            for k in range(DT):
                for b in range(NB):
                    mm = pe.matmul(ps[:, 6 + k // 4, k % 4 * 2 * S:k % 4 * 2 * S + 2 * S], ht[:, b, k * P:k * P + P], sel[:, b, :],
                                   start=(b == 0), stop=(b == NB - 1))
            mm.then_inc(gathered.sem, 1)

        def scatter(pe, u):
            pe.wait_ge(copied.sem, copied.at(u))
            pe.wait_ge(gates_copied.sem, gates_copied.at(u))
            pe.wait_ge(added.sem, added.at(u * 4))
            for t, bank in enumerate(scatter_banks):
                pe.matmul(ps[:, bank, :], ytok[:, t * P:t * P + P], selt[:, :], start=True, stop=True).then_inc(scattered.sem, 1)

        def add(dve, u):
            for t, bank in enumerate(scatter_banks):
                dve.wait_ge(scattered.sem, scattered.at(u * 4 + (t + 1)))
                dve.tensor_tensor(acc[:, t::4, :], acc[:, t::4, :],
                                  ps[:, bank, :].rearrange("p (k n) -> p k n", n=TOK), ALU.add).then_inc(added.sem, 1)

        with core.block() as block:
            @block.sync
            def _(sp):
                n = unit_count(sp)
                with sp.Fori(0, n) as u:
                    e = sp.value_load(unit_int[0:1, bass.ds(u, 1)], min_val=0, max_val=E - 1)
                    for j in range(PANELS):
                        sp.wait_ge(used.sem, used.at(u * PANELS + (j + 1)))
                        if j < 8:
                            src = core.a["w1"][bass.ds(e * 8 + j, 1)].rearrange("a p n -> p (a n)")
                            dst = core.ring[:, j % RING, :]
                        else:
                            src = core.a["w2"][bass.ds(e * 4 + (j - 8), 1)].rearrange("a (k p) n -> p (a k) n", p=P)
                            dst = core.ring[:, j % RING, :].rearrange("p (k n) -> p k n", n=D)
                        sp.dma_start(dst, src).then_inc(loaded[j % RING].sem, 16)

            @block.tensor
            def _(pe):
                n = unit_count(pe)
                ident = core.m("ident")
                pe.wait_ge(picked.sem, picked.at(1))
                gather(pe)
                halves = [(slice(0, S), 0), (slice(S, P), D // 2)]
                with pe.Fori(0, n) as u:
                    def panel(j):
                        pe.wait_ge(loaded[j % RING].sem, loaded[j % RING].at(u * (16 * PANELS // RING) + 16 * (j // RING + 1)))
                        return core.ring[:, j % RING, :]
                    pe.wait_ge(expert_picked.sem, expert_picked.at(u + 1))
                    pe.wait_ge(xg_ready.sem, xg_ready.at(u + 1))
                    for bank in range(2):
                        for out, at in halves:
                            pe.matmul(ps[out, bank, :], pick[:, :], bias[:, bank * D + at:bank * D + at + 512], start=True, stop=False)
                    for j in range(8):
                        w = panel(j)
                        for bank in range(2):
                            for out, at in halves:
                                mm = pe.matmul(ps[out, bank, :], xg[:, j, 0:S], w[:, bank * D + at:bank * D + at + 512],
                                               start=False, stop=(j == 7))
                        mm.then_inc(used.sem, 1)
                    pe.sem_inc(hidden.sem, 1)
                    scatter(pe, u)
                    pe.wait_ge(picked.sem, picked.at(u + 2))
                    gather(pe)
                    pe.wait_ge(gates_picked.sem, gates_picked.at(u + 1))
                    pe.wait_ge(added.sem, added.at(u * 4 + 4))
                    for b in range(NB):
                        mm = pe.transpose(ps[:, 5, b * P:b * P + P], selg[:, b, :], ident)
                    mm.then_inc(gates_turned.sem, 1)
                    pe.wait_ge(hid_ready.sem, hid_ready.at(u + 1))
                    for c in range(4):
                        mm = pe.transpose(ps[:, 3, c * P:c * P + P], lin[:, c * P:c * P + P], ident)
                    mm.then_inc(hid_turned.sem, 1)
                    for out, at in halves:
                        mm = pe.matmul(ps[out, 2, :], pick[:, :], bias[:, 2 * D + at:2 * D + at + 512], start=True, stop=False)
                    mm.then_inc(bias_used.sem, 1)
                    pe.wait_ge(hid_copied.sem, hid_copied.at(u + 1))
                    for q in range(4):
                        w = panel(8 + q)
                        for i in range(2):
                            k = 2 * q + i
                            at_k = k % 4 * P + k // 4 * S
                            for out, at in halves:
                                mm = pe.matmul(ps[out, 2, :], hidt[:, at_k:at_k + S], w[:, i * D + at:i * D + at + 512],
                                               start=False, stop=(k == DT - 1))
                        mm.then_inc(used.sem, 1)
                    pe.sem_inc(outs.sem, 1)
                scatter(pe, n)

            @block.scalar
            def _(act):
                n = unit_count(act)
                with act.Fori(0, n) as u:
                    act.wait_ge(glu_ready.sem, glu_ready.at(u + 1))
                    act.activation(sg[:, :], glu[:, :], ACT.Sigmoid, scale=SWIGLU_ALPHA).then_inc(sig_ready.sem, 1)

            @block.vector
            def _(dve):
                n = unit_count(dve)
                link = core.link("dve", dve)
                pick_tokens(dve, link, 0)
                pick_gates(dve, link, 0)
                pick_expert(dve, 0)
                dve.wait_ge(gathered.sem, gathered.at(1))
                copy_gathered(dve)
                with dve.Fori(0, n) as u:
                    link = LoopChain(turn, dve, u, 5)
                    dve.wait_ge(gathered.sem, gathered.at(u + 1))
                    pick_tokens(dve, link, u + 1)
                    dve.wait_ge(used.sem, used.at(u * PANELS + (RING + 8)))
                    dve.tensor_scalar(glu[:, :], ps[:, 0, :], SWIGLU_LIMIT, None, ALU.min).then_inc(glu_ready.sem, 1)
                    link(dve.tensor_scalar(lin[:, :], ps[:, 1, :], SWIGLU_LIMIT, -SWIGLU_LIMIT, ALU.min, ALU.max))
                    dve.wait_ge(glu_ready.sem, glu_ready.at(u + 1))
                    link(dve.scalar_tensor_tensor(out=lin[:, :], in0=lin[:, :], scalar=1.0, in1=glu[:, :], op0=ALU.add,
                                                  op1=ALU.mult))
                    dve.wait_ge(sig_ready.sem, sig_ready.at(u + 1))
                    link(dve.tensor_tensor(lin[:, :], lin[:, :], sg[:, :], ALU.mult))
                    dve.sem_inc(hid_ready.sem, 1)
                    add(dve, u)
                    dve.wait_ge(gathered.sem, gathered.at(u + 2))
                    copy_gathered(dve)
                    dve.wait_ge(gates_turned.sem, gates_turned.at(u + 1))
                    dve.tensor_copy(selt[0:S, 0:TOK], ps[0:S, 5, 0:TOK])
                    dve.tensor_copy(selt[S:P, TOK:], ps[S:P, 5, 0:TOK]).then_inc(gates_copied.sem, 1)
                    dve.wait_ge(hid_turned.sem, hid_turned.at(u + 1))
                    dve.tensor_copy(hidt[:, :], ps[:, 3, :]).then_inc(hid_copied.sem, 1)
                    pick_gates(dve, link, u + 1)
                    dve.wait_ge(bias_used.sem, bias_used.at(u + 1))
                    pick_expert(dve, u + 1)
                    dve.wait_ge(used.sem, used.at(u * PANELS + (RING + 12)))
                    dve.tensor_copy(ytok[:, :], ps[:, 2, :]).then_inc(copied.sem, 1)
                    link.done()
                add(dve, n)


def moe_layer(core, bias):
    nc = core.nc
    with ExitStack() as s:
        h = s.enter_context(nc.sbuf_tensor("moe_h", [P, DT, TOK], F32))
        acc = s.enter_context(nc.sbuf_tensor("moe_acc", [P, DT, TOK], F32))
        mod = core.mod2
        rms_modulate(core, h, core.vs("norm2"), mod[:, 32:40], mod[:, 24:32]).run()
        mixture_of_experts(core, h, acc, bias)
        with core.block() as block:
            @block.vector
            def _(dve):
                for k in range(DT):
                    dve.scalar_tensor_tensor(out=core.x[:, k, :], in0=acc[:, k, :], scalar=mod[:, 40 + k:41 + k],
                                             in1=core.x[:, k, :], op0=ALU.mult, op1=ALU.add)


def switch_stream(core, stream):
    assert core.issued == core.used == len(core.stream)
    for slot in range(RING):
        core.panel_loaded[slot].close(16 * len(range(slot, len(core.stream), RING)))
    core.panel_used.close(len(core.stream))
    core.stream, core.issued, core.used = panels_of(stream), 0, 0


def rms_tiles(core, name, t, g, width):
    n = width // P
    with ExitStack() as s:
        sq = s.enter_context(core.nc.sbuf_tensor(f"{name}_sq", [P, n, TOK], F32))
        rs = s.enter_context(core.nc.sbuf_tensor(f"{name}_rs", [P, TOK], F32))
        with core.block() as block:
            @block.scalar
            def _(act):
                act.activation(sq[:, :, :], t, ACT.Square)
        column_sums(core, [(core.ps[:, 4, 0:TOK], core.m("ones"), [sq[:, k, :] for k in range(n)])], ACT.Sqrt)
        rstd_of(core, core.ps[:, 4, 0:TOK], rs[:, :], 1.0 / width, RMS_EPS)
        with core.block() as block:
            @block.vector
            def _(dve):
                for k in range(n):
                    dve.scalar_tensor_tensor(out=t[:, k, :], in0=t[:, k, :], scalar=core.v(g, k), in1=rs[:, :],
                                             op0=ALU.mult, op1=ALU.mult)


TWO_PI_PARTS = (6.28125, 1.935303211212158e-03, 2.535181590533e-09)
ROUND = 1.5 * 2.0 ** 23
HALF_PI = float(np.float32(np.pi / 2))
PI = float(np.nextafter(np.float32(np.pi), np.float32(0)))


def rope_tables(core, pos, ang, turns, tables):
    def angles(dve, link):
        for invf, cos, sin in tables:
            for out, lead in ((sin, 0.0), (cos, HALF_PI)):
                link(dve.tensor_scalar(ang, pos, core.m(invf), None, ALU.mult))
                link(dve.tensor_scalar(turns, ang, 1.0 / (2 * np.pi), lead / (2 * np.pi), ALU.mult, ALU.add))
                link(dve.tensor_scalar(turns, turns, ROUND, None, ALU.add))
                link(dve.tensor_scalar(turns, turns, ROUND, None, ALU.subtract))
                for c in TWO_PI_PARTS:
                    link(dve.scalar_tensor_tensor(out=ang, in0=turns, scalar=-c, in1=ang, op0=ALU.mult, op1=ALU.add))
                if lead:
                    link(dve.tensor_scalar(ang, ang, lead, None, ALU.add))
                link(dve.tensor_scalar(out, ang, PI, -PI, ALU.min, ALU.max))

        dve.sem_inc(core.sem_c.sem, 1)

    def sines(act, link, wait_tile):
        act.wait_ge(core.sem_c.sem, core.sem_c.at(1))
        for _, cos, sin in tables:
            act.activation(cos, cos, ACT.Sin)
            ins = act.activation(sin, sin, ACT.Sin)
        ins.then_inc(core.sem_d.sem, 1)
    return angles, sines


def rope(core, part, rotation, cos, sin, tiles):
    swapped, taken = core.sem_a, core.sem_b

    def rotate(pe, i):
        if i >= 4:
            pe.wait_ge(taken.sem, taken.at(i - 3))
        pe.matmul(core.ps[:, 4 + i % 4, 0:TOK], core.m(rotation(i)), tiles[i], start=True, stop=True).then_inc(swapped.sem, 1)

    def combine(dve, link, i):
        t = tiles[i]
        dve.wait_ge(swapped.sem, swapped.at(i + 1))
        dve.tensor_tensor(part[:, i % 2, :], core.ps[:, 4 + i % 4, 0:TOK], sin(i), ALU.mult).then_inc(taken.sem, 1)
        link(dve.tensor_tensor(t, t, cos(i), ALU.mult))
        dve.wait_ge(taken.sem, taken.at(i + 1))
        link(dve.tensor_tensor(t, t, part[:, i % 2, :], ALU.add))

    def close():
        swapped.close(len(tiles))
        taken.close(len(tiles))
    return rotate, combine, close


def third_block(core):
    nc, x = core.nc, core.x
    switch_stream(core, STREAM_2)
    with ExitStack() as s:
        def sb(name, shape, dt=F32):
            return s.enter_context(nc.sbuf_tensor("third_" + name, shape, dt))
        pos_int, pos = sb("pos_int", [P, TOK], I32), sb("pos", [P, TOK])
        tab = sb("tab", [P, 6, TOK])
        cos32, sin32, cos64, sin64, ang, turns = (tab[:, i, :] for i in range(6))
        with core.block() as block:
            @block.sync
            def _(sp):
                issue_panels(core, sp, RING)

            @block.scalar
            def _(act):
                act.dma_start(pos_int[:, :], core.a["positions"]).then_inc(core.const_loaded.sem, 16)

            @block.vector
            def _(dve):
                dve.wait_ge(core.const_loaded.sem, core.const_loaded.at(16))
                dve.tensor_copy(pos[:, :], pos_int[:, :])
        core.const_loaded.close(16)
        angles, sines = rope_tables(core, pos[:, :], ang, turns, [("invf32", cos32, sin32), ("invf64", cos64, sin64)])
        shift, scale, gate = (core.mod3[:, 8 * i:8 * i + 8] for i in range(3))
        n_lat, n_z, n_mb = 4, 4, 12
        lat = sb("lat", [P, n_lat, TOK])
        z_mla, z_mb = sb("z_mla", [P, n_z, TOK]), sb("z_mb", [P, n_z, TOK])
        mb = sb("moba_qkv", [P, n_mb, TOK])
        merge = sb("merge", [P, 2 * DT, TOK])
        h = sb("h", [P, DT, TOK])
        norm = rms_modulate(core, h, core.vs("g_pre"), scale, shift)

        def plain(dst):
            return [("act", copy_tiles(core, lambda m: dst[:, m, :])(m), None) for m in range(dst.shape[1])]

        def silu(dst):
            return [("act", copy_tiles(core, lambda m: dst[:, m, :], func=ACT.Silu)(m), None) for m in range(n_z)]
        gates = [("act", copy_tiles(core, lambda m: merge[:, m, :], func=ACT.Sigmoid,
                                    bias=lambda m: core.v("b_merge", m))(m), None) for m in range(2 * DT)]
        tiles = plain(lat) + silu(z_mla) + plain(mb) + silu(z_mb) + gates
        tiles[5] = (*tiles[5][:2], sines)
        part = sb("part", [P, 2, TOK])
        first_mb = n_lat + n_z
        rotate, combine, close = rope(core, part, lambda i: "rot64" if i else "rot32", lambda i: cos64 if i else cos32,
                                      lambda i: sin64 if i else sin32, [lat[:, 3, :]] + [mb[:, t, :] for t in range(8)])

        def rotations(pe, j, wait_tile):
            i = j - first_mb
            if 0 <= i <= 8:
                wait_tile(pe, first_mb + i - 1 if i else 3)
                rotate(pe, i)

        def tables_and_rope(dve, link):
            angles(dve, link)
            dve.wait_ge(core.sem_d.sem, core.sem_d.at(1))
            for i in range(9):
                combine(dve, link, i)
        linear(core, "w_in3", lambda k: h[:, k, :], tiles, head=tables_and_rope, pe_work=rotations,
               source=norm)
        close()
        core.sem_c.close(1)
        core.sem_d.close(1)

        o = sb("o", [P, n_z, TOK])
        vt = sb("vt", [P, NB, 4 * P])
        with ExitStack() as s2:
            q = s2.enter_context(nc.sbuf_tensor("mla_q", [P, DT, TOK], F32))
            kv = s2.enter_context(nc.sbuf_tensor("mla_kv", [P, DT + 4, TOK], F32))
            rms_tiles(core, "q_lat", lat[:, 0:2, :], "g_q_lat", 2 * P)
            rms_tiles(core, "kv_lat", lat[:, 2:3, :], "g_kv_lat", P)
            linear(core, "w_uq", lambda k: lat[:, k, :], plain(q))
            rotate, combine, close = rope(core, part, lambda i: "rot32", lambda i: cos32, lambda i: sin32,
                                          [q[:, t, :] for t in range(DT)])

            def rotate_queries(pe, j, wait_tile):
                if j < 4:
                    rotate(pe, 2 * j)
                    rotate(pe, 2 * j + 1)

            def queries_and_shared_keys(dve, link):
                for i in range(DT):
                    combine(dve, link, i)
                for t in range(DT):
                    dve.wait_ge(core.act_evac.sem, core.act_evac.at(t + 1))
                    dve.tensor_copy(kv[64:96, t, :], lat[64:96, 3, :])
            linear(core, "w_ukv", lambda k: lat[:, 2, :], plain(kv), head=queries_and_shared_keys, pe_work=rotate_queries)
            close()
            to_token_major(core, [kv[:, DT + t, :] for t in range(4)], lambda t, b: vt[:, b, t * P:t * P + P])
            softmax_attention(core, "mla", range(8), lambda u: q[:, u, :], lambda u: kv[:, u, :],
                              lambda u, b: vt[:, b, HD * u:HD * u + HD], "causal", 96 ** -0.5,
                              lambda e, j, p: e.tensor_tensor(o[:, j, :], p, z_mla[:, j, :], ALU.mult))
        y = h
        tiles = []
        for m in range(DT):
            def take_a(e, p, m=m):
                return e.tensor_tensor(y[:, m, :], p, merge[:, m, :], ALU.mult)
            tiles.append(("dve", take_a, None))
        linear(core, "w_om", lambda k: o[:, k, :], tiles)

        to_token_major(core, [mb[:, 8 + t, :] for t in range(4)], lambda t, b: vt[:, b, t * P:t * P + P])

        kz = sb("kz", [P, 8, TOK])
        pad_keys(core, mb[:, 4:8, :], kz)
        softmax_attention(core, "moba", range(8), lambda u: mb[:, u // 2, :], lambda u: kz[:, u, :],
                          lambda u, b: vt[:, b, HD * u:HD * u + HD], "causal", HD ** -0.5,
                          lambda e, j, p: e.tensor_tensor(o[:, j, :], p, z_mb[:, j, :], ALU.mult))
        tiles = []
        for m in range(DT):
            def take_b(e, p, m=m):
                return e.tensor_tensor(merge[:, DT + m, :], p, merge[:, DT + m, :], ALU.mult)

            def after(e, link, wait_tile, m=m):
                wait_tile(e, m)
                link(e.tensor_tensor(y[:, m, :], y[:, m, :], merge[:, DT + m, :], ALU.add))
            tiles.append(("dve", take_b, after))
        linear(core, "w_ob", lambda k: o[:, k, :], tiles)

        out = merge[:, 0:DT, :]
        linear(core, "w_out3", lambda k: y[:, k, :], plain(out))
        sq, rs, gg = merge[:, DT:, :], sb("out_rs", [P, TOK]), sb("gg", [P, DT])
        with core.block() as block:
            @block.scalar
            def _(act):
                core.load_table(act, ACT.Sqrt)
                for k in range(DT):
                    act.activation(sq[:, k, :], out[:, k, :], ACT.Square).then_inc(core.sem_a.sem, 1)

            @block.tensor
            def _(pe):
                for k in range(DT):
                    pe.wait_ge(core.sem_a.sem, core.sem_a.at(k + 1))
                    pe.matmul(core.ps[:, 4, 0:TOK], core.m("ones"), sq[:, k, :], start=(k == 0), stop=(k == DT - 1))

            @block.vector
            def _(dve):
                dve.tensor_tensor(gg[:, :], gate, core.vs("g_post"), ALU.mult)
        core.sem_a.close(DT)
        rstd_of(core, core.ps[:, 4, 0:TOK], rs[:, :], 1.0 / D, RMS_EPS)
        with core.block() as block:
            @block.vector
            def _(dve):
                link = core.link("dve", dve)
                for k in range(DT):
                    link(dve.scalar_tensor_tensor(out=out[:, k, :], in0=out[:, k, :], scalar=gg[:, k:k + 1], in1=rs[:, :],
                                                  op0=ALU.mult, op1=ALU.mult))
                    link(dve.tensor_tensor(x[:, k, :], x[:, k, :], out[:, k, :], ALU.add))


def start(core):
    with core.block() as block:
        @block.scalar
        def _(act):
            act.dma_start(core.x[:, :, :], core.a["x"]).then_inc(core.const_loaded.sem, 16)
            act.dma_start(core.vec[:, :], core.a["vectors"]).then_inc(core.const_loaded.sem, 16)
            act.dma_start(core.mat[:, :], core.a["matrices"]).then_inc(core.const_loaded.sem, 16)
            act.wait_ge(core.const_loaded.sem, core.const_loaded.at(48))
    core.const_loaded.close(48)


def finish(core):
    with core.block() as block:
        @block.scalar
        def _(act):
            act.dma_start(core.a["out"], core.x[:, :, :]).then_inc(core.const_loaded.sem, 16)
            act.wait_ge(core.const_loaded.sem, core.const_loaded.at(16))
    core.const_loaded.close(16)


def blocks_kernel(nc, a):
    with ExitStack() as ctx:
        core = Core(nc, a, ctx)
        start(core)
        with ExitStack() as s:
            start_modulation(core, s)
            norm = ssd_layer(core)
            norm = ffn(core, 0, norm)
            per_layer_embedding(core, 0, norm)
            norm = attention_layer(core)
            norm = ffn(core, 1, norm)
            per_layer_embedding(core, 1, norm)
        second_block(core)
        third_block(core)
        finish(core)


def tokens_last(x):
    return np.ascontiguousarray(x.reshape(x.shape[0], -1, P).transpose(2, 1, 0))


def column(v):
    return v.reshape(-1, P).T


def panels(w, width=PANEL):
    k, n = w.shape
    return np.ascontiguousarray(w.reshape(k // P, P, n // width, width).transpose(2, 1, 0, 3)).reshape(n // width, P, -1)


def short(v):
    out = np.zeros((P, 1), np.float32)
    out[:v.size, 0] = v.ravel()
    return out


def rows(v):
    return np.broadcast_to(v.reshape(1, -1), (P, v.size))


def head_order(first):
    order = []
    for t in range(8):
        pair = t // 4
        for half in range(2):
            h = 8 * pair + 4 * half + t % 4
            order += [first + HD * h + i for i in range(HD)]
    return order


def layout(i):
    f = {k: np.asarray(v) for k, v in i.items()}
    a = {"x": tokens_last(f["x"][0]), "p": np.stack([tokens_last(f["p"][l, 0]) for l in range(DEPTH)])}
    w = f["w_in_mix"][0]
    z, xbc, dt, sc = np.split(w, [1024, 2560, 2576], axis=1)
    sb, sc_c, sc_h = np.split(sc, 3, axis=1)
    a["w_in"] = panels(np.concatenate([xbc, sc_c, sc_h, sb, z], axis=1))
    a["w_dt"] = np.ascontiguousarray(dt.reshape(DT, P, 16).transpose(1, 0, 2))
    a["w_out"] = panels(f["w_out_mix"][0])
    for l in range(DEPTH):
        g, u = f["w_ffn_gate"][l].reshape(D, FF_T, P), f["w_ffn_up"][l].reshape(D, FF_T, P)
        a[f"ffn_up{l}"] = panels(np.stack([g, u], axis=2).reshape(D, 2 * D_FF))
        a[f"ffn_dn{l}"] = panels(f["w_ffn_down"][l])
        a[f"ple_g{l}"] = panels(f["w_ple_gate"][l])
        a[f"ple_p{l}"] = panels(f["w_ple"][l])
    qo = head_order(0)
    perm = np.array(qo + list(range(D, 1536)))
    a["qkv"] = panels(f["w_qkv"][0][:, perm])
    a["w_o"] = panels(f["w_o"][0][np.array(qo), :])
    vec = {
        "junk": np.ones((P, 1), np.float32),
        "dt_bias": short(f["ssd_dt_bias"]), "a_log": short(f["ssd_a_log"]),
        "conv_w": column(f["ssd_conv_w"][0]), "conv_b": column(f["ssd_conv_b"][0]), "sc_w": column(f["sc_conv_w"][0]),
        "ssd_d": column(np.repeat(f["ssd_d"][0], HD)), "ssd_norm": column(f["ssd_norm_w"][0]),
        "ln_mix_g": column(f["ln_mix_g"]), "ln_mix_b": column(f["ln_mix_b"]),
        "ln_ffn_g": column(f["ln_ffn_g"]), "ln_ffn_b": column(f["ln_ffn_b"]), "b_ple": column(f["b_ple_gate"]),
        "b_qkv": column(f["b_qkv"][0][perm]), "b_o": column(f["b_o"]), "sinks": rows(f["attn_sinks"][0]),
        "c_2": column(f["c_2"]), "norm1": column(f["norm1_g_2"]), "norm2": column(f["norm2_g_2"]),
        "ada_b_2": column(f["ada_b_2"]), "mu": column(f["shift_mu_2"]), "decay_w0": column(f["decay_w0_2"]),
        "iclr_a0": column(f["iclr_a0_2"]), "k_k": column(f["k_k_2"]), "k_a": column(f["k_a_2"]),
        "r_k": column(f["r_k_2"]), "lnx_w": column(f["lnx_w_2"]), "lnx_b": column(f["lnx_b_2"]),
        "q_norm": np.tile(f["q_norm_g_2"].reshape(HD, 1), (2, 1)), "k_norm": np.tile(f["k_norm_g_2"].reshape(HD, 1), (2, 1)),
        "sb_out": column(f["sb_out_g_2"]), "router_b": rows(f["router_b_2"]),
        "c_3": column(f["c_3"]), "b_ada_3": column(f["b_ada_3"]), "g_pre": column(f["g_pre_3"]),
        "g_post": column(f["g_post_3"]), "g_q_lat": column(f["g_q_lat_3"]), "g_kv_lat": column(f["g_kv_lat_3"]),
        "b_merge": column(f["b_merge_3"]),
    }
    assert all(vec[n].shape == (P, w) for n, w in VECTORS), [n for n, w in VECTORS if vec[n].shape != (P, w)]
    a["vectors"] = np.ascontiguousarray(np.concatenate([vec[n] for n, _ in VECTORS], axis=1))
    a["matrices"] = constant_matrices()
    a["ada2"] = panels(f["ada_w_2"][0])
    a["w_in2"] = panels(f["w_in_2"][0])
    a["w_out2"] = panels(f["w_out_2"][0])
    a["lora"] = np.ascontiguousarray(np.concatenate([
        np.concatenate([f["decay_up_2"][0], f["iclr_up_2"][0]], axis=0), f["gate_up_2"][0]], axis=1))
    a["router"] = np.ascontiguousarray(f["router_w_2"][0].reshape(DT, P, N_EXPERTS).transpose(1, 0, 2))
    a["w1"] = f["exp_w1_2"][0].reshape(N_EXPERTS * 8, P, SLOT)
    a["w2"] = f["exp_w2_2"][0].reshape(N_EXPERTS * 4, 2 * P, D)
    a["eb"] = np.ascontiguousarray(np.concatenate([f["exp_b1_2"][0], f["exp_b2_2"][0]], axis=1))
    w = f["w_in_3"][0]
    q_lat, kv_lat, k_rope, z_mla, q_mb, k_mb, v_mb, z_mb, merge = np.split(
        w, np.cumsum([256, 128, 32, 512, 512, 512, 512, 512]), axis=1)
    a["w_in3"] = panels(np.concatenate([q_lat, kv_lat, np.tile(k_rope, (1, 4)), z_mla, q_mb, k_mb, v_mb, z_mb, merge], axis=1))
    a["ada3"] = panels(f["w_ada_3"][0])
    uq = f["w_uq_3"][0].reshape(256, 8, 96)
    a["w_uq"] = panels(np.pad(uq, ((0, 0), (0, 0), (0, 32))).reshape(256, 1024))
    ukv = f["w_ukv_3"][0].reshape(128, 8, 2, 64)
    k_nope = np.pad(ukv[:, :, 0], ((0, 0), (0, 0), (0, 64))).reshape(128, 1024)
    a["w_ukv"] = panels(np.concatenate([k_nope, ukv[:, :, 1].reshape(128, 512)], axis=1))
    a["w_om"] = panels(f["w_o_mla_3"][0])
    a["w_ob"] = panels(f["w_o_moba_3"][0])
    a["w_out3"] = panels(f["w_out_3"][0])
    a["positions"] = np.ascontiguousarray(np.broadcast_to(f["positions_3"].astype(np.int32).reshape(1, TOK), (P, TOK)))
    return a


def kernel(**inputs):
    import concourse.bacc as bacc
    from concourse.bass_utils import run_bass_kernel_spmd

    nc = bacc.Bacc("TRN2", target_bir_lowering=False, num_devices=1)
    arrays = layout(inputs)
    a = {n: nc.dram_tensor(f"{n}_dram", v.shape, mybir.dt.from_np(v.dtype), kind="ExternalInput").ap()
         for n, v in arrays.items()}
    a["out"] = nc.dram_tensor("out_dram", (P, DT, TOK), F32, kind="ExternalOutput").ap()
    blocks_kernel(nc, a)
    r = run_bass_kernel_spmd(nc, [{f"{n}_dram": v for n, v in arrays.items()}], core_ids=[0])
    out = r.results[0]["out_dram"]
    return np.ascontiguousarray(out.transpose(2, 1, 0)).reshape(1, TOK, D)
```
